# Optimizing a Trainium2 kernel written in Bass

```python
import jax, jax.numpy as jnp
from jax import lax
import numpy as np

D_MODEL = 1024
BATCH = 1
SEQ = 256
DEPTH = 1
DEC_BATCH = 8
DEC_SEQ = 8
PAST_LEN = 2048
PAGE_SIZE = 128

HEAD_DIM = 64
H_A = 8
W_A = H_A * HEAD_DIM
MOBA_BLOCK = 256
MOBA_TOPK = 3
H_B = 8
KV_B = 2
GROUP_B = H_B // KV_B
W_B = H_B * HEAD_DIM
W_KVB = KV_B * HEAD_DIM
CMP_LEN = 32
CMP_STRIDE = 16
CMP_HID = 256
SEL_BLOCK = 64
SEL_TOPN = 16
SEL_LOCAL = 2
WINDOW = 512
D_FF = -(-8 * D_MODEL // (3 * 256)) * 256
Q_CHUNK = 128
N_ADA = 6
EPS = 1e-6
NEG_INF = -1e30
FORCE_SCORE = 1e9
_SPLIT_SIZES = (W_A, W_A, W_A, W_B) + (W_KVB,) * 6 + (H_B * 3, D_MODEL, D_MODEL)
SPLIT_AT = tuple(int(v) for v in np.cumsum(_SPLIT_SIZES)[:-1])
IN_WIDTH = int(sum(_SPLIT_SIZES))

kernel_name = 'moba_nsa_gated_parallel_decoder_step'

def _rmsnorm(x, g):
    xf = x.astype(jnp.float32)
    y = xf * lax.rsqrt(jnp.mean(xf * xf, axis=-1, keepdims=True) + EPS)
    return (y * g.astype(jnp.float32)).astype(x.dtype)

def _alibi_slopes(n):
    return jnp.exp2(-8.0 * (jnp.arange(n, dtype=jnp.float32) + 1.0) / n)

def _masked_softmax(s, mask, axis):
    s = jnp.where(mask, s, NEG_INF)
    e = jnp.where(mask, jnp.exp(s - jnp.max(s, axis=axis, keepdims=True)), 0.0)
    return e / jnp.maximum(jnp.sum(e, axis=axis, keepdims=True), 1e-30)

def _gathered_block_attn(q, k, v, idx, ok, offset, block, slopes):
    B, T, KV, G, Dh = q.shape
    L = k.shape[1]
    nb = -(-L // block)
    pad = ((0, 0), (0, nb * block - L), (0, 0), (0, 0))
    kb = jnp.pad(k, pad).reshape(B, nb, block, KV, Dh).transpose(0, 1, 3, 2, 4)
    vb = jnp.pad(v, pad).reshape(B, nb, block, KV, Dh).transpose(0, 1, 3, 2, 4)
    n = idx.shape[-1]
    qc = min(Q_CHUNK, T)
    nc = T // qc
    kv_ar = jnp.arange(KV)[None, :, None]
    inner = jnp.arange(block)
    scale = Dh ** -0.5

    def one(args):
        q_c, i_c, ok_c, b, p0 = args
        ks = kb[b, i_c, kv_ar]
        vs = vb[b, i_c, kv_ar]
        qpos = (p0 + jnp.arange(qc))[:, None, None, None]
        kpos = i_c[..., None] * block + inner
        s = jnp.einsum('qkgd,qknsd->qkgns', q_c.astype(jnp.float32), ks.astype(jnp.float32)) * scale
        s = s - slopes[None, :, :, None, None] * (qpos - kpos).astype(jnp.float32)[:, :, None]
        mask = (ok_c[..., None] & (kpos <= qpos))[:, :, None]
        p = _masked_softmax(s, mask, (-2, -1))
        return jnp.einsum('qkgns,qknsd->qkgd', p, vs.astype(jnp.float32)).astype(q_c.dtype)

    step = jnp.arange(B * nc)
    xs = (q.reshape(B * nc, qc, KV, G, Dh), idx.reshape(B * nc, qc, KV, n),
          ok.reshape(B * nc, qc, KV, n), step // nc, offset + (step % nc) * qc)
    return lax.map(one, xs).reshape(B, T, KV, G, Dh)

def _moba(q, k, v, offset, slopes):
    B, T, H = q.shape[:3]
    L = k.shape[1]
    nb = -(-L // MOBA_BLOCK)
    kp = jnp.pad(k, ((0, 0), (0, nb * MOBA_BLOCK - L), (0, 0), (0, 0)))
    kmean = jnp.mean(kp.reshape(B, nb, MOBA_BLOCK, H, HEAD_DIM).astype(jnp.float32), axis=2)
    own = ((offset + jnp.arange(T)) // MOBA_BLOCK)[None, :, None, None]
    gate = jnp.einsum('bthd,bnhd->bthn', q[:, :, :, 0].astype(jnp.float32), kmean)
    gate = jnp.where(jnp.arange(nb) < own, gate, NEG_INF)
    _, top = lax.top_k(gate, min(MOBA_TOPK, nb))
    idx = jnp.concatenate([top, jnp.broadcast_to(own, (B, T, H, 1))], axis=-1)
    ok = jnp.concatenate([top < own, jnp.ones((B, T, H, 1), bool)], axis=-1)
    return _gathered_block_attn(q, k, v, idx, ok, offset, MOBA_BLOCK, slopes.reshape(H, 1))

def _compress(k, pe, w1, b1, w2, b2):
    B, L, KV, Dh = k.shape
    r = CMP_LEN // CMP_STRIDE
    nseg = -(-L // CMP_STRIDE)
    kp = jnp.pad(k, ((0, 0), (0, nseg * CMP_STRIDE - L), (0, 0), (0, 0)))
    seg = kp.reshape(B, nseg, CMP_STRIDE, KV, Dh)
    n_cmp = nseg - r + 1
    blk = jnp.concatenate([seg[:, j:j + n_cmp] for j in range(r)], axis=2)
    blk = blk + pe[:, None, :]
    flat = jnp.swapaxes(blk, 2, 3).reshape(B, n_cmp, KV, CMP_LEN * Dh)
    return jax.nn.gelu(flat @ w1 + b1) @ w2 + b2

def _nsa_cmp_sel(q, k_cmp, v_cmp, k_sel, v_sel, offset, w, slopes):
    B, T = q.shape[:2]
    L = k_cmp.shape[1]
    qpos = offset + jnp.arange(T)
    ck = _compress(k_cmp, w['cmp_pe'][0], w['cmp_w1'][0], w['cmp_b1'][0], w['cmp_w2'][0], w['cmp_b2'][0])
    cv = _compress(v_cmp, w['cmp_pe'][1], w['cmp_w1'][1], w['cmp_b1'][1], w['cmp_w2'][1], w['cmp_b2'][1])
    n_cmp = ck.shape[1]
    c_end = jnp.arange(n_cmp) * CMP_STRIDE + (CMP_LEN - 1)
    s = jnp.einsum('btkgd,bnkd->btkgn', q.astype(jnp.float32), ck.astype(jnp.float32)) * HEAD_DIM ** -0.5
    p_cmp = _masked_softmax(s, (c_end[None, :] <= qpos[:, None])[None, :, None, None, :], -1)
    o_cmp = jnp.einsum('btkgn,bnkd->btkgd', p_cmp, cv.astype(jnp.float32)).astype(q.dtype)
    nsb = -(-L // SEL_BLOCK)
    c_start = jnp.arange(n_cmp)[:, None] * CMP_STRIDE
    s_start = jnp.arange(nsb)[None, :] * SEL_BLOCK
    overlap = ((c_start < s_start + SEL_BLOCK) & (c_start + CMP_LEN > s_start)).astype(jnp.float32)
    imp = jnp.einsum('btkgn,nj->btkj', p_cmp, overlap)
    cur = (qpos // SEL_BLOCK)[None, :, None, None]
    jr = jnp.arange(nsb)
    forced = (jr == 0) | ((jr <= cur) & (jr > cur - SEL_LOCAL))
    imp = jnp.where(jr <= cur, jnp.where(forced, FORCE_SCORE, imp), NEG_INF)
    _, idx = lax.top_k(imp, min(SEL_TOPN, nsb))
    o_sel = _gathered_block_attn(q, k_sel, v_sel, idx, idx <= cur, offset, SEL_BLOCK,
                                 slopes.reshape(KV_B, GROUP_B))
    return o_cmp, o_sel

def _window_attn(q, k, v, qpos, kpos, slopes):
    s = jnp.einsum('btkgd,bskd->btkgs', q.astype(jnp.float32), k.astype(jnp.float32)) * HEAD_DIM ** -0.5
    dist = (qpos[:, None] - kpos[None, :]).astype(jnp.float32)
    s = s - slopes[None, None, :, :, None] * dist[None, :, None, None, :]
    mask = (kpos[None, :] <= qpos[:, None]) & (kpos[None, :] > qpos[:, None] - WINDOW) & (kpos[None, :] >= 0)
    p = _masked_softmax(s, mask[None, :, None, None, :], -1)
    return jnp.einsum('btkgs,bskd->btkgd', p, v.astype(jnp.float32)).astype(q.dtype)

def _window_banded(q, k, v, slopes):
    B, T = q.shape[:2]
    qc = min(Q_CHUNK, T)
    nc = T // qc
    pad = ((0, 0), (WINDOW, 0), (0, 0), (0, 0))
    kp = jnp.pad(k, pad)
    vp = jnp.pad(v, pad)

    def one(c):
        t0 = c * qc
        q_c = lax.dynamic_slice_in_dim(q, t0, qc, axis=1)
        k_c = lax.dynamic_slice_in_dim(kp, t0, WINDOW + qc, axis=1)
        v_c = lax.dynamic_slice_in_dim(vp, t0, WINDOW + qc, axis=1)
        return _window_attn(q_c, k_c, v_c, t0 + jnp.arange(qc), t0 - WINDOW + jnp.arange(WINDOW + qc), slopes)

    o = lax.map(one, jnp.arange(nc))
    return jnp.moveaxis(o, 0, 1).reshape(q.shape)

def _layer_inputs(x, c, w):
    B, T, _ = x.shape
    mod = jax.nn.silu(c) @ w['w_ada'] + w['b_ada']
    shift1, scale1, gate1, shift2, scale2, gate2 = jnp.split(mod[:, None, :], N_ADA, axis=-1)
    u = _rmsnorm(x, w['g_attn']) * (1.0 + scale1) + shift1
    qa, ka, va, qb, kc, vc, ks, vs, kw, vw, gn, ga, gb = jnp.split(u @ w['w_in'], SPLIT_AT, axis=-1)
    kvh = lambda t: t.reshape(B, T, KV_B, HEAD_DIM)
    m = {
        'q_a': qa.reshape(B, T, H_A, 1, HEAD_DIM),
        'k_a': ka.reshape(B, T, H_A, HEAD_DIM),
        'v_a': va.reshape(B, T, H_A, HEAD_DIM),
        'q_b': qb.reshape(B, T, KV_B, GROUP_B, HEAD_DIM),
        'k_cmp': kvh(kc), 'v_cmp': kvh(vc),
        'k_sel': kvh(ks), 'v_sel': kvh(vs),
        'k_win': kvh(kw), 'v_win': kvh(vw),
        'g_nsa': jax.nn.sigmoid(gn).reshape(B, T, KV_B, GROUP_B, 3),
        'g_a': jax.nn.sigmoid(ga),
        'g_b': jax.nn.sigmoid(gb),
    }
    return m, (gate1, shift2, scale2, gate2)

def _layer_output(x, o_a, o_cmp, o_sel, o_win, m, ada, w):
    B, T, _ = x.shape
    gate1, shift2, scale2, gate2 = ada
    g = m['g_nsa']
    o_b = g[..., 0:1] * o_cmp + g[..., 1:2] * o_sel + g[..., 2:3] * o_win
    y_a = o_a.reshape(B, T, W_A) @ w['w_pa']
    y_b = o_b.reshape(B, T, W_B) @ w['w_pb']
    mixed = (m['g_a'] * y_a + m['g_b'] * y_b) @ w['w_out']
    x = x + gate1 * mixed
    h = _rmsnorm(x, w['g_ffn']) * (1.0 + scale2) + shift2
    a, b = jnp.split(h @ w['w_gu'], 2, axis=-1)
    return x + gate2 * ((jax.nn.silu(a) * b) @ w['w_down'])

def _prompt_layer(x, c, w, slopes_a, slopes_b):
    B, T, _ = x.shape
    m, ada = _layer_inputs(x, c, w)
    o_a = _moba(m['q_a'], m['k_a'], m['v_a'], 0, slopes_a)
    o_cmp, o_sel = _nsa_cmp_sel(m['q_b'], m['k_cmp'], m['v_cmp'], m['k_sel'], m['v_sel'], 0, w, slopes_b)
    o_win = _window_banded(m['q_b'], m['k_win'], m['v_win'], slopes_b.reshape(KV_B, GROUP_B))
    y = _layer_output(x, o_a, o_cmp, o_sel, o_win, m, ada, w)
    moba_kv = jnp.stack([m['k_a'], m['v_a']], axis=2)
    nsa_kv = jnp.stack([m['k_cmp'], m['v_cmp'], m['k_sel'], m['v_sel']], axis=2)
    keep = min(WINDOW, T)
    nsa_win = jnp.stack([m['k_win'], m['v_win']], axis=2)[:, T - keep:]
    return y, moba_kv, nsa_kv, nsa_win

def _past_rows(cache, page_table, slot):
    rows = cache[page_table, :, slot]
    DB, n_pages, page = rows.shape[:3]
    return rows.reshape(DB, n_pages * page, rows.shape[3], rows.shape[4])

def _sample_layer(x, c, cache_moba_kv, cache_nsa_kv, cache_nsa_win, page_table, w, slopes_a, slopes_b):
    DB, T, _ = x.shape
    past = page_table.shape[1] * cache_moba_kv.shape[1]
    n_buf = cache_nsa_win.shape[1]
    m, ada = _layer_inputs(x, c, w)
    full = lambda cache, slot, new: jnp.concatenate([_past_rows(cache, page_table, slot), new], axis=1)
    o_a = _moba(m['q_a'], full(cache_moba_kv, 0, m['k_a']), full(cache_moba_kv, 1, m['v_a']), past, slopes_a)
    o_cmp, o_sel = _nsa_cmp_sel(m['q_b'], full(cache_nsa_kv, 0, m['k_cmp']), full(cache_nsa_kv, 1, m['v_cmp']),
                                full(cache_nsa_kv, 2, m['k_sel']), full(cache_nsa_kv, 3, m['v_sel']),
                                past, w, slopes_b)
    win_all = jnp.concatenate([cache_nsa_win, jnp.stack([m['k_win'], m['v_win']], axis=2)], axis=1)
    o_win = _window_attn(m['q_b'], win_all[:, :, 0], win_all[:, :, 1], past + jnp.arange(T),
                         past - n_buf + jnp.arange(n_buf + T), slopes_b.reshape(KV_B, GROUP_B))
    y = _layer_output(x, o_a, o_cmp, o_sel, o_win, m, ada, w)
    moba_kv = jnp.stack([m['k_a'], m['v_a']], axis=2)
    nsa_kv = jnp.stack([m['k_cmp'], m['v_cmp'], m['k_sel'], m['v_sel']], axis=2)
    return y, moba_kv, nsa_kv, win_all[:, T:]

def setup_inputs(seed: int = 0) -> dict:
    key = jax.random.key(seed)
    ks = jax.random.split(key, 24)
    n_pages = PAST_LEN // PAGE_SIZE
    n_pool = 5 * DEC_BATCH * n_pages // 4
    n_buf = min(WINDOW, PAST_LEN)

    def nrm(k, shape, scale):
        return jax.random.normal(k, shape, jnp.float32) * scale

    page_table = jax.random.permutation(ks[0], n_pool)[:DEC_BATCH * n_pages].reshape(DEC_BATCH, n_pages).astype(jnp.int32)
    return {
        'x_prompt': nrm(ks[1], (BATCH, SEQ, D_MODEL), 1.0),
        'x_sample': nrm(ks[2], (DEC_BATCH, DEC_SEQ, D_MODEL), 1.0),
        'cache_moba_kv': nrm(ks[3], (n_pool, PAGE_SIZE, 2, H_A, HEAD_DIM), 1.0),
        'cache_nsa_kv': nrm(ks[4], (n_pool, PAGE_SIZE, 4, KV_B, HEAD_DIM), 1.0),
        'cache_nsa_win': nrm(ks[5], (DEC_BATCH, n_buf, 2, KV_B, HEAD_DIM), 1.0),
        'page_table': page_table,
        'c_prompt': nrm(ks[6], (BATCH, D_MODEL), 1.0),
        'c_sample': nrm(ks[7], (DEC_BATCH, D_MODEL), 1.0),
        'w_ada': nrm(ks[8], (D_MODEL, N_ADA * D_MODEL), 0.5 * D_MODEL ** -0.5),
        'b_ada': nrm(ks[9], (N_ADA * D_MODEL,), 0.02),
        'g_attn': 1.0 + nrm(ks[10], (D_MODEL,), 0.02),
        'w_in': nrm(ks[11], (D_MODEL, IN_WIDTH), D_MODEL ** -0.5),
        'cmp_pe': nrm(ks[12], (2, CMP_LEN, HEAD_DIM), 0.1),
        'cmp_w1': nrm(ks[13], (2, CMP_LEN * HEAD_DIM, CMP_HID), (CMP_LEN * HEAD_DIM) ** -0.5),
        'cmp_b1': nrm(ks[14], (2, CMP_HID), 0.02),
        'cmp_w2': nrm(ks[15], (2, CMP_HID, HEAD_DIM), CMP_HID ** -0.5),
        'cmp_b2': nrm(ks[16], (2, HEAD_DIM), 0.02),
        'w_pa': nrm(ks[17], (W_A, D_MODEL), W_A ** -0.5),
        'w_pb': nrm(ks[18], (W_B, D_MODEL), W_B ** -0.5),
        'w_out': nrm(ks[19], (D_MODEL, D_MODEL), D_MODEL ** -0.5),
        'g_ffn': 1.0 + nrm(ks[20], (D_MODEL,), 0.02),
        'w_gu': nrm(ks[21], (D_MODEL, 2 * D_FF), D_MODEL ** -0.5),
        'w_down': nrm(ks[22], (D_FF, D_MODEL), D_FF ** -0.5),
        'g_final': 1.0 + nrm(ks[23], (D_MODEL,), 0.02),
    }

def reference(x_prompt, x_sample, cache_moba_kv, cache_nsa_kv, cache_nsa_win, page_table, c_prompt, c_sample,
              w_ada, b_ada, g_attn, w_in, cmp_pe, cmp_w1, cmp_b1, cmp_w2, cmp_b2, w_pa, w_pb, w_out,
              g_ffn, w_gu, w_down, g_final):
    w = {'w_ada': w_ada, 'b_ada': b_ada, 'g_attn': g_attn, 'w_in': w_in, 'cmp_pe': cmp_pe,
         'cmp_w1': cmp_w1, 'cmp_b1': cmp_b1, 'cmp_w2': cmp_w2, 'cmp_b2': cmp_b2, 'w_pa': w_pa,
         'w_pb': w_pb, 'w_out': w_out, 'g_ffn': g_ffn, 'w_gu': w_gu, 'w_down': w_down}
    slopes_a = _alibi_slopes(H_A)
    slopes_b = _alibi_slopes(H_B)
    xp, xs = x_prompt, x_sample
    for _ in range(DEPTH):
        xp, moba_kv_prompt, nsa_kv_prompt, nsa_win_prompt = _prompt_layer(xp, c_prompt, w, slopes_a, slopes_b)
        xs, moba_kv_sample, nsa_kv_sample, nsa_win_sample = _sample_layer(
            xs, c_sample, cache_moba_kv, cache_nsa_kv, cache_nsa_win, page_table, w, slopes_a, slopes_b)
    y_prompt = _rmsnorm(xp, g_final)
    y_sample = _rmsnorm(xs, g_final)
    return (y_prompt, y_sample, moba_kv_prompt, nsa_kv_prompt, nsa_win_prompt,
            moba_kv_sample, nsa_kv_sample, nsa_win_sample)


_drawn_inputs = setup_inputs


def setup_inputs(seed=0):
    import zlib

    import numpy as np

    out = dict(_drawn_inputs(seed))
    spreads = {}
    factors = {'cache_nsa_kv': 2.994,
     'g_attn': 3.007,
     'cmp_pe': 8.0,
     'cmp_b1': 8.0,
     'cmp_b2': 8.0,
     'g_ffn': 8.0,
     'g_final': 2.914}
    for name, (base, spread) in spreads.items():
        noise = np.random.default_rng([zlib.crc32(name.encode()), seed]).standard_normal(out[name].shape)
        drawn = base * np.exp(spread * noise) if base else spread * noise
        out[name] = __import__('jax').numpy.asarray(drawn.astype(out[name].dtype))
    for name, factor in factors.items():
        out[name] = (out[name] * factor).astype(out[name].dtype)
    return out
```

```python
from contextlib import ExitStack

import concourse.bass as bass
from concourse import mybir

F32 = mybir.dt.float32
I32 = mybir.dt.int32
U32 = mybir.dt.uint32
ALU = mybir.AluOpType
ACT = mybir.ActivationFunctionType
AX = mybir.AxisListType

P = 128
D = 1024
KT = D // P
SEQ = 256
NB = 8
T = 8
NS = NB * T
TOK = SEQ + NS
PAST = 2048
PAGE = 128
DH = 64
H = 8
KV = 2
G = H // KV
SEG = 16
NSEG = PAST // SEG
NCMP = NSEG - 1
PSEG = SEQ // SEG
PCMP = PSEG - 1
PC1 = 2 * PCMP + 1
MB = 256
NMB = PAST // MB
MTOP = 3
SB = 64
NSB = PAST // SB
CAND = NSB - 2
STOP = 16 - 3
WIN = 512
FF = 2816
FT = FF // P
NADA = 6
EPS = 1e-6
NEG = -1e30
SCALE = DH ** -0.5
QA, KA, VA, QB, KC, GN, GA, GB = 0, 512, 1024, 1536, 2048, 2816, 2840, 3864
RKA, RVA, RKC, RKS, RVS, RKW, RVW, ROWW = 0, 512, 1024, 1280, 1408, 1536, 1664, 1792
SLOTS = 4
OPEN = 4
SLABW = 2048
V_ADA, V_GA, V_GF, V_GZ, V_B1, V_PE, V_B2, NVEC = 0, 48, 56, 64, 72, 76, 108, 109
C_GSUM, C_BDEC, C_BOWN, C_BWIN, C_TIE, C_TIE8 = 0, 64, 64 + PAST, 64 + PAST + 512, 64 + PAST + 1024, 64 + PAST + 1024 + CAND * CAND
C64W = C_TIE8 + 64
C_BP0, C_BP1, C_MADD, C_MMUL, CPW = 0, 1024, 3072, 3104, 3136
T_TILES = [(0, 128), (128, 128), (256, 64)]


class Steps:

    def __init__(self, eng, sem, base=0):
        self.eng, self.sem, self.base, self.n = eng, sem, base, 0

    def do(self, ins):
        self.n += 1
        ins.then_inc(self.sem, 1)
        self.eng.wait_ge(self.sem, self.base + self.n)


def apart(eng, turns):
    eng.sem_inc(turns, 1)


def front_block(nc, sem, t, d, ps):
    loaded, x_loaded, c_loaded = sem("f_loaded"), sem("f_x_loaded"), sem("f_c_loaded")
    slab_landed = [sem(f"f_slab_landed{s}") for s in range(SLOTS)]
    slab_used = [sem(f"f_slab_used{s}") for s in range(SLOTS)]
    silu_done, x_tr, vec_tr, c_tr = sem("f_silu"), sem("f_x_tr"), sem("f_vec_tr"), sem("f_c_tr")
    xT_dve, xT_act, vecT_done, cT_done = sem("f_xT_dve"), sem("f_xT_act"), sem("f_vecT"), sem("f_cT")
    ada_mm, mod_done, sq_done, ss_mm, root_done = sem("f_ada_mm"), sem("f_mod"), sem("f_sq"), sem("f_ss_mm"), sem("f_root")
    u_done, q_mm, q_dve, q_act = sem("f_u"), sem("f_q_mm"), sem("f_q_dve"), sem("f_q_act")
    row_mm, row_dve, row_act = sem("f_row_mm"), sem("f_row_dve"), sem("f_row_act")
    kt_tr, kt_dve, kt_act = sem("f_kt_tr"), sem("f_kt_dve"), sem("f_kt_act")
    dve_step, stored, spilled = sem("f_dve_step"), sem("f_stored"), sem("f_spilled")
    u_pre, u_mid, modn_done, mod_tr = sem("f_u_pre"), sem("f_u_mid"), sem("f_modn"), sem("f_mod_tr")
    modn = t["modn"]
    table_landed, later_loaded, gn_mm, gn_done = sem("f_table"), sem("f_later"), sem("f_gn_mm"), sem("f_gn")
    slab, xn, cn, vecn = t["slab"], t["xn"], t["cn"], t["vecn"]
    xT, uT, sq, cT, vecT, mod = t["xT"], t["uT"], t["sq"], t["cT"], t["vecT"], t["mod"]
    ident, ones = t["ident"], t["ones"]
    rows_p, rows_s = t["rows_p"], t["rows_s"]
    NROWJ = 21

    def w_slab(w, c0, n):
        return w[:, c0:c0 + n] if isinstance(c0, int) else w[:, bass.ds(c0, n)]

    with nc.Block() as block:

        @block.sync
        def _(sp):
            sp.dma_start(ident[:, :], d["c_ident"]).then_inc(c_loaded, 16)
            sp.dma_start(cn[0:1, :], d["c_prompt"]).then_inc(c_loaded, 16)
            sp.dma_start(cn[1:1 + NB, :], d["c_sample"]).then_inc(c_loaded, 16)
            w_ada = d["w_ada"].rearrange("(k p) n -> p k n", p=P)
            with sp.Fori(0, NADA) as it:
                for s in range(SLOTS):
                    sp.wait_ge(slab_used[s], it + OPEN)
                    half = 4 * (s % 2)
                    sp.dma_start(slab[:, s, :].rearrange("p (k n) -> p k n", k=4),
                                 w_ada[:, half:half + 4, bass.ds(it * D + 512 * (s // 2), 512)])\
                      .then_inc(slab_landed[s], 16)
            w_in = d["w_in"].rearrange("(k p) n -> p k n", p=P)
            for j in range(11):
                s = j % SLOTS
                sp.wait_ge(slab_used[s], NADA + j // SLOTS + OPEN)
                if j in (2, 3):
                    for n, (g, kv) in enumerate([(g, kv) for g in range(2) for kv in range(KV)]):
                        c0 = QB + kv * 256 + (2 * (j - 2) + g) * DH
                        sp.dma_start(slab[:, s, :].rearrange("p (k n) -> p k n", k=KT)[:, :, n * DH:n * DH + DH],
                                     w_in[:, :, c0:c0 + DH]).then_inc(slab_landed[s], 16)
                else:
                    c0 = [QA, QA + 256, 0, 0, KA, KA + 256, VA, VA + 256, KC, KC + 256, KC + 512][j]
                    sp.dma_start(slab[:, s, :].rearrange("p (k n) -> p k n", k=KT),
                                 w_in[:, :, c0:c0 + 256]).then_inc(slab_landed[s], 16)
            sp.wait_ge(u_done, KT)
            sp.dma_start(d["spill_x"], xT[:, :, :].rearrange("p k n -> p (k n)")).then_inc(spilled, 16)
            sp.dma_start(d["spill_u"], uT[:, :, :].rearrange("p k n -> p (k n)")).then_inc(spilled, 16)
            sp.wait_ge(row_dve, 11)
            sp.wait_ge(row_act, 10)
            for i in range(2):
                tok = slice(P * i, P * i + P)
                sp.dma_start(d["moba_kv_prompt"][tok, :], rows_p[:, i, RKA:RKC]).then_inc(stored, 16)
                sp.dma_start(d["nsa_kv_prompt"][tok, :], rows_p[:, i, RKC:RKW]).then_inc(stored, 16)
                sp.dma_start(d["nsa_win_prompt"][tok, :], rows_p[:, i, RKW:ROWW]).then_inc(stored, 16)
            sp.dma_start(d["moba_kv_sample"], rows_s[:, RKA:RKC]).then_inc(stored, 16)
            sp.dma_start(d["nsa_kv_sample"], rows_s[:, RKC:RKW]).then_inc(stored, 16)
            for b in range(NB):
                sp.dma_start(d["nsa_win_sample"][b, WIN - T:WIN, :],
                             rows_s[T * b:T * b + T, RKW:ROWW]).then_inc(stored, 16)
            sp.wait_ge(stored, 16 * (6 + 2 + NB))
            sp.wait_ge(spilled, 32)

        @block.gpsimd
        def _(pool):
            for i, (t0, n) in enumerate(T_TILES):
                src = d["x_sample"] if i == 2 else d["x_prompt"][t0:t0 + n, :]
                pool.dma_start(xn[0:n, i, :], src).then_inc(x_loaded, 16)
            pool.dma_start(vecn[V_ADA:V_GA, :], d["b_ada"].rearrange("(r c) -> r c", c=P)).then_inc(loaded, 16)
            pool.dma_start(vecn[V_GA:V_GF, :], d["g_attn"].rearrange("(r c) -> r c", c=P)).then_inc(loaded, 16)
            pool.dma_start(vecn[V_GF:V_GZ, :], d["g_ffn"].rearrange("(r c) -> r c", c=P)).then_inc(loaded, 16)
            pool.dma_start(vecn[V_GZ:V_B1, :], d["g_final"].rearrange("(r c) -> r c", c=P)).then_inc(loaded, 16)
            pool.dma_start(vecn[V_B1:V_PE, :], d["cmp_b1"].rearrange("w (r c) -> (w r) c", c=P)).then_inc(loaded, 16)
            pool.dma_start(vecn[V_PE:V_B2, :],
                           d["cmp_pe"].rearrange("w (r two) e -> (w r) (two e)", two=2)).then_inc(loaded, 16)
            for kv in range(KV):
                pool.dma_start(vecn[V_B2:NVEC, DH * kv:DH * kv + DH], d["cmp_b2"][0:1, :]).then_inc(loaded, 16)
            pool.dma_start(ones[:, :], d["c_ones"]).then_inc(loaded, 16)
            table = d["page_table"].rearrange("b g -> g b")
            for s in range(PAGE // SEG):
                pool.dma_start(t["table"][s:P:PAGE // SEG, :], table, allow_slow_non_contiguous=True).then_inc(table_landed, 16)
            pool.dma_start(t["seg_col"][:, :], d["c_seg"]).then_inc(table_landed, 16)
            pool.dma_start(t["cp"][:, :], d["c_p"]).then_inc(later_loaded, 16)
            pool.dma_start(t["c64"][:, :], d["c_64"]).then_inc(later_loaded, 16)
            pool.dma_start(t["wgn"][:, :].rearrange("p (k n) -> p k n", k=KT),
                           d["w_in"].rearrange("(k p) n -> p k n", p=P)[:, :, GN:GN + 24]).then_inc(table_landed, 16)
            pool.dma_start(d["nsa_win_sample"][:, 0:WIN - T, :], d["cache_nsa_win"][:, T:WIN, :]).then_inc(later_loaded, 16)
            pool.wait_ge(later_loaded, 48)

        @block.tensor
        def _(pe):
            pe.wait_ge(c_loaded, 48)
            pe.wait_ge(silu_done, 1)
            for k in range(KT):
                last = pe.transpose(ps[5][:, 9 * k:9 * k + 9], cn[0:9, P * k:P * k + P], ident[0:9, 0:9])
            last.then_inc(c_tr, 1)
            pe.wait_ge(cT_done, 1)
            pe.wait_ge(x_loaded, 48)
            for k in range(KT):
                if k >= 4:
                    pe.wait_ge(xT_dve if k % 2 == 0 else xT_act, k // 2 - 1)
                for i, (t0, n) in enumerate(T_TILES):
                    last = pe.transpose(ps[k % 4][:, t0:t0 + n], xn[0:n, i, P * k:P * k + P], ident[0:n, 0:n])
                last.then_inc(x_tr, 1)
            pe.wait_ge(loaded, 16 * 9)
            pe.transpose(ps[4][:, 0:NVEC], vecn[0:NVEC, :], ident[0:NVEC, 0:NVEC]).then_inc(vec_tr, 1)
            for k in range(KT):
                pe.wait_ge(sq_done, k + 1)
                last = pe.matmul(ps[7][:, 0:TOK], ones[:, :], sq[:, k, :], start=k == 0, stop=k == KT - 1)
            last.then_inc(ss_mm, 1)

            def ada(it):
                for g in range(2):
                    pe.wait_ge(modn_done, it * 2 + g - 1 + OPEN)
                    for half in range(2):
                        s = 2 * g + half
                        pe.wait_ge(slab_landed[s], it * 16 + 16)
                        for k in range(4):
                            c0 = 9 * (4 * half + k)
                            last = pe.matmul(ps[5 + g][0:9, :], cT[:, c0:c0 + 9], slab[:, s, 512 * k:512 * k + 512],
                                             start=s % 2 == 0 and k == 0, stop=s % 2 == 1 and k == 3)
                        last.then_inc(slab_used[s], 1)

            def mod_transposes(bank, first, n):
                pe.wait_ge(modn_done, (first + n) // 4 + OPEN)
                for i in range(n):
                    last = pe.transpose(bank[:, 9 * i:9 * i + 9], modn[:, P * (first + i):P * (first + i) + P],
                                        ident[0:9, 0:9])
                last.then_inc(mod_tr, 1)

            for nothing_yet in slab_used:
                pe.sem_inc(nothing_yet, OPEN)
            with pe.Fori(0, 2) as it:
                ada(it)
            mod_transposes(ps[0], 0, 16)
            with pe.Fori(2, NADA) as it:
                ada(it)
            mod_transposes(ps[1], 16, 32)
            pe.wait_ge(u_done, KT)
            for m in range(8):
                s, ct = m // 2, m % 2
                if ct == 0:
                    pe.wait_ge(slab_landed[s], 16 * NADA + (16 if s < 2 else 64))
                if m == 0:
                    pe.wait_ge(mod_done, 2)
                if m >= 2:
                    pe.wait_ge(q_dve if m % 2 == 0 else q_act, m - 1 if m % 2 else m)
                for k in range(KT):
                    w = slab[:, s, 256 * k + P * ct:256 * k + P * ct + P]
                    last = pe.matmul(ps[m % 2][:, 0:TOK], w, uT[:, k, :], start=k == 0, stop=k == KT - 1)
                last.then_inc(q_mm, 1)
                if ct == 1:
                    pe.wait_ge(q_mm, m + 1)
                    pe.sem_inc(slab_used[s], 1)
            pe.wait_ge(table_landed, 16 * (PAGE // SEG + 2))
            for k in range(KT):
                last = pe.matmul(ps[7][0:24, 0:TOK], t["wgn"][:, 24 * k:24 * k + 24], uT[:, k, :],
                                 start=k == 0, stop=k == KT - 1)
            last.then_inc(gn_mm, 1)
            for j in range(4, 11):
                s = j % SLOTS
                pe.wait_ge(slab_landed[s], 16 * (NADA + j // SLOTS + 1) + (48 if s in (2, 3) else 0))
                for i, (t0, n) in enumerate(T_TILES):
                    r = 3 * (j - 4) + i
                    if r >= 4:
                        pe.wait_ge(row_dve if r % 2 == 0 else row_act, r // 2 - 1)
                    for k in range(KT):
                        last = pe.matmul(ps[2 + r % 4][0:n, 0:256], uT[:, k, t0:t0 + n],
                                         slab[:, s, 256 * k:256 * k + 256], start=k == 0, stop=k == KT - 1)
                    last.then_inc(row_mm, 1)
                pe.wait_ge(row_mm, 3 * (j - 3))
                pe.sem_inc(slab_used[s], 1)
            pe.wait_ge(row_dve, 11)
            pe.wait_ge(row_act, 10)
            pe.wait_ge(q_dve, 8)
            pe.wait_ge(q_act, 8)
            for g, c0 in enumerate([RKA, RKA + 128, RKA + 256, RKA + 384, RKS, RKW]):
                if g >= 2:
                    pe.wait_ge(kt_dve if g % 2 == 0 else kt_act, 2 * (g // 2))
                for i, (t0, n) in enumerate(T_TILES):
                    src = rows_s[:, c0:c0 + P] if i == 2 else rows_p[:, i, c0:c0 + P]
                    last = pe.transpose(ps[g % 2][:, t0:t0 + n], src, ident[0:n, 0:n])
                last.then_inc(kt_tr, 1)

        def kT_dst(g):
            if g < 4:
                return t["kaT_p"][:, g, :], t["kaT_s"][:, g, 0:NS]
            return t["ksT_p" if g == 4 else "kwT_p"][:, :], t["ksT_s" if g == 4 else "kwT_s"][:, 0:NS]

        def q_dst(m):
            n = "qaT" if m < 4 else "qbT"
            return t[n + "_p"][:, m % 4, :], t[n + "_s"][:, m % 4, 0:NS]

        def row_dst(r):
            j, i = r // 3, r % 3
            return rows_s[:, 256 * j:256 * j + 256] if i == 2 else rows_p[:, i, 256 * j:256 * j + 256]

        @block.scalar
        def _(act):
            act.sem_inc(modn_done, OPEN)
            act.wait_ge(c_loaded, 48)
            act.activation(cn[0:9, :], cn[0:9, :], ACT.Silu).then_inc(silu_done, 1)
            for k in range(1, KT, 2):
                act.wait_ge(x_tr, k + 1)
                act.activation(xT[:, k, :], ps[k % 4][:, 0:TOK], ACT.Copy).then_inc(xT_act, 1)
            act.wait_ge(xT_dve, 4)
            act.wait_ge(xT_act, 4)
            for k in range(KT):
                act.activation(sq[:, k, :], xT[:, k, :], ACT.Square).then_inc(sq_done, 1)
            act.wait_ge(ss_mm, 1)
            act.activation(t["root"][:, :], ps[7][:, 0:TOK], ACT.Sqrt, bias=t["eps"][:, 0:1], scale=1.0 / D)\
               .then_inc(root_done, 1)
            with act.Fori(0, NADA) as it:
                for g in range(2):
                    act.wait_ge(slab_used[2 * g + 1], it + 1 + OPEN)
                    act.activation(modn[:, bass.ds(it * D + 512 * g, 512)], ps[5 + g][0:9, :], ACT.Copy)\
                       .then_inc(modn_done, 1)
            for m in range(1, 8, 2):
                p_out, s_out = q_dst(m)
                act.wait_ge(q_mm, m + 1)
                act.activation(p_out, ps[1][:, 0:SEQ], ACT.Copy).then_inc(q_act, 1)
                act.activation(s_out, ps[1][:, SEQ:TOK], ACT.Copy).then_inc(q_act, 1)
            act.wait_ge(gn_mm, 1)
            act.activation(t["gn"][:, :], ps[7][0:24, 0:TOK], ACT.Sigmoid).then_inc(gn_done, 1)
            for r in range(1, NROWJ, 2):
                n = T_TILES[r % 3][1]
                act.wait_ge(row_mm, r + 1)
                act.activation(row_dst(r), ps[2 + r % 4][0:n, 0:256], ACT.Copy).then_inc(row_act, 1)
            for g in range(1, 6, 2):
                p_out, s_out = kT_dst(g)
                act.wait_ge(kt_tr, g + 1)
                act.activation(p_out, ps[1][:, 0:SEQ], ACT.Copy).then_inc(kt_act, 1)
                act.activation(s_out, ps[1][:, SEQ:TOK], ACT.Copy).then_inc(kt_act, 1)

        @block.vector
        def _(dve):
            steps = Steps(dve, dve_step)
            steps.do(dve.memset(t["eps"][:, :], EPS))
            for n in ("qaT_s", "qbT_s"):
                steps.do(dve.memset(t[n][:, :, NS:NS + T], 0.0))
            dve.wait_ge(c_tr, 1)
            dve.tensor_copy(cT[:, :], ps[5][:, 0:72]).then_inc(cT_done, 1)
            for k in range(0, KT, 2):
                dve.wait_ge(x_tr, k + 1)
                dve.tensor_copy(xT[:, k, :], ps[k % 4][:, 0:TOK]).then_inc(xT_dve, 1)
            dve.wait_ge(vec_tr, 1)
            dve.tensor_copy(vecT[:, :], ps[4][:, 0:NVEC]).then_inc(vecT_done, 1)
            dve.wait_ge(table_landed, 16 * (PAGE // SEG + 2))
            steps.do(dve.tensor_scalar(t["index"][:, :], t["table"][:, :], float(PAGE // SEG), t["seg_col"][:, 0:1],
                                       ALU.mult, ALU.add))
            dve.wait_ge(vecT_done, 1)
            dve.wait_ge(root_done, 1)
            dve.wait_ge(xT_act, 4)
            steps.do(dve.reciprocal(t["rstd"][:, :], t["root"][:, :]))

            def vectors(bank, first, n, which, scale, g0):
                bias = vecT[:, V_ADA + first:V_ADA + first + n].unsqueeze(2).to_broadcast([P, n, 9])
                dve.wait_ge(mod_tr, which + 1)
                dve.tensor_tensor(mod[:, first:first + n, :], bank[:, 0:9 * n].rearrange("p (a b) -> p a b", b=9),
                                  bias, ALU.add).then_inc(mod_done, 1)
                dve.wait_ge(mod_done, which + 1)
                g = vecT[:, g0:g0 + KT].unsqueeze(2).to_broadcast([P, KT, 9])
                steps.do(dve.scalar_tensor_tensor(t["amp"][:, which, :, :], mod[:, scale:scale + KT, :], 1.0, g,
                                                  ALU.add, ALU.mult))

            vectors(ps[0], 0, 16, 0, 8, V_GA)
            modulate(dve, t, 0, 0, u_pre, u_mid, u_done)
            vectors(ps[1], 16, 32, 1, 32, V_GF)
            for m in range(0, 8, 2):
                p_out, s_out = q_dst(m)
                dve.wait_ge(q_mm, m + 1)
                dve.tensor_copy(p_out, ps[0][:, 0:SEQ]).then_inc(q_dve, 1)
                dve.tensor_copy(s_out, ps[0][:, SEQ:TOK]).then_inc(q_dve, 1)
            for r in range(0, NROWJ, 2):
                n = T_TILES[r % 3][1]
                dve.wait_ge(row_mm, r + 1)
                dve.tensor_copy(row_dst(r), ps[2 + r % 4][0:n, 0:256]).then_inc(row_dve, 1)
            for g in range(0, 6, 2):
                p_out, s_out = kT_dst(g)
                dve.wait_ge(kt_tr, g + 1)
                dve.tensor_copy(p_out, ps[0][:, 0:SEQ]).then_inc(kt_dve, 1)
                dve.tensor_copy(s_out, ps[0][:, SEQ:TOK]).then_inc(kt_dve, 1)


def modulate(dve, t, which, shift, pre, mid, done):
    xT, uT, amp, mod = t["xT"], t["uT"], t["amp"], t["mod"]
    for step in range(KT + 2):
        if step < KT:
            dve.tensor_tensor(uT[:, step, :], xT[:, step, :], t["rstd"][:, :], ALU.mult).then_inc(pre, 1)
        k = step - 1
        if 0 <= k < KT:
            dve.wait_ge(pre, k + 1)
            dve.tensor_scalar(uT[:, k, 0:SEQ], uT[:, k, 0:SEQ], amp[:, which, k, 0:1], mod[:, shift + k, 0:1],
                              ALU.mult, ALU.add)
            u = uT[:, k, SEQ:TOK].rearrange("p (b t) -> p b t", t=T)
            dve.tensor_tensor(u, u, amp[:, which, k, 1:9].unsqueeze(2).to_broadcast([P, NB, T]), ALU.mult)\
               .then_inc(mid, 1)
        k = step - 2
        if k >= 0:
            dve.wait_ge(mid, k + 1)
            u = uT[:, k, SEQ:TOK].rearrange("p (b t) -> p b t", t=T)
            dve.tensor_tensor(u, u, mod[:, shift + k, 1:9].unsqueeze(2).to_broadcast([P, NB, T]), ALU.add)\
               .then_inc(done, 1)


UNITS = [(br, qt) for br in (0, 2, 3) for qt in range(2)]
BR_MOBA, BR_CMP, BR_SEL, BR_WIN = range(4)


def head_at(branch, half, tile):
    return 2 * tile + half if branch == BR_MOBA else G * half + tile


def score_banks(u):
    return 4 if UNITS[u][1] else 2


def prompt_block(nc, sem, t, d, ps):
    w1_landed, segs_landed = sem("p_w1"), sem("p_segs")
    seg_tr, segs_done, hidn_done, hid_tr, hbias_done = (sem("p_seg_tr"), sem("p_segs_done"), sem("p_hidn"),
                                                        sem("p_hid_tr"), sem("p_hbias"))
    conv_mm, gelu_done, ckcv_mm, ck_done, cv_done = (sem("p_conv_mm"), sem("p_gelu"), sem("p_ckcv_mm"), sem("p_ck"),
                                                     sem("p_cv"))
    cs_mm, csub_done, cexp_done, cp_ready = sem("p_cs_mm"), sem("p_csub"), sem("p_cexp"), sem("p_cprob")
    scores_mm, scores_taken, max_done, exp_done, p_ready = (sem("p_scores_mm"), sem("p_scores_taken"), sem("p_max"),
                                                            sem("p_exp"), sem("p_prob"))
    pt_tr, pt_dve, pt_act, pv_mm, pv_taken = (sem("p_pt_tr"), sem("p_pt_dve"), sem("p_pt_act"), sem("p_pv_mm"),
                                              sem("p_pv_taken"))
    dve_step, spilled = sem("p_dve_step"), sem("p_spilled")
    w1 = t["slab"][:, :, :].rearrange("p (w a) (b n) -> p w (a b) n", w=2, n=256)
    segs, XT, hid, ckT, cv = t["segs"], t["XTp"], t["hid_p"], t["ckT_p"], t["cv_p"]
    S, PT, Sc, PTc, cp, oT = t["S_p"], t["PT_p"], t["Sc_p"], t["PTc_p"], t["cp"], t["oT_p"]
    ident, vecT, hbias, rows = t["ident"], t["vecT"], t["hbias"], t["rows_p"]
    hidn = t["hidn"]
    NU = len(UNITS)
    jobs_of = [2 * (qt + 1) for _, qt in UNITS]
    first_job = [sum(jobs_of[:u]) for u in range(NU)]
    first_cmp_job = sum(jobs_of)

    with nc.Block() as block:

        @block.sync
        def _(sp):
            src = d["nsa_kv_prompt"].rearrange("(s lp l2) c -> s lp l2 c", lp=8, l2=2)
            for c in range(4):
                for l2 in range(2):
                    sp.dma_start(segs[:, :, c, l2, :], src[:, :, l2, DH * c:DH * c + DH]).then_inc(segs_landed, 16)
            for w in range(2):
                sp.dma_start(w1[:, w, :, :], d["cmp_w1"][w].rearrange("(lp p) n -> p lp n", p=P)).then_inc(w1_landed, 16)
                sp.dma_start(t["w2"][:, w, :, :], d["cmp_w2"][w].rearrange("(h p) e -> p h e", p=P)).then_inc(w1_landed, 16)
            sp.dma_start(t["b2v"][:, :], d["cmp_b2"][1:2, :]).then_inc(w1_landed, 16)
            sp.wait_ge(pv_taken, NU + 2)
            sp.dma_start(d["spill_o"], oT[:, :, :, :].rearrange("p b g t -> p (b g t)")).then_inc(spilled, 16)
            sp.wait_ge(spilled, 16)

        @block.tensor
        def _(pe):
            def scores(u):
                br, qt = UNITS[u]
                nk = P * (qt + 1)
                before = sum(score_banks(v) for v in range(u))
                if u:
                    pe.wait_ge(scores_taken, before)
                for slot in range(H):
                    half, tile = slot // 4, slot % 4
                    rows64 = slice(DH * half, DH * half + DH)
                    qT = t["qaT_p" if br == BR_MOBA else "qbT_p"][rows64, tile, P * qt:P * qt + P]
                    kT = (t["kaT_p"][rows64, tile, 0:nk] if br == BR_MOBA
                          else t["ksT_p" if br == BR_SEL else "kwT_p"][rows64, 0:nk])
                    col = slot * nk
                    last = pe.matmul(ps[col // 512][:, col % 512:col % 512 + nk], qT, kT, start=True, stop=True)
                    if (col + nk) % 512 == 0:
                        last.then_inc(scores_mm, 1)

            def staging(job):
                if job >= 2:
                    pe.wait_ge(pt_dve if job % 2 == 0 else pt_act, job // 2)
                return ps[4 + job % 2]

            def attend(u):
                br, qt = UNITS[u]
                pe.wait_ge(p_ready, u + 1)
                for i in range(jobs_of[u]):
                    bank = staging(first_job[u] + i)
                    kt, h0 = i // 2, 4 * (i % 2)
                    for h in range(h0, h0 + 4):
                        col = h * P * (qt + 1) + P * kt
                        last = pe.transpose(bank[:, P * (h - h0):P * (h - h0) + P], S[:, u % 3, col:col + P], ident[:, :])
                    last.then_inc(pt_tr, 1)
                done = first_job[u] + jobs_of[u]
                pe.wait_ge(pt_dve, done // 2)
                pe.wait_ge(pt_act, done // 2)
                if u:
                    pe.wait_ge(pv_taken, u)
                if u == 5:
                    pe.wait_ge(csub_done, 1)
                for slot in range(H):
                    half, tile = slot // 4, slot % 4
                    h = head_at(br, half, tile)
                    c0 = {BR_MOBA: RVA + h * DH, BR_SEL: RVS + half * DH, BR_WIN: RVW + half * DH}[br]
                    for kt in range(qt + 1):
                        last = pe.matmul(ps[6][DH * half:DH * half + DH, P * tile:P * tile + P],
                                         rows[:, kt, c0:c0 + DH], PT[:, u % 2, kt, slot, :], start=kt == 0, stop=kt == qt)
                last.then_inc(pv_mm, 1)

            def segment_transposes():
                pe.wait_ge(segs_landed, 16 * 8)
                for lp in range(8):
                    for c in range(4):
                        last = pe.transpose(ps[7][:, (c * 8 + lp) * PSEG:(c * 8 + lp + 1) * PSEG],
                                            segs[:, lp, c, :, :].rearrange("s a e -> s (a e)"), ident[0:PSEG, 0:PSEG])
                last.then_inc(seg_tr, 1)

            def hidden_layer():
                pe.wait_ge(w1_landed, 16 * 5)
                pe.wait_ge(segs_done, 5)
                for w in range(2):
                    for part in range(2):
                        for lp in range(8):
                            last = pe.matmul(ps[7][0:PC1, 256 * w:256 * w + 256], XT[:, w, part, lp, :],
                                             w1[:, w, 8 * part + lp, :], start=part == 0 and lp == 0,
                                             stop=part == 1 and lp == 7)
                last.then_inc(conv_mm, 1)

            def hidden_transposes():
                pe.wait_ge(hidn_done, 1)
                for c in range(4):
                    last = pe.transpose(ps[7][:, 32 * c:32 * c + PC1], hidn[:, P * c:P * c + P], ident[0:PC1, 0:PC1])
                last.then_inc(hid_tr, 1)

            def keys_and_values():
                pe.wait_ge(gelu_done, 4)
                compressed_keys(pe, ps[7], t, hid, 0, PCMP)
                last = compressed_values(pe, ps[7][:, P:2 * P], t, hid, 0, PCMP)
                last.then_inc(ckcv_mm, 1)

            def compressed_scores():
                pe.wait_ge(ck_done, 2)
                pe.wait_ge(cv_done, 2)
                pe.wait_ge(pv_taken, 5)
                for qt in range(2):
                    for slot in range(H):
                        half, g = slot // 4, slot % 4
                        rows64 = slice(DH * half, DH * half + DH)
                        col = (qt * G + g) * PSEG
                        last = pe.matmul(ps[6 if half else 7][:, col:col + PSEG],
                                         t["qbT_p"][rows64, g, P * qt:P * qt + P], ckT[rows64, :], start=True, stop=True)
                last.then_inc(cs_mm, 1)

            between = [segment_transposes, hidden_layer, hidden_transposes, keys_and_values, compressed_scores, None]
            scores(0)
            scores(1)
            for u in range(NU):
                if u + 2 < NU:
                    scores(u + 2)
                attend(u)
                if between[u]:
                    between[u]()
            pe.wait_ge(cp_ready, 2)
            for j in range(4):
                bank = staging(first_cmp_job + j)
                for i in range(4):
                    n = 4 * j + i
                    last = pe.transpose(bank[0:PSEG, P * i:P * i + P], Sc[:, n * PSEG:n * PSEG + PSEG], ident[:, :])
                last.then_inc(pt_tr, 1)
            for qt in range(2):
                pe.wait_ge(pt_act, first_cmp_job // 2 + qt + 1)
                pe.wait_ge(pt_dve, first_cmp_job // 2 + qt + 1)
                pe.wait_ge(pv_taken, NU + qt)
                for h in range(H):
                    half, g = h // 4, h % 4
                    last = pe.matmul(ps[6][DH * half:DH * half + DH, P * g:P * g + P], cv[:, DH * half:DH * half + DH],
                                     PTc[:, qt * H + h, :], start=True, stop=True)
                last.then_inc(pv_mm, 1)

        def pt_dst(job):
            if job >= first_cmp_job:
                j = job - first_cmp_job
                return PTc[:, 4 * j:4 * j + 4, :].rearrange("p a b -> p (a b)")
            u = max(v for v in range(NU) if first_job[v] <= job)
            i = job - first_job[u]
            return PT[:, u % 2, i // 2, 4 * (i % 2):4 * (i % 2) + 4, :].rearrange("p a b -> p (a b)")

        def pt_rows(job):
            return PSEG if job >= first_cmp_job else P

        @block.scalar
        def _(act):
            def pt_copy(job):
                act.wait_ge(pt_tr, job + 1)
                act.activation(pt_dst(job), ps[4 + job % 2][0:pt_rows(job), :], ACT.Copy).then_inc(pt_act, 1)

            def pv_copy(n, br, qt):
                act.wait_ge(pv_mm, n + 1)
                act.activation(oT[:, br, :, P * qt:P * qt + P], ps[6][:, :].rearrange("p (g q) -> p g q", g=4),
                               ACT.Copy).then_inc(pv_taken, 1)

            def exps(u):
                qt = UNITS[u][1]
                nk = P * (qt + 1)
                act.wait_ge(max_done, u + 1)
                for h in range(H):
                    act.activation(S[:, u % 3, h * nk:h * nk + nk], S[:, u % 3, h * nk:h * nk + nk], ACT.Exp,
                                   bias=t["nmax_p"][:, u % 3, h:h + 1], accum_out=t["sum_p"][:, u % 3, h:h + 1])\
                       .then_inc(exp_done, 1)

            def hidden_copy():
                act.wait_ge(conv_mm, 1)
                act.activation(hidn[:, :], ps[7][0:PC1, :], ACT.Copy).then_inc(hidn_done, 1)

            def gelu():
                act.wait_ge(hbias_done, 1)
                for w in range(2):
                    for ht in range(2):
                        c = 2 * w + ht
                        act.activation(hid[:, w, ht, :], ps[7][:, 32 * c:32 * c + 2 * PCMP], ACT.Gelu_apprx_tanh,
                                       bias=hbias[:, c:c + 1]).then_inc(gelu_done, 1)

            def keys_and_values():
                act.wait_ge(ckcv_mm, 1)
                act.wait_ge(ck_done, 1)
                act.activation(ckT[:, 0:PCMP], ps[7][:, 0:PCMP], ACT.Identity, bias=vecT[:, V_B2:V_B2 + 1])\
                   .then_inc(ck_done, 1)
                act.wait_ge(cv_done, 1)
                act.activation(cv[0:PCMP, :], ps[7][0:PCMP, P:2 * P], ACT.Copy).then_inc(cv_done, 1)

            def compressed_exps():
                act.wait_ge(csub_done, 1)
                act.activation(Sc[:, :], Sc[:, :], ACT.Exp).then_inc(cexp_done, 1)

            between = [None, hidden_copy, gelu, keys_and_values, compressed_exps, None]
            exps(0)
            exps(1)
            for u, (br, qt) in enumerate(UNITS):
                for job in range(first_job[u] + 1, first_job[u] + jobs_of[u], 2):
                    pt_copy(job)
                if u + 2 < NU:
                    exps(u + 2)
                pv_copy(u, br, qt)
                if between[u]:
                    between[u]()
            for j in (1, 3):
                pt_copy(first_cmp_job + j)
            for qt in range(2):
                pv_copy(NU + qt, BR_CMP, qt)

        @block.vector
        def _(dve):
            steps = Steps(dve, dve_step)

            def pt_copy(job):
                dve.wait_ge(pt_tr, job + 1)
                dve.tensor_copy(pt_dst(job), ps[4 + job % 2][0:pt_rows(job), :]).then_inc(pt_dve, 1)

            def biased(u):
                qt = UNITS[u][1]
                nk = P * (qt + 1)
                before = sum(score_banks(v) for v in range(u))
                c0 = C_BP1 if qt else C_BP0
                if u >= 3:
                    dve.wait_ge(pt_tr, first_job[u - 3] + jobs_of[u - 3])
                bias = cp[:, c0:c0 + H * nk].rearrange("p (h k) -> p h k", h=H)
                n = 512 // nk
                for b in range(score_banks(u)):
                    h0 = head_at(UNITS[u][0], n * b // 4, n * b % 4)
                    step = 2 if UNITS[u][0] == BR_MOBA else 1
                    dve.wait_ge(scores_mm, before + b + 1)
                    dve.scalar_tensor_tensor(S[:, u % 3, 512 * b:512 * b + 512].rearrange("p (h k) -> p h k", h=n),
                                             ps[b][:, :].rearrange("p (h k) -> p h k", h=n), SCALE,
                                             bias[:, h0:h0 + step * (n - 1) + 1:step, :], ALU.mult, ALU.add)\
                       .then_inc(scores_taken, 1)
                dve.wait_ge(scores_taken, before + score_banks(u))
                dve.tensor_reduce(t["nmax_p"][:, u % 3, :], S[:, u % 3, 0:H * nk].rearrange("p (h k) -> p h k", h=H),
                                  AX.X, ALU.max, negate=True).then_inc(max_done, 1)

            def normed(u):
                qt = UNITS[u][1]
                nk = P * (qt + 1)
                dve.wait_ge(exp_done, H * (u + 1))
                steps.do(dve.reciprocal(t["rsum_p"][:, :], t["sum_p"][:, u % 3, :]))
                s = S[:, u % 3, 0:H * nk].rearrange("p (h k) -> p h k", h=H)
                dve.tensor_tensor(s, s, t["rsum_p"][:, :].unsqueeze(2).to_broadcast([P, H, nk]), ALU.mult)\
                   .then_inc(p_ready, 1)

            def segment_copies():
                dve.wait_ge(seg_tr, 1)
                for w in range(2):
                    for part in range(2):
                        dve.tensor_copy(XT[:, w, part, :, 0:2 * PCMP].rearrange("p l (v n) -> p v l n", v=KV),
                                        ps[7][:, 256 * w:256 * w + 256].rearrange("p (v l s) -> p v l s", v=KV, l=8)
                                        [:, :, :, part:part + PCMP]).then_inc(segs_done, 1)
                dve.tensor_copy(XT[:, :, :, :, :].rearrange("p w a l n -> p (w a l) n")[:, :, 2 * PCMP],
                                vecT[:, V_PE:V_B2]).then_inc(segs_done, 1)

            def hidden_bias():
                dve.wait_ge(hid_tr, 1)
                dve.tensor_tensor(hbias[:, :], ps[7][:, 2 * PCMP:P:32], vecT[:, V_B1:V_PE], ALU.add)\
                   .then_inc(hbias_done, 1)

            s3 = Sc[:, :].rearrange("p (r n) -> p r n", n=PSEG)
            stat = t["cstat_p"]

            def compressed_scores():
                dve.wait_ge(cs_mm, 1)
                for qt, half in [(0, 0), (0, 1), (1, 0), (1, 1)]:
                    m = cp[:, C_MADD + PSEG * qt:C_MADD + PSEG * qt + PSEG].unsqueeze(1).to_broadcast([P, G, PSEG])
                    c = slice(P * qt + 64 * half, P * qt + 64 * half + 64)
                    raw = ps[6 if half else 7][:, 64 * qt:64 * qt + 64]
                    last = dve.scalar_tensor_tensor(Sc[:, c].rearrange("p (h n) -> p h n", h=G),
                                                    raw.rearrange("p (h n) -> p h n", h=G), SCALE, m,
                                                    ALU.mult, ALU.add)
                steps.do(last)
                steps.do(dve.tensor_reduce(stat[:, :], s3, AX.X, ALU.max))
                dve.tensor_tensor(s3, s3, stat[:, :].unsqueeze(2).to_broadcast([P, 2 * H, PSEG]), ALU.subtract)\
                   .then_inc(csub_done, 1)

            def compressed_probs():
                dve.wait_ge(cexp_done, 1)
                for qt in range(2):
                    m = cp[:, C_MMUL + PSEG * qt:C_MMUL + PSEG * qt + PSEG].unsqueeze(1).to_broadcast([P, H, PSEG])
                    s = Sc[:, P * qt:P * qt + P].rearrange("p (h n) -> p h n", h=H)
                    last = dve.tensor_tensor(s, s, m, ALU.mult)
                steps.do(last)
                steps.do(dve.tensor_reduce(stat[:, :], s3, AX.X, ALU.add))
                steps.do(dve.tensor_scalar(stat[:, :], stat[:, :], 1e-30, None, ALU.max))
                steps.do(dve.reciprocal(stat[:, :], stat[:, :]))
                for qt in range(2):
                    s = Sc[:, P * qt:P * qt + P].rearrange("p (h n) -> p h n", h=H)
                    dve.tensor_tensor(s, s, stat[:, H * qt:H * qt + H].unsqueeze(2).to_broadcast([P, H, PSEG]), ALU.mult)\
                       .then_inc(cp_ready, 1)

            dve.memset(ckT[:, :], 0.0).then_inc(ck_done, 1)
            dve.memset(cv[:, :], 0.0).then_inc(cv_done, 1)
            between = [segment_copies, None, hidden_bias, None, compressed_scores, compressed_probs]
            biased(0)
            biased(1)
            for u in range(NU):
                normed(u)
                if u + 2 < NU:
                    biased(u + 2)
                for job in range(first_job[u], first_job[u] + jobs_of[u], 2):
                    pt_copy(job)
                if between[u]:
                    between[u]()
            for j in (0, 2):
                pt_copy(first_cmp_job + j)


def compress(pe, out, w1, XT, w, ht, n):
    for part in range(2):
        for lp in range(8):
            last = pe.matmul(out, w1[:, w, 8 * part + lp, P * ht:P * ht + P], XT[:, w, :, lp, part:part + n],
                             start=part == 0 and lp == 0, stop=part == 1 and lp == 7)
    return last


def compressed_keys(pe, bank, t, hid, w, n):
    for kv in range(KV):
        for ht in range(2):
            last = pe.matmul(bank[DH * kv:DH * kv + DH, 0:n], t["w2"][:, 0, ht, :], hid[:, 0, ht, n * kv:n * kv + n],
                             start=ht == 0, stop=ht == 1)
    return last


def compressed_values(pe, bank, t, hid, w, n):
    for kv in range(KV):
        out = bank[0:n, DH * kv:DH * kv + DH]
        for ht in range(2):
            pe.matmul(out, hid[:, 1, ht, n * kv:n * kv + n], t["w2"][:, 1, ht, :], start=ht == 0, stop=False)
        last = pe.matmul(out, t["ones"][0:1, 0:n], t["b2v"][:, :], start=False, stop=True)
    return last


GROUPS = ([grp for q in range(4) for grp in [("cmp", q, 0), ("cmp", q, 1), ("sel", q, 0)]
           + [("moba", q, hp) for hp in range(4)]] + [("win", 0, 0)])
NG = len(GROUPS)
SCORED = [g for g in range(NG) if GROUPS[g][0] != "cmp"]
NM = len(SCORED)
EVEN, ODD = (NG + 1) // 2, NG // 2
N_SCORE = 9
N_RING, N_SMALL, N_OUT = 13, 4, 3
DVE_STEPS = 20
V_SLOTS = 12
E_MOBA, E_WIN, E_CMP, E_SEL = range(4)


def bank_of_scores(g):
    kind, q, _ = GROUPS[g]
    return {"sel": 2 * q, "moba": 2 * q + 1, "win": 8}[kind]


def last_group(s):
    return max(g for g in SCORED if bank_of_scores(g) == s)


def transposed(kind, q):
    return max(g for g in range(NG) if GROUPS[g][:2] == (kind, q)) + 1


def decode_block(nc, sem, t, d, ps):
    k_landed = [sem(f"d_k{s}") for s in range(2)]
    v_landed = [sem(f"d_v{s}") for s in range(V_SLOTS // 4)]
    nsa_landed = [sem(f"d_nsa{s}") for s in range(2)]
    win_landed, mask_zeroed, staged_index = sem("d_win"), sem("d_mask_zeroed"), sem("d_staged_index")
    q_zeroed, q_staged, relaid, kept = sem("d_q_zeroed"), sem("d_q_staged"), sem("d_relaid"), sem("d_kept")
    tr, copied_dve, copied_act, scored, scores_taken = (sem("d_tr"), sem("d_copied_dve"), sem("d_copied_act"),
                                                        sem("d_scored"), sem("d_scores_taken"))
    ring_mm, ring_taken, small_mm, small_taken = sem("d_ring_mm"), sem("d_ring_taken"), sem("d_small_mm"), sem("d_small_taken")
    out_mm, out_taken, v_used = sem("d_out_mm"), sem("d_out_taken"), sem("d_v_used")
    max_done, exp_done, pc_ready, dve_step = sem("d_max"), sem("d_exp"), sem("d_pc"), sem("d_dve_step")
    pe_turns, pool_turns = sem("d_pe_turns"), sem("d_pool_turns")
    w1 = t["slab"][:, :, :].rearrange("p (w a) (b n) -> p w (a b) n", w=2, n=256)
    Kr, Vr, nsa, relay, vsel, XT, KTr = t["Kr"], t["Vr"], t["nsa"], t["relay"], t["vsel"], t["XT"], t["KTr"]
    Sm, Ss, Sw, Sc, PTm, PTs, PTw = t["Sm"], t["Ss"], t["Sw"], t["Sc"], t["PTm"], t["PTs"], t["PTw"]
    hid, ckT, cv, wkv, qa, qb = t["hid"], t["ckT"], t["cv"], t["wkv"], t["qa_cur"], t["qb_cur"]
    c64, ident, rows, oT = t["c64"], t["ident"], t["rows_s"], t["oT_s"]
    ident64 = ident[0:64, 0:64]
    OWN = PAST

    with nc.Block() as block:

        @block.sync
        def _(sp):
            with sp.Fori(0, NB) as it:
                sp.wait_ge(out_mm, it * N_OUT + OPEN)
                sp.dma_start(wkv[:, :, :].rearrange("p c x -> p (c x)"),
                             d["cache_nsa_win"].rearrange("b (p c) x -> p b (c x)", c=4)[:, bass.ds(it, 1), :]
                             .rearrange("p b x -> p (b x)")).then_inc(win_landed, 16)

        @block.gpsimd
        def _(pool):
            def gather(dst, src, which, offset, landed):
                pool.indirect_dma_start(out=dst, out_offset=None, in_=src,
                                        in_offset=bass.IndirectOffsetOnAxis(ap=t["index_now"][:, which:which + 1], axis=0),
                                        element_offset=offset).then_inc(landed, 16)

            def gather_k(lq, which):
                for l in range(4 * lq, 4 * lq + 4):
                    gather(Kr[:, l % 8, :], d["cache_moba_kv"], which, l * 1024, k_landed[lq % 2])

            def gather_v(lq, which):
                for l in range(4 * lq, 4 * lq + 4):
                    s = l % V_SLOTS
                    gather(Vr[:, s, :], d["cache_moba_kv"], which, l * 1024 + 512, v_landed[s // 4])

            def gather_nsa(q, which):
                gather(nsa[:, q % 2, :], d["cache_nsa_kv"], which, q * 2048, nsa_landed[q % 2])

            def stage_index(which, column):
                pool.tensor_copy(t["index_now"][:, which:which + 1], t["index"][:, column]).then_inc(staged_index, 1)

            def gather_nsa_after(it, q, quarter, which):
                pool.wait_ge(kept, it * 4 + q + 1)
                pool.wait_ge(relaid, it * 8 + 2 * q + 2)
                gather_after(tr, it * NG + transposed("sel", q) + OPEN, gather_nsa, quarter, which)

            def gather_k_after(it, q, quarter, which):
                gather_after(tr, it * NG + transposed("moba", q) + OPEN, gather_k, quarter, which)

            def sequence(it, odd, more):
                for q in range(2):
                    gather_nsa_after(it, q, q + 2, odd)
                    gather_k_after(it, q, q + 2, odd)
                if more:
                    pool.wait_ge(v_used, it * 4 + OPEN)
                    stage_index(1 - odd, bass.ds(it + 1, 1))
                    pool.wait_ge(staged_index, it + 2)
                    for q in range(2, 4):
                        gather_nsa_after(it, q, q - 2, 1 - odd)
                        gather_k_after(it, q, q - 2, 1 - odd)
                gather_after(v_used, it * 4 + 1 + OPEN, gather_v, 3, odd)
                if more:
                    for q in (1, 2, 0):
                        gather_after(v_used, it * 4 + (q + 1 if q else 4) + OPEN, gather_v, q, 1 - odd)

            def gather_after(used, count, gather_quarter, q, which):
                pool.wait_ge(used, count)
                apart(pool, pool_turns)
                gather_quarter(q, which)

            stage_index(0, slice(0, 1))
            pool.wait_ge(staged_index, 1)
            for q in range(2):
                gather_nsa(q, 0)
                gather_k(q, 0)
            for q in range(3):
                gather_v(q, 0)
            with pool.Fori(0, NB - 2, 2) as it:
                sequence(it, 0, True)
                sequence(it + 1, 1, True)
            sequence(NB - 2, 0, True)
            sequence(NB - 1, 1, False)

        @block.tensor
        def _(pe):
            def transposes(it, g):
                kind, q, i = GROUPS[g]
                if g % 2 == 0:
                    pe.wait_ge(copied_dve, it * EVEN + g // 2 + OPEN)
                else:
                    pe.wait_ge(copied_act, it * ODD + g // 2 + OPEN)
                if kind == "moba":
                    if i == 0:
                        pe.wait_ge(k_landed[q % 2], it * 128 + 64 * (q // 2 + 1))
                    srcs = [Kr[:, l % 8, P * i:P * i + P] for l in range(4 * q, 4 * q + 4)]
                elif kind == "cmp":
                    pe.wait_ge(relaid, it * 8 + 2 * q + i + 1)
                    srcs = [relay[:, i, P * c:P * c + P] for c in range(4)]
                elif kind == "sel":
                    pe.wait_ge(nsa_landed[q % 2], it * 32 + 16 * (q // 2 + 1))
                    srcs = [nsa[:, q % 2, 512 * l + 256:512 * l + 384] for l in range(4)]
                else:
                    pe.wait_ge(win_landed, it * 16 + 16)
                    srcs = [wkv[:, c, 0:P] for c in range(4)]
                for n, src in enumerate(srcs):
                    last = pe.transpose(ps[g % 2][:, P * n:P * n + P], src, ident[:, :])
                last.then_inc(tr, 1)

            def score(it, g):
                kind, q, i = GROUPS[g]
                s, m = bank_of_scores(g), SCORED.index(g)
                if g % 2 == 0:
                    pe.wait_ge(copied_dve, it * EVEN + g // 2 + 1 + OPEN)
                else:
                    pe.wait_ge(copied_act, it * ODD + g // 2 + 1 + OPEN)
                if i == 0:
                    pe.wait_ge(scores_taken, it * N_SCORE + s - 1 + OPEN)
                lhsT = qa[:, 64 * i:64 * i + 64] if kind == "moba" else qb[:, :]
                pe.matmul(ps[2 + s % 2][0:64, :], lhsT, KTr[:, m % 4, :], start=i == 0,
                          stop=kind != "moba" or i == 3).then_inc(scored, 1)

            def ring_bank(it, r):
                pe.wait_ge(ring_taken, it * N_RING + r - 1 + OPEN)
                return ps[4 + r % 2]

            def prob_transposes(it, S, r):
                for n in range(2):
                    bank = ring_bank(it, r + n)
                    for i in range(8):
                        c0 = P * (8 * n + i)
                        if i == 0:
                            apart(pe, pe_turns)
                        last = pe.transpose(bank[:, 64 * i:64 * i + 64], S[:, c0:c0 + P], ident64)
                    last.then_inc(ring_mm, 1)
                bank = ring_bank(it, r + 2)
                apart(pe, pe_turns)
                pe.transpose(bank[0:64, 0:64], S[:, OWN:OWN + 64], ident64).then_inc(ring_mm, 1)

            def sequence(it):
                pe.wait_ge(q_staged, it * 4 + 4)
                pe.wait_ge(small_taken, it * N_SMALL + OPEN)
                for hp in range(4):
                    pe.matmul(ps[7][0:64, 0:64], qa[:, 64 * hp:64 * hp + 64], t["kaT_s"][:, hp, :],
                              start=hp == 0, stop=hp == 3)
                pe.matmul(ps[7][0:64, 64:128], qb[:, :], t["ksT_s"][:, :], start=True, stop=True)
                pe.matmul(ps[7][0:64, 128:192], qb[:, :], t["kwT_s"][:, :], start=True, stop=True).then_inc(small_mm, 1)
                for g in range(NG):
                    transposes(it, g)
                    if g >= 2 and g - 2 in SCORED:
                        score(it, g - 2)
                score(it, NG - 2)
                score(it, NG - 1)
                last_cmp = transposed("cmp", 3) - 1
                pe.wait_ge(copied_dve, it * EVEN + last_cmp // 2 + 1 + OPEN)
                pe.wait_ge(copied_act, it * ODD + (last_cmp + 1) // 2 + OPEN)
                for w in range(2):
                    for ht in range(2):
                        out = ring_bank(it, 2 * w + ht)[:, 0:2 * NCMP]
                        compress(pe, out, w1, XT, w, ht, NCMP).then_inc(ring_mm, 1)
                bank = ring_bank(it, 4)
                compressed_keys(pe, bank, t, hid, 0, NCMP).then_inc(ring_mm, 1)
                bank = ring_bank(it, 5)
                compressed_values(pe, bank, t, hid, 0, NCMP).then_inc(ring_mm, 1)
                pe.wait_ge(ring_taken, it * N_RING + 5 + OPEN)
                pe.wait_ge(small_taken, it * N_SMALL + 1 + OPEN)
                pe.matmul(ps[7][0:64, 0:NCMP], qb[:, :], ckT[:, 0:NCMP], start=True, stop=True).then_inc(small_mm, 1)
                pe.wait_ge(exp_done, it * 4 + E_MOBA + 1)
                prob_transposes(it, Sm, 6)
                pe.wait_ge(out_taken, it * N_OUT + OPEN)
                for l in range(SEG):
                    if l % 8 == 0:
                        pe.wait_ge(ring_taken, it * N_RING + 7 + l // 8 + OPEN)
                    if l == 8:
                        pe.wait_ge(pc_ready, it + 1)
                        pe.wait_ge(small_taken, it * N_SMALL + 2 + OPEN)
                        apart(pe, pe_turns)
                        pe.matmul(ps[7][0:64, 0:NCMP], c64[:, C_GSUM:C_GSUM + 64], Sc[:, 0:NCMP], start=True, stop=True)\
                          .then_inc(small_mm, 1)
                    vs = l % V_SLOTS
                    if l % 4 == 0:
                        pe.wait_ge(v_landed[vs // 4], it * (64 if vs else 128) + 64 * (l // V_SLOTS + 1))
                    last = pe.matmul(ps[6][0:64, :], PTm[:, l, :], Vr[:, vs, :], start=l == 0, stop=False)
                    if l % 4 == 3:
                        last.then_inc(v_used, 1)
                pe.wait_ge(ring_taken, it * N_RING + 9 + OPEN)
                apart(pe, pe_turns)
                pe.matmul(ps[6][0:64, :], PTm[0:64, SEG, :], rows[:, RVA:RVA + 512], start=False, stop=True)\
                  .then_inc(out_mm, 1)
                pe.wait_ge(exp_done, it * 4 + E_WIN + 1)
                bank = ring_bank(it, 9)
                apart(pe, pe_turns)
                pe.transpose(bank[0:NCMP, 0:64], Sc[:, 0:NCMP], ident64)
                for c in range(4):
                    pe.transpose(bank[:, 64 * (1 + c):64 * (2 + c)], Sw[:, P * c:P * c + P], ident64)
                pe.transpose(bank[0:64, 320:384], Sw[:, WIN:WIN + 64], ident64).then_inc(ring_mm, 1)
                pe.wait_ge(ring_taken, it * N_RING + 10 + OPEN)
                pe.wait_ge(out_taken, it * N_OUT + 1 + OPEN)
                pe.matmul(ps[6][0:64, 0:P], PTw[0:NCMP, 0, :], cv[0:NCMP, :], start=True, stop=True)
                for c in range(4):
                    pe.matmul(ps[6][0:64, P:2 * P], PTw[:, 1 + c, :], wkv[:, c, P:2 * P], start=c == 0, stop=False)
                pe.matmul(ps[6][0:64, P:2 * P], PTw[0:64, 5, :], rows[:, RVW:RVW + P], start=False, stop=True)\
                  .then_inc(out_mm, 1)
                pe.wait_ge(exp_done, it * 4 + E_SEL + 1)
                prob_transposes(it, Ss, 10)
                pe.wait_ge(out_taken, it * N_OUT + 2 + OPEN)
                pe.wait_ge(kept, it * 4 + 4)
                for l in range(SEG):
                    if l % 8 == 0:
                        pe.wait_ge(ring_taken, it * N_RING + 11 + l // 8 + OPEN)
                    pe.matmul(ps[6][0:64, 0:P], PTs[:, l, :], vsel[:, l, :], start=l == 0, stop=False)
                pe.wait_ge(ring_taken, it * N_RING + 13 + OPEN)
                apart(pe, pe_turns)
                pe.matmul(ps[6][0:64, 0:P], PTs[0:64, SEG, :], rows[:, RVS:RVS + P], start=False, stop=True)\
                  .then_inc(out_mm, 1)
                pe.wait_ge(out_taken, it * N_OUT + 3 + OPEN)
                pe.wait_ge(small_taken, it * N_SMALL + 3 + OPEN)
                apart(pe, pe_turns)
                for n in range(4):
                    pe.transpose(ps[7][:, 64 * n:64 * n + 64], t["Om"][:, P * n:P * n + P], ident64)
                for n in range(3):
                    last = pe.transpose(ps[7][:, 256 + 64 * n:320 + 64 * n], t["On"][:, n, :], ident64)
                last.then_inc(small_mm, 1)

            for nothing_yet in (tr, scored, ring_mm, out_mm, v_used):
                pe.sem_inc(nothing_yet, OPEN)
            with pe.Fori(0, NB) as it:
                sequence(it)

        def group_copy(eng, copy, it, g, done):
            kind, q, i = GROUPS[g]
            eng.wait_ge(tr, it * NG + g + 1 + OPEN)
            if kind == "cmp":
                eng.wait_ge(ring_mm, it * N_RING + OPEN)
                dst = XT[:, :, :, 2 * q + i, :].rearrange("p w v s -> p (w v) s")
                copy(dst, ps[g % 2][:, :].rearrange("p (c s) -> p c s", c=4)).then_inc(done, 1)
            else:
                m = SCORED.index(g)
                eng.wait_ge(scored, it * NM + m - 3 + OPEN)
                copy(KTr[:, m % 4, :], ps[g % 2][:, :]).then_inc(done, 1)

        @block.scalar
        def _(act):
            def copy(dst, src):
                return act.activation(dst, src, ACT.Copy)

            def stage_queries(b):
                cols = bass.ds(b * T, T) if not isinstance(b, int) else slice(b * T, b * T + T)
                for half in range(2):
                    rows64 = slice(DH * half, DH * half + DH)
                    copy(qa[rows64, 8 * half:8 * half + 320].rearrange("p (g c) -> p g c", c=80)[:, :, 0:T],
                         t["qaT_s"][rows64, :, cols]).then_inc(q_staged, 1)
                    copy(qb[rows64, 32 * half:32 * half + 32].rearrange("p (g c) -> p g c", c=T),
                         t["qbT_s"][rows64, :, cols]).then_inc(q_staged, 1)

            def exp(it, which, S, n):
                act.wait_ge(max_done, it * 4 + which + 1)
                act.activation(S[:, 0:n], S[:, 0:n], ACT.Exp, bias=t["nmax"][:, which:which + 1],
                               accum_out=t["sums"][:, which:which + 1]).then_inc(exp_done, 1)

            def prob_copies(it, PT, r):
                for n in range(2):
                    act.wait_ge(ring_mm, it * N_RING + r + n + 1 + OPEN)
                    copy(PT[:, 8 * n:8 * n + 8, :].rearrange("p l r -> p (l r)"), ps[4 + (r + n) % 2][:, :])\
                        .then_inc(ring_taken, 1)
                act.wait_ge(ring_mm, it * N_RING + r + 3 + OPEN)
                copy(PT[0:64, SEG, :], ps[4 + r % 2][0:64, 0:64]).then_inc(ring_taken, 1)

            def relay_quarter(it, q):
                act.wait_ge(nsa_landed[q % 2], it * 32 + 16 * (q // 2 + 1))
                act.wait_ge(tr, it * NG + (transposed("cmp", q - 1) if q else 0) + OPEN)
                src = nsa[:, q % 2, :].rearrange("p (a b x) -> p a b x", a=2, b=2)
                for a in range(2):
                    copy(relay[:, a, :].rearrange("p (c b e) -> p c b e", c=4, b=2),
                         src[:, a, :, 0:256].rearrange("p b (c e) -> p c b e", c=4)).then_inc(relaid, 1)
                if q == 0:
                    act.wait_ge(out_mm, it * N_OUT + OPEN)
                copy(vsel[:, 4 * q:4 * q + 4, :],
                     nsa[:, q % 2, :].rearrange("p (l x) -> p l x", l=4)[:, :, 384:512]).then_inc(kept, 1)

            act.sem_inc(copied_act, OPEN)
            act.sem_inc(ring_taken, OPEN)
            act.wait_ge(q_zeroed, 2)
            stage_queries(0)
            with act.Fori(0, NB) as it:
                relay_quarter(it, 0)
                for g in range(1, NG, 2):
                    group_copy(act, copy, it, g, copied_act)
                    for q in range(1, 4):
                        if g in (transposed("cmp", q - 1) + 1, transposed("cmp", q - 1) + 2):
                            relay_quarter(it, q)
                exp(it, E_MOBA, Sm, PAST + 64)
                exp(it, E_WIN, Sw, WIN + 64)
                for w in range(2):
                    for ht in range(2):
                        r = 2 * w + ht
                        act.wait_ge(ring_mm, it * N_RING + r + 1 + OPEN)
                        act.activation(hid[:, w, ht, :], ps[4 + r % 2][:, 0:2 * NCMP], ACT.Gelu_apprx_tanh,
                                       bias=t["hbias"][:, r:r + 1]).then_inc(ring_taken, 1)
                act.wait_ge(ring_mm, it * N_RING + 5 + OPEN)
                act.activation(ckT[:, 0:NCMP], ps[4][:, 0:NCMP], ACT.Identity, bias=t["vecT"][:, V_B2:V_B2 + 1])\
                   .then_inc(ring_taken, 1)
                act.wait_ge(ring_mm, it * N_RING + 6 + OPEN)
                copy(cv[0:NCMP, :], ps[5][0:NCMP, 0:P]).then_inc(ring_taken, 1)
                prob_copies(it, PTm, 6)
                exp(it, E_CMP, Sc, NCMP)
                act.wait_ge(ring_mm, it * N_RING + 10 + OPEN)
                copy(PTw[0:NCMP, 0, :], ps[5][0:NCMP, 0:64])
                copy(PTw[:, 1:5, :].rearrange("p c r -> p (c r)"), ps[5][:, 64:320])
                copy(PTw[0:64, 5, :], ps[5][0:64, 320:384]).then_inc(ring_taken, 1)
                exp(it, E_SEL, Ss, PAST + 64)
                prob_copies(it, PTs, 10)
                act.wait_ge(small_mm, it * N_SMALL + 2)
                stage_queries(it + 1)

        @block.vector
        def _(dve):
            def ranks(steps, value, n, above, equal, tie, rank):
                one = value.unsqueeze(1).to_broadcast([64, n, n])
                other = value.unsqueeze(2).to_broadcast([64, n, n])
                steps.do(dve.tensor_tensor(above, one, other, ALU.is_gt))
                steps.do(dve.tensor_tensor(equal, one, other, ALU.is_equal))
                steps.do(dve.tensor_tensor(equal, equal, tie.rearrange("p (j i) -> p j i", i=n), ALU.mult))
                steps.do(dve.tensor_tensor(above, above, equal, ALU.add))
                steps.do(dve.tensor_reduce(rank, above, AX.X, ALU.add))

            def take_scores(it, s):
                bank = ps[2 + s % 2][0:64, :]
                dve.wait_ge(scored, it * NM + SCORED.index(last_group(s)) + 1 + OPEN)
                q = s // 2
                c0 = 512 * q
                if s == 8:
                    dst, bias = Sw[:, 0:WIN], c64[:, C_BWIN:C_BWIN + WIN]
                elif s % 2:
                    dve.tensor_reduce(t["gates4"][:, :, q], bank.rearrange("p (l n s) -> p n l s", l=4, n=NMB),
                                      AX.XY, ALU.add)
                    dst, bias = Sm[:, c0:c0 + 512], c64[:, C_BDEC + c0:C_BDEC + c0 + 512]
                else:
                    dst, bias = Ss[:, c0:c0 + 512], c64[:, C_BDEC + c0:C_BDEC + c0 + 512]
                dve.scalar_tensor_tensor(dst, bank, SCALE, bias, ALU.mult, ALU.add).then_inc(scores_taken, 1)

            def row_max(which, S, n):
                dve.tensor_reduce(t["nmax"][:, which:which + 1], S[:, 0:n], AX.X, ALU.max, negate=True)\
                   .then_inc(max_done, 1)

            def inverse(it, steps, which):
                dve.wait_ge(exp_done, it * 4 + which + 1)
                steps.do(dve.reciprocal(t["inv"][:, which:which + 1], t["sums"][:, which:which + 1]))

            for nothing_yet in (copied_dve, scores_taken, small_taken, out_taken):
                dve.sem_inc(nothing_yet, OPEN)
            dve.memset(qa[:, :], 0.0).then_inc(q_zeroed, 1)
            dve.memset(qb[:, :], 0.0).then_inc(q_zeroed, 1)
            dve.memset(t["sel_mask"][:, :], 0.0).then_inc(mask_zeroed, 1)
            dve.wait_ge(mask_zeroed, 1)
            with dve.Fori(0, NB) as it:
                steps = Steps(dve, dve_step, it * DVE_STEPS)
                dve.wait_ge(small_mm, it * N_SMALL + 1)
                own = c64[:, C_BOWN:C_BOWN + 512].rearrange("p (b u) -> p b u", u=64)[:, bass.ds(it, 1), :]\
                    .rearrange("p b u -> p (b u)")
                for n, dst in enumerate([Sm[:, OWN:OWN + 64], Ss[:, OWN:OWN + 64], Sw[:, WIN:WIN + 64]]):
                    last = dve.scalar_tensor_tensor(dst, ps[7][0:64, 64 * n:64 * n + 64], SCALE, own, ALU.mult, ALU.add)
                last.then_inc(small_taken, 1)
                after = {(last_group(s) + 2) // 2 * 2: s for s in range(8)}
                for g in range(0, NG, 2):
                    group_copy(dve, dve.tensor_copy, it, g, copied_dve)
                    if g in after:
                        take_scores(it, after[g])
                take_scores(it, 8)
                dve.wait_ge(scores_taken, it * N_SCORE + 9 + OPEN)
                steps.do(dve.tensor_reduce(t["gate"][:, :], t["gates4"][:, :, :], AX.X, ALU.add))
                ranks(steps, t["gate"][:, :], NMB, t["above8"][:, :, :], t["equal8"][:, :, :],
                      c64[:, C_TIE8:C64W], t["rank"][:, 0:NMB])
                steps.do(dve.tensor_scalar(t["mb_mask"][:, :], t["rank"][:, 0:NMB], float(MTOP), NEG, ALU.is_ge, ALU.mult))
                s4 = Sm[:, 0:PAST].rearrange("p (l n s) -> p l n s", l=SEG, n=NMB)
                steps.do(dve.tensor_tensor(s4, s4, t["mb_mask"][:, :].unsqueeze(1).unsqueeze(3)
                                           .to_broadcast([64, SEG, NMB, SEG]), ALU.add))
                row_max(E_MOBA, Sm, PAST + 64)
                row_max(E_WIN, Sw, WIN + 64)
                dve.wait_ge(small_mm, it * N_SMALL + 2)
                dve.tensor_scalar(Sc[:, 0:NCMP], ps[7][0:64, 0:NCMP], SCALE, None, ALU.mult).then_inc(small_taken, 1)
                dve.wait_ge(small_taken, it * N_SMALL + 2 + OPEN)
                row_max(E_CMP, Sc, NCMP)
                inverse(it, steps, E_CMP)
                dve.tensor_scalar(Sc[:, 0:NCMP], Sc[:, 0:NCMP], t["inv"][:, E_CMP:E_CMP + 1], None, ALU.mult)\
                   .then_inc(pc_ready, 1)
                dve.wait_ge(small_mm, it * N_SMALL + 3)
                steps.do(dve.tensor_reduce(t["imp"][:, :], ps[7][0:64, 4:4 + 4 * CAND].rearrange("p (j n) -> p j n", n=4),
                                           AX.X, ALU.add))
                dve.tensor_tensor(t["imp"][:, :], t["imp"][:, :], ps[7][0:64, 3:3 + 4 * CAND:4], ALU.add)\
                   .then_inc(small_taken, 1)
                dve.wait_ge(small_taken, it * N_SMALL + 3 + OPEN)
                above, equal = [Sm[:, c:c + CAND * CAND].rearrange("p (j i) -> p j i", i=CAND)
                                for c in (0, CAND * CAND)]
                ranks(steps, t["imp"][:, :], CAND, above, equal,
                      c64[:, C_TIE:C_TIE8], t["rank"][:, :])
                steps.do(dve.tensor_scalar(t["sel_mask"][:, 1:1 + CAND], t["rank"][:, :], float(STOP), NEG,
                                           ALU.is_ge, ALU.mult))
                s4 = Ss[:, 0:PAST].rearrange("p (l j s) -> p l j s", l=SEG, j=NSB)
                steps.do(dve.tensor_tensor(s4, s4, t["sel_mask"][:, :].unsqueeze(1).unsqueeze(3)
                                           .to_broadcast([64, SEG, NSB, 4]), ALU.add))
                row_max(E_SEL, Ss, PAST + 64)
                inverse(it, steps, E_MOBA)
                dve.wait_ge(out_mm, it * N_OUT + 1 + OPEN)
                dve.tensor_scalar(t["Om"][:, :], ps[6][0:64, :], t["inv"][:, E_MOBA:E_MOBA + 1], None, ALU.mult)\
                   .then_inc(out_taken, 1)
                inverse(it, steps, E_WIN)
                dve.wait_ge(out_mm, it * N_OUT + 2 + OPEN)
                dve.tensor_copy(t["On"][:, 0, :], ps[6][0:64, 0:P])
                dve.tensor_scalar(t["On"][:, 2, :], ps[6][0:64, P:2 * P], t["inv"][:, E_WIN:E_WIN + 1], None, ALU.mult)\
                   .then_inc(out_taken, 1)
                inverse(it, steps, E_SEL)
                dve.wait_ge(out_mm, it * N_OUT + 3 + OPEN)
                dve.tensor_scalar(t["On"][:, 1, :], ps[6][0:64, 0:P], t["inv"][:, E_SEL:E_SEL + 1], None, ALU.mult)\
                   .then_inc(out_taken, 1)
                dve.wait_ge(small_mm, it * N_SMALL + 4)
                for half in range(2):
                    rows64 = slice(DH * half, DH * half + DH)
                    dve.tensor_copy(oT[rows64, BR_MOBA, :, bass.ds(it * T, T)],
                                    ps[7][rows64, 8 * half:8 * half + 320].rearrange("p (g c) -> p g c", c=80)[:, :, 0:T])
                    last = dve.tensor_copy(oT[rows64, BR_CMP:, :, bass.ds(it * T, T)],
                                           ps[7][rows64, 256:448].rearrange("p (c v g t) -> p c v g t", c=3, v=KV, g=G)
                                           [:, :, half, :, :])
                last.then_inc(small_taken, 1)
                assert steps.n == DVE_STEPS, steps.n
            dve.wait_ge(small_taken, NB * N_SMALL + OPEN)


def square_norm(nc, pe, t, bank, sq_done, first, ss_mm):
    for k in range(KT):
        pe.wait_ge(sq_done, first + k + 1)
        last = pe.matmul(bank[:, 0:TOK], t["ones"][:, :], t["sq"][:, k, :], start=k == 0, stop=k == KT - 1)
    last.then_inc(ss_mm, 1)


def back_block(nc, sem, t, d, ps):
    slab_landed = [sem(f"b_slab_landed{s}") for s in range(SLOTS)]
    sp_turns = sem("b_sp_turns")
    u_back, x_back, o_back, exp_landed, o_whole = sem("b_u_back"), sem("b_x_back"), sem("b_o_back"), sem("b_expand"), sem("b_o_whole")
    ge_mm, ge_taken, ob_done = sem("b_ge_mm"), sem("b_ge"), sem("b_ob")
    gate_mm, gate_done, y_mm, z_part, z_done = (sem("b_gate_mm"), sem("b_gate"), sem("b_y_mm"), sem("b_z_part"),
                                                sem("b_z"))
    mix_mm, x_step, x_done = sem("b_mix_mm"), sem("b_x_step"), sem("b_x")
    sq_done, ss_mm, root_done = sem("b_sq"), sem("b_ss_mm"), sem("b_root")
    h_pre, h_mid, h_done = sem("b_h_pre"), sem("b_h_mid"), sem("b_h")
    a_mm, b_mm, silu_done, f_done = sem("b_a_mm"), sem("b_b_mm"), sem("b_silu"), sem("b_f")
    down_mm, y_done, y_tr, y_act, y_dve, dve_step, stored = (sem("b_down_mm"), sem("b_y"), sem("b_y_tr"), sem("b_y_act"),
                                                             sem("b_y_dve"), sem("b_dve_step"), sem("b_stored"))
    slab, xT, uT, oT, sq = t["slab"], t["xT"], t["uT"], t["oT"], t["sq"]
    gn, ex, ob, zT, GT, gates, prod, yn = (t["gn"], t["expand"], t["ob"], t["zT"], t["GT"], t["gates"], t["prod"],
                                           t["yn"])
    mod, ident = t["mod"], t["ident"]
    N_MIX, N_OUT, N_GU, N_DOWN = 0, 16, 20, 42

    with nc.Block() as block:

        @block.sync
        def _(sp):
            def load(n, dst, src):
                sp.dma_start(dst, src).then_inc(slab_landed[n % SLOTS], 16)

            def in_tiles(n, k, values=SLABW):
                return slab[:, n % SLOTS, 0:values].rearrange("p (k n) -> p k n", k=k)

            w_in = d["w_in"].rearrange("(k p) n -> p k n", p=P)
            sp.dma_start(uT[:, :, :].rearrange("p k n -> p (k n)"), d["spill_u"]).then_inc(u_back, 16)
            w_pa = d["w_pa"].rearrange("(k p) n -> p k n", p=P)
            w_pb = d["w_pb"].rearrange("(v g e) n -> v e g n", v=KV, g=G)
            with sp.Fori(0, 4) as it:
                for i in range(4):
                    sp.wait_ge(gate_mm if i < 2 else y_mm, it * 4 + i % 2 - 1 + OPEN)
                    apart(sp, sp_turns)
                    cols = bass.ds(it * 256, 256)
                    if i < 2:
                        load(i, in_tiles(i, KT), w_in[:, :, bass.ds(it * 256 + (GB if i else GA), 256)])
                    elif i == 2:
                        load(i, in_tiles(i, 4, 1024), w_pa[:, :, cols])
                    else:
                        for v in range(KV):
                            sp.dma_start(slab[DH * v:DH * v + DH, i, 0:1024].rearrange("p (k n) -> p k n", k=4),
                                         w_pb[v][:, :, cols]).then_inc(slab_landed[i], 16)
            sp.dma_start(xT[:, :, :].rearrange("p k n -> p (k n)"), d["spill_x"]).then_inc(x_back, 16)
            w_out = d["w_out"].rearrange("(k p) n -> p k n", p=P)
            for i in range(4):
                sp.wait_ge(gate_mm if i < 2 else y_mm, 15 + i % 2 + OPEN)
                load(N_OUT + i, in_tiles(i, KT), w_out[:, :, 256 * i:256 * i + 256])
            w_gu = d["w_gu"].rearrange("(k p) n -> p k n", p=P)
            with sp.Fori(0, 5) as it:
                for i in range(4):
                    sp.wait_ge(b_mm if i % 2 else a_mm, it * 4 + 2 * (i // 2) - 2 + OPEN)
                    sp.wait_ge(mix_mm, 2 * i + 2)
                    load(N_GU + i, in_tiles(i, KT), w_gu[:, :, bass.ds(it * 512 + 256 * (i // 2) + FF * (i % 2), 256)])
            for i in range(2):
                sp.wait_ge(b_mm if i else a_mm, 18 + OPEN)
                load(N_GU + 20 + i, in_tiles(i, KT), w_gu[:, :, 2560 + FF * i:2816 + FF * i])
            w_down = d["w_down"].rearrange("(f p) n -> p f n", p=P)

            sp.wait_ge(a_mm, 20 + OPEN)
            load(N_DOWN, in_tiles(N_DOWN, 2), w_down[:, 0:2, :])
            with sp.Fori(0, 2) as it:
                for i in range(4):
                    n = N_DOWN + 1 + i
                    sp.wait_ge(down_mm, it * 4 + i - 2 + OPEN)
                    if i < 3:
                        sp.wait_ge(b_mm if i % 2 == 0 else a_mm, (20 if i == 0 else 22) + OPEN)
                    else:
                        apart(sp, sp_turns)
                    load(n, in_tiles(n, 2), w_down[:, bass.ds(it * 8 + 2 + 2 * i, 2), :])
            for i in range(2):
                sp.wait_ge(down_mm, 6 + i + OPEN)
                load(N_DOWN + 9 + i, in_tiles(N_DOWN + 9 + i, 2), w_down[:, 18 + 2 * i:20 + 2 * i, :])
            for i, (t0, n) in enumerate(T_TILES):
                sp.wait_ge(y_act, i + 1)
                sp.wait_ge(y_dve, i + 1)
                dst = d["y_sample"] if i == 2 else d["y_prompt"][t0:t0 + n, :]
                sp.dma_start(dst, yn[0:n, i, :]).then_inc(stored, 16)
            sp.wait_ge(stored, 48)

        @block.gpsimd
        def _(pool):
            pool.dma_start(ex[:, :], d["c_expand"]).then_inc(exp_landed, 16)
            for br in range(4):
                pool.dma_start(oT[:, br, :, 0:SEQ],
                               d["spill_o"][:, br * 4 * SEQ:(br + 1) * 4 * SEQ].rearrange("p (g t) -> p g t", g=4))\
                    .then_inc(o_back, 16)
                pool.tensor_copy(oT[:, br, :, SEQ:TOK], t["oT_s"][:, br, :, :]).then_inc(o_whole, 1)
            pool.wait_ge(exp_landed, 16)

        @block.tensor
        def _(pe):
            for nothing_yet in (gate_mm, y_mm, a_mm, b_mm, down_mm):
                pe.sem_inc(nothing_yet, OPEN)
            pe.wait_ge(exp_landed, 16)
            for n in range(12):
                c, g = n // 4, n % 4
                if n >= 4:
                    pe.wait_ge(ge_taken, n - 3)
                pe.matmul(ps[n % 4][:, 0:TOK], ex[:, (c * 4 + g) * P:(c * 4 + g) * P + P], gn[:, :],
                          start=True, stop=True).then_inc(ge_mm, 1)
            pe.wait_ge(ge_taken, 12)
            pe.wait_ge(u_back, 16)
            with pe.Fori(0, 4) as it:
                for m in range(2):
                    for i in range(4):
                        bank = ps[4 * m + i]
                        if m == 0:
                            pe.wait_ge(slab_landed[i], it * (32 if i == 3 else 16) + (32 if i == 3 else 16))
                        if i == 0:
                            pe.wait_ge(z_done, it * 2 + m - 1 + OPEN)
                        if i < 2:
                            for k in range(KT):
                                last = pe.matmul(bank[:, 0:TOK], slab[:, i, 256 * k + P * m:256 * k + P * m + P],
                                                 uT[:, k, :], start=k == 0, stop=k == KT - 1)
                            last.then_inc(gate_mm, 1)
                        else:
                            if m == 0:
                                pe.wait_ge(ob_done, 1)
                            for k in range(4):
                                rhs = oT[:, 0, k, :] if i == 2 else ob[:, k, :]
                                last = pe.matmul(bank[:, 0:TOK], slab[:, i, 256 * k + P * m:256 * k + P * m + P],
                                                 rhs, start=k == 0, stop=k == 3)
                            last.then_inc(y_mm, 1)

            def landed(n, it=0):
                s = n % SLOTS
                pe.wait_ge(slab_landed[s], it * 16 + 16 * (n // SLOTS + 1) + (64 if s == 3 else 0))

            pe.wait_ge(z_done, 8 + OPEN)
            for m in range(KT):
                n = N_OUT + m // 2
                if m % 2 == 0:
                    landed(n)
                if m >= 2:
                    pe.wait_ge(x_done, m - 1)
                for k in range(KT):
                    c0 = 256 * k + P * (m % 2)
                    last = pe.matmul(ps[m % 2][:, 0:TOK], slab[:, n % SLOTS, c0:c0 + P], zT[:, k, :],
                                     start=k == 0, stop=k == KT - 1)
                last.then_inc(mix_mm, 1)
            square_norm(nc, pe, t, ps[7], sq_done, 0, ss_mm)

            def up(it, group):
                for f in range(2):
                    pe.wait_ge(f_done, it * 4 + 2 * group + f - 3 + OPEN)
                    for half in range(2):
                        n = N_GU + 2 * group + half
                        if f == 0:
                            landed(n, it)
                        bank = ps[4 * group + 2 * f + half]
                        for k in range(KT):
                            c0 = 256 * k + P * f
                            if group == f == half == 0:
                                pe.wait_ge(h_done, k + 1)
                            last = pe.matmul(bank[:, 0:TOK], slab[:, n % SLOTS, c0:c0 + P], uT[:, k, :],
                                             start=k == 0, stop=k == KT - 1)
                        last.then_inc(b_mm if half else a_mm, 1)

            with pe.Fori(0, 5) as it:
                for group in range(2):
                    up(it, group)
            up(5, 0)

            def down(n, it, tile, first=False, final=False):
                landed(n, it)
                for f in range(2):
                    for m in (4, 5, 6, 7, 0, 1, 2, 3):
                        if first and f == 0 and m % 4 == 0:
                            pe.wait_ge(f_done, (FT - 2 if m else FT) + OPEN)
                        c0 = D * f + P * m
                        rhs = GT[:, tile + f, :] if isinstance(tile, int) else \
                            GT[:, bass.ds(tile + f, 1), :].rearrange("p a b -> p (a b)")
                        last = pe.matmul(ps[m][:, 0:TOK], slab[:, n % SLOTS, c0:c0 + P], rhs,
                                         start=first and f == 0, stop=final and f == 1, skip_group_check=True)
                last.then_inc(down_mm, 1)

            down(N_DOWN, 0, 0, first=True)
            with pe.Fori(0, 2) as it:
                for i in range(4):
                    down(N_DOWN + 1 + i, it, it * 8 + 2 + 2 * i)
            down(N_DOWN + 9, 0, 18)
            down(N_DOWN + 10, 0, 20, final=True)
            pe.wait_ge(x_done, 2 * KT)
            square_norm(nc, pe, t, ps[7], sq_done, KT, ss_mm)
            for j in range(6):
                i, half = j // 2, j % 2
                pe.wait_ge(y_done, 4 * half + 4)
                t0, n = T_TILES[i]
                if j >= 2:
                    pe.wait_ge(y_dve if half else y_act, i)
                for k in range(4):
                    last = pe.transpose(ps[half][0:n, P * k:P * k + P], uT[:, 4 * half + k, t0:t0 + n], ident[:, :])
                last.then_inc(y_tr, 1)

        @block.scalar
        def _(act):
            def root(n):
                for k in range(KT):
                    act.wait_ge(x_done, (n - 1) * KT + k + 1)
                    act.activation(sq[:, k, :], xT[:, k, :], ACT.Square).then_inc(sq_done, 1)
                act.wait_ge(ss_mm, n)
                act.activation(t["root"][:, :], ps[7][:, 0:TOK], ACT.Sqrt, bias=t["eps"][:, 0:1], scale=1.0 / D)\
                   .then_inc(root_done, 1)

            with act.Fori(0, 4) as it:
                for m in range(2):
                    act.wait_ge(z_done, it * 2 + m - 1 + OPEN)
                    for i in range(2):
                        act.wait_ge(gate_mm, it * 4 + 2 * m + i + 1 + OPEN)
                        act.activation(gates[:, m, i, :], ps[4 * m + i][:, 0:TOK], ACT.Sigmoid).then_inc(gate_done, 1)
            root(1)

            def silu(f, it):
                act.wait_ge(f_done, it * 4 + f - 3 + OPEN)
                act.wait_ge(a_mm, it * 4 + f + 1 + OPEN)
                act.activation(gates[:, f % 4 // 2, f % 2, :], ps[2 * (f % 4)][:, 0:TOK], ACT.Silu).then_inc(silu_done, 1)

            with act.Fori(0, 5) as it:
                for f in range(4):
                    silu(f, it)
            for f in range(20, 22):
                silu(f, 0)
            root(2)
            for i, (t0, n) in enumerate(T_TILES):
                act.wait_ge(y_tr, 2 * i + 1)
                act.activation(yn[0:n, i, 0:512], ps[0][0:n, :], ACT.Copy).then_inc(y_act, 1)

        @block.vector
        def _(dve):
            steps = Steps(dve, dve_step)
            dve.sem_inc(z_done, OPEN)
            dve.sem_inc(f_done, OPEN)
            dve.wait_ge(o_back, 64)
            dve.wait_ge(o_whole, 4)
            for n in range(12):
                c, g = n // 4, n % 4
                dve.wait_ge(ge_mm, n + 1)
                dve.tensor_tensor(oT[:, 1 + c, g, :], oT[:, 1 + c, g, :], ps[n % 4][:, 0:TOK], ALU.mult)\
                   .then_inc(ge_taken, 1)
            dve.wait_ge(ge_taken, 12)
            steps.do(dve.tensor_tensor(ob[:, :, :], oT[:, 1, :, :], oT[:, 2, :, :], ALU.add))
            dve.tensor_tensor(ob[:, :, :], ob[:, :, :], oT[:, 3, :, :], ALU.add).then_inc(ob_done, 1)
            with dve.Fori(0, 4) as it:
                for m in range(2):
                    dve.wait_ge(z_done, it * 2 + m + OPEN)
                    for i in range(2):
                        dve.wait_ge(gate_done, it * 4 + 2 * m + i + 1)
                        dve.wait_ge(y_mm, it * 4 + 2 * m + i + 1 + OPEN)
                        dve.tensor_tensor(prod[:, i, :], gates[:, m, i, :], ps[4 * m + 2 + i][:, 0:TOK], ALU.mult)\
                           .then_inc(z_part, 1)
                    dve.wait_ge(z_part, it * 4 + 2 * m + 2)
                    dve.tensor_tensor(zT[:, bass.ds(it * 2 + m, 1), :].rearrange("p a b -> p (a b)"), prod[:, 0, :],
                                      prod[:, 1, :], ALU.add).then_inc(z_done, 1)

            def residual(m, bank, gate, before):
                dve.wait_ge(x_done, m + before)
                dve.scalar_tensor_tensor(xT[:, m, 0:SEQ], bank[:, 0:SEQ], mod[:, gate + m, 0:1], xT[:, m, 0:SEQ],
                                         ALU.mult, ALU.add)
                y = bank[:, SEQ:TOK].rearrange("p (b t) -> p b t", t=T)
                steps.do(dve.tensor_tensor(prod[:, 0, 0:NS].rearrange("p (b t) -> p b t", t=T), y,
                                           mod[:, gate + m, 1:9].unsqueeze(2).to_broadcast([P, NB, T]), ALU.mult))
                dve.tensor_tensor(xT[:, m, SEQ:TOK], xT[:, m, SEQ:TOK], prod[:, 0, 0:NS], ALU.add).then_inc(x_done, 1)

            dve.wait_ge(x_back, 16)
            for m in range(KT):
                dve.wait_ge(mix_mm, m + 1)
                residual(m, ps[m % 2], 16, 0)
            dve.wait_ge(root_done, 1)
            steps.do(dve.reciprocal(t["rstd"][:, :], t["root"][:, :]))
            modulate(dve, t, 1, 24, h_pre, h_mid, h_done)

            def product(f, it, col):
                dve.wait_ge(silu_done, it * 4 + f + 1)
                dve.wait_ge(b_mm, it * 4 + f + 1 + OPEN)
                dst = GT[:, col, :] if isinstance(col, int) else GT[:, bass.ds(col, 1), :].rearrange("p a b -> p (a b)")
                dve.tensor_tensor(dst, gates[:, f % 4 // 2, f % 2, :], ps[2 * (f % 4) + 1][:, 0:TOK], ALU.mult)\
                   .then_inc(f_done, 1)

            with dve.Fori(0, 5) as it:
                for f in range(4):
                    product(f, it, it * 4 + f)
            for f in range(20, 22):
                product(f, 0, f)
            dve.wait_ge(down_mm, 11 + OPEN)
            for m in range(KT):
                residual(m, ps[m], 40, KT)
            dve.wait_ge(root_done, 2)
            steps.do(dve.reciprocal(t["rstd"][:, :], t["root"][:, :]))
            for k in range(KT):
                dve.scalar_tensor_tensor(uT[:, k, :], xT[:, k, :], t["vecT"][:, V_GZ + k:V_GZ + k + 1], t["rstd"][:, :],
                                         ALU.mult, ALU.mult).then_inc(y_done, 1)
            for i, (t0, n) in enumerate(T_TILES):
                dve.wait_ge(y_tr, 2 * i + 2)
                dve.tensor_copy(yn[0:n, i, 512:1024], ps[1][0:n, :]).then_inc(y_dve, 1)


def build(nc, d):
    with ExitStack() as persist:
        def sb(stack, name, shape, dt=F32):
            return stack.enter_context(nc.sbuf_tensor("t_" + name, shape, dt))

        def sem(name):
            return persist.enter_context(nc.semaphore(name))

        t = {}
        for name, shape in [("slab", [P, SLOTS, SLABW]), ("ident", [P, P]), ("ones", [P, P]), ("c64", [64, C64W]),
                            ("vecT", [P, NVEC]), ("mod", [P, 48, 9]), ("amp", [P, 2, KT, 9]), ("eps", [P, 1]),
                            ("qaT_s", [P, 4, NS + T]), ("qbT_s", [P, 4, NS + T]), ("kaT_s", [P, 4, NS]),
                            ("ksT_s", [P, NS]), ("kwT_s", [P, NS]), ("rows_s", [NS, ROWW]),
                            ("oT_s", [P, 4, 4, NS]), ("hbias", [P, 4]),
                            ("w2", [P, 2, 2, DH]), ("b2v", [1, DH]), ("seg_col", [P, 1]), ("gn", [24, TOK])]:
            t[name] = sb(persist, name, shape)
        t["table"], t["index"] = sb(persist, "table", [P, NB], I32), sb(persist, "index", [P, NB], U32)
        ps = [persist.enter_context(nc.psum_tensor(f"ps{i}", [P, 512], F32)) for i in range(8)]
        with ExitStack() as early:
            for name, shape in [("rows_p", [P, 2, ROWW]), ("qaT_p", [P, 4, SEQ]), ("qbT_p", [P, 4, SEQ]),
                                ("kaT_p", [P, 4, SEQ]), ("ksT_p", [P, SEQ]), ("kwT_p", [P, SEQ]),
                                ("cp", [P, CPW])]:
                t[name] = sb(early, name, shape)
            with ExitStack() as temps:
                for name, shape in [("root", [P, TOK]), ("rstd", [P, TOK]), ("wgn", [P, KT * 24]), ("xn", [P, 3, D]), ("cn", [9, D]), ("modn", [9, NADA * D]), ("vecn", [P, P]), ("cT", [P, 72]),
                                    ("xT", [P, KT, TOK]), ("uT", [P, KT, TOK]), ("sq", [P, KT, TOK])]:
                    t[name] = sb(temps, name, shape)
                front_block(nc, sem, t, d, ps)
            with ExitStack() as temps:
                for name, shape in [("segs", [PSEG, 8, 4, 2, DH]), ("XTp", [P, 2, 2, 8, PC1]),
                                    ("hidn", [PC1, 512]), ("hid_p", [P, 2, 2, 2 * PCMP]), ("ckT_p", [P, PSEG]), ("cv_p", [PSEG, P]),
                                    ("S_p", [P, 3, 2048]), ("PT_p", [P, 2, 2, H, P]),
                                    ("Sc_p", [P, 256]), ("PTc_p", [PSEG, 2 * H, P]), ("oT_p", [P, 4, 4, SEQ]),
                                    ("nmax_p", [P, 3, H]), ("sum_p", [P, 3, H]), ("rsum_p", [P, H]),
                                    ("cstat_p", [P, 2 * H])]:
                    t[name] = sb(temps, name, shape)
                prompt_block(nc, sem, t, d, ps)
        with ExitStack() as mid:
            for name, shape, dt in [("Kr", [P, 8, 512], F32), ("Vr", [P, V_SLOTS, 512], F32), ("nsa", [P, 2, 2048], F32),
                                    ("relay", [P, 2, 512], F32), ("vsel", [P, SEG, P], F32),
                                    ("XT", [P, 2, KV, 8, NSEG], F32), ("KTr", [P, 4, 512], F32),
                                    ("Sm", [64, PAST + 64], F32), ("Ss", [64, PAST + 64], F32), ("Sw", [64, WIN + 64], F32),
                                    ("Sc", [64, P], F32), ("PTm", [P, SEG + 1, 64], F32), ("PTs", [P, SEG + 1, 64], F32),
                                    ("PTw", [P, 6, 64], F32), ("hid", [P, 2, 2, 2 * NCMP], F32), ("ckT", [P, P], F32),
                                    ("cv", [P, P], F32), ("wkv", [P, 4, 256], F32), ("qa_cur", [P, 328], F32),
                                    ("qb_cur", [P, 64], F32), ("above8", [64, NMB, NMB], F32),
                                    ("equal8", [64, NMB, NMB], F32), ("gates4", [64, NMB, 4], F32), ("gate", [64, NMB], F32),
                                    ("rank", [64, CAND], F32), ("mb_mask", [64, NMB], F32), ("sel_mask", [64, NSB], F32),
                                    ("imp", [64, CAND], F32), ("nmax", [64, 4], F32), ("sums", [64, 4], F32),
                                    ("inv", [64, 4], F32), ("Om", [64, 512], F32), ("On", [64, 3, P], F32),
                                    ("index_now", [P, 2], U32)]:
                t[name] = sb(mid, name, shape, dt)
            decode_block(nc, sem, t, d, ps)
        with ExitStack() as late:
            for name, shape in [("root", [P, TOK]), ("rstd", [P, TOK]), ("xT", [P, KT, TOK]), ("uT", [P, KT, TOK]),
                                ("sq", [P, KT, TOK]), ("oT", [P, 4, 4, TOK]),
                                ("expand", [24, 12 * P]), ("ob", [P, 4, TOK]), ("zT", [P, KT, TOK]),
                                ("GT", [P, FT, TOK]), ("gates", [P, 2, 2, TOK]), ("prod", [P, 2, TOK]),
                                ("yn", [P, 3, D])]:
                t[name] = late.enter_context(nc.sbuf_tensor("b_" + name, shape, F32))
            back_block(nc, sem, t, d, ps)


_OUTS = [("y_prompt", (1, 256, 1024)), ("y_sample", (8, 8, 1024)), ("moba_kv_prompt", (1, 256, 2, 8, 64)),
         ("nsa_kv_prompt", (1, 256, 4, 2, 64)), ("nsa_win_prompt", (1, 256, 2, 2, 64)),
         ("moba_kv_sample", (8, 8, 2, 8, 64)), ("nsa_kv_sample", (8, 8, 4, 2, 64)),
         ("nsa_win_sample", (8, 512, 2, 2, 64))]


def constants():
    import numpy as np
    slope = 2.0 ** -(np.arange(H) + 1.0)
    ident = np.eye(P)
    ones = np.ones((P, P))
    row_h, row_t = np.repeat(np.arange(H), T), np.tile(np.arange(T), H)
    row_kv = row_h // G
    c64 = np.zeros((64, C64W))
    c64[:, C_GSUM:C_BDEC] = (row_kv[:, None] == row_kv) & (row_t[:, None] == row_t)
    kpos = SEG * np.arange(NSEG)[None, :] + np.arange(SEG)[:, None]
    c64[:, C_BDEC:C_BOWN] = -slope[row_h][:, None] * (PAST + row_t[:, None] - kpos.reshape(1, -1))
    own = np.full((64, NB, NB, T), NEG)
    for r in range(64):
        for b in range(NB):
            for u in range(row_t[r] + 1):
                own[r, b, b, u] = -slope[row_h[r]] * (row_t[r] - u)
    c64[:, C_BOWN:C_BWIN] = own.reshape(64, -1)
    wpos = PAST - WIN + (4 * np.arange(128)[None, :] + np.arange(4)[:, None]).reshape(1, -1)
    qpos = PAST + row_t[:, None]
    c64[:, C_BWIN:C_TIE] = np.where(wpos > qpos - WIN, -slope[row_h][:, None] * (qpos - wpos), NEG)
    c64[:, C_TIE:C_TIE8] = (np.arange(CAND)[None, :] < np.arange(CAND)[:, None]).reshape(1, -1)
    c64[:, C_TIE8:C64W] = (np.arange(NMB)[None, :] < np.arange(NMB)[:, None]).reshape(1, -1)
    cp = np.zeros((P, CPW))
    q, k = np.arange(P)[:, None, None], np.arange(256)[None, None, :]
    for qt, c0, nk in [(0, C_BP0, 128), (1, C_BP1, 256)]:
        dist = q + P * qt - k[:, :, :nk]
        cp[:, c0:c0 + 8 * nk] = np.where(dist >= 0, -slope[None, :, None] * dist, NEG).reshape(P, -1)
    n = np.arange(PSEG)[None, None, :]
    seen = (SEG * n + 2 * SEG - 1 <= np.arange(P)[:, None, None] + P * np.arange(2)[None, :, None]) & (n < PCMP)
    cp[:, C_MADD:C_MMUL] = np.where(seen, 0.0, NEG).reshape(P, -1)
    cp[:, C_MMUL:CPW] = seen.reshape(P, -1)
    expand = np.zeros((24, 3, 4, P))
    for kv in range(KV):
        for g in range(G):
            for c in range(3):
                expand[(kv * G + g) * 3 + c, c, g, DH * kv:DH * kv + DH] = 1.0
    return {"c_ident": ident, "c_ones": ones, "c_64": c64, "c_p": cp, "c_expand": expand.reshape(24, -1),
            "c_seg": np.arange(P)[:, None] % (PAGE // SEG)}


def kernel(**inputs):
    import numpy as np
    import concourse.bacc as bacc
    from concourse.bass_utils import run_bass_kernel_spmd

    nc = bacc.Bacc("TRN2", target_bir_lowering=False, num_devices=1)
    arrays, d = {}, {}
    shapes = {
        "x_prompt": (256, 1024), "x_sample": (64, 1024), "cache_moba_kv": (160 * 8, 16 * 1024),
        "cache_nsa_kv": (160 * 8, 16 * 512), "cache_nsa_win": (8, 512, 256)}
    for name, a in inputs.items():
        arrays[name] = np.ascontiguousarray(a)
    for name, a in constants().items():
        arrays[name] = np.ascontiguousarray(a.astype(np.float32))
    for name, a in arrays.items():
        if name in shapes:
            arrays[name] = a = a.reshape(shapes[name])
        d[name] = nc.dram_tensor(name, a.shape, mybir.dt.from_np(a.dtype), kind="ExternalInput").ap()
    flat = {"y_prompt": (256, 1024), "y_sample": (64, 1024), "moba_kv_prompt": (256, 1024), "nsa_kv_prompt": (256, 512),
            "nsa_win_prompt": (256, 256), "moba_kv_sample": (64, 1024), "nsa_kv_sample": (64, 512),
            "nsa_win_sample": (8, 512, 256)}
    for name, _ in _OUTS:
        d[name] = nc.dram_tensor(name, flat[name], F32, kind="ExternalOutput").ap()
    for name, shape in [("spill_x", (P, KT * TOK)), ("spill_u", (P, KT * TOK)), ("spill_o", (P, 16 * SEQ))]:
        d[name] = nc.dram_tensor(name, shape, F32, kind="Internal").ap()
    build(nc, d)
    r = run_bass_kernel_spmd(nc, [arrays], core_ids=[0]).results[0]
    return tuple(np.asarray(r[name]).reshape(shape) for name, shape in _OUTS)
```

```python
from contextlib import ExitStack

import concourse.bass as bass
from concourse import mybir

F32 = mybir.dt.float32
F32R = mybir.dt.float32r
I32 = mybir.dt.int32
U32 = mybir.dt.uint32
ALU = mybir.AluOpType
ACT = mybir.ActivationFunctionType
AX = mybir.AxisListType

P = 128
D = 1024
KT = D // P
SEQ = 256
NB = 8
T = 8
NS = NB * T
TOK = SEQ + NS
PAST = 2048
PAGE = 128
DH = 64
H = 8
KV = 2
G = H // KV
SEG = 16
NSEG = PAST // SEG
NCMP = NSEG - 1
PSEG = SEQ // SEG
PCMP = PSEG - 1
PC1 = 2 * PCMP + 1
MB = 256
NMB = PAST // MB
MTOP = 3
SB = 64
NSB = PAST // SB
CAND = NSB - 2
STOP = 16 - 3
WIN = 512
FF = 2816
FT = FF // P
NADA = 6
EPS = 1e-6
NEG = -1e30
SCALE = DH ** -0.5
QA, KA, VA, QB, KC, GN, GA, GB = 0, 512, 1024, 1536, 2048, 2816, 2840, 3864
RKA, RVA, RKC, RKS, RVS, RKW, RVW, ROWW = 0, 512, 1024, 1280, 1408, 1536, 1664, 1792
SLOTS = 4
OPEN = 4
SLABW = 2048
V_ADA, V_GA, V_GF, V_GZ, V_B1, V_PE, V_B2, NVEC = 0, 48, 56, 64, 72, 76, 108, 109
C_GSUM, C_BDEC, C_BOWN, C_BWIN, C_TIE, C_TIE8 = 0, 64, 64 + PAST, 64 + PAST + 512, 64 + PAST + 1024, 64 + PAST + 1024 + CAND * CAND
C64W = C_TIE8 + 64
C_BP0, C_BP1, C_MADD, C_MMUL, CPW = 0, 1024, 3072, 3104, 3136
T_TILES = [(0, 128), (128, 128), (256, 64)]


class Steps:

    def __init__(self, eng, sem, base=0):
        self.eng, self.sem, self.base, self.n = eng, sem, base, 0

    def do(self, ins):
        self.n += 1
        ins.then_inc(self.sem, 1)
        self.eng.wait_ge(self.sem, self.base + self.n)


def apart(eng, turns):
    eng.sem_inc(turns, 1)


def front_block(nc, sem, t, d, ps):
    loaded, x_loaded, c_loaded = sem("f_loaded"), sem("f_x_loaded"), sem("f_c_loaded")
    slab_landed = [sem(f"f_slab_landed{s}") for s in range(SLOTS)]
    slab_used = [sem(f"f_slab_used{s}") for s in range(SLOTS)]
    silu_done, x_tr, vec_tr, c_tr = sem("f_silu"), sem("f_x_tr"), sem("f_vec_tr"), sem("f_c_tr")
    xT_dve, xT_act, vecT_done, cT_done = sem("f_xT_dve"), sem("f_xT_act"), sem("f_vecT"), sem("f_cT")
    ada_mm, mod_done, sq_done, ss_mm, root_done = sem("f_ada_mm"), sem("f_mod"), sem("f_sq"), sem("f_ss_mm"), sem("f_root")
    u_done, q_mm, q_dve, q_act = sem("f_u"), sem("f_q_mm"), sem("f_q_dve"), sem("f_q_act")
    row_mm, row_dve, row_act = sem("f_row_mm"), sem("f_row_dve"), sem("f_row_act")
    kt_tr, kt_dve, kt_act = sem("f_kt_tr"), sem("f_kt_dve"), sem("f_kt_act")
    dve_step, stored, spilled = sem("f_dve_step"), sem("f_stored"), sem("f_spilled")
    u_pre, u_mid, modn_done, mod_tr = sem("f_u_pre"), sem("f_u_mid"), sem("f_modn"), sem("f_mod_tr")
    modn = t["modn"]
    table_landed, later_loaded, gn_mm, gn_done = sem("f_table"), sem("f_later"), sem("f_gn_mm"), sem("f_gn")
    slab, xn, cn, vecn = t["slab"], t["xn"], t["cn"], t["vecn"]
    xT, uT, sq, cT, vecT, mod = t["xT"], t["uT"], t["sq"], t["cT"], t["vecT"], t["mod"]
    ident, ones = t["ident"], t["ones"]
    rows_p, rows_s = t["rows_p"], t["rows_s"]
    NROWJ = 21

    def w_slab(w, c0, n):
        return w[:, c0:c0 + n] if isinstance(c0, int) else w[:, bass.ds(c0, n)]

    with nc.Block() as block:

        @block.sync
        def _(sp):
            sp.dma_start(ident[:, :], d["c_ident"]).then_inc(c_loaded, 16)
            sp.dma_start(cn[0:1, :], d["c_prompt"]).then_inc(c_loaded, 16)
            sp.dma_start(cn[1:1 + NB, :], d["c_sample"]).then_inc(c_loaded, 16)
            w_ada = d["w_ada"].rearrange("(k p) n -> p k n", p=P)
            with sp.Fori(0, NADA) as it:
                for s in range(SLOTS):
                    sp.wait_ge(slab_used[s], it + OPEN)
                    half = 4 * (s % 2)
                    sp.dma_start(slab[:, s, :].rearrange("p (k n) -> p k n", k=4),
                                 w_ada[:, half:half + 4, bass.ds(it * D + 512 * (s // 2), 512)])\
                      .then_inc(slab_landed[s], 16)
            w_in = d["w_in"].rearrange("(k p) n -> p k n", p=P)
            for j in range(11):
                s = j % SLOTS
                sp.wait_ge(slab_used[s], NADA + j // SLOTS + OPEN)
                if j in (2, 3):
                    for n, (g, kv) in enumerate([(g, kv) for g in range(2) for kv in range(KV)]):
                        c0 = QB + kv * 256 + (2 * (j - 2) + g) * DH
                        sp.dma_start(slab[:, s, :].rearrange("p (k n) -> p k n", k=KT)[:, :, n * DH:n * DH + DH],
                                     w_in[:, :, c0:c0 + DH]).then_inc(slab_landed[s], 16)
                else:
                    c0 = [QA, QA + 256, 0, 0, KA, KA + 256, VA, VA + 256, KC, KC + 256, KC + 512][j]
                    sp.dma_start(slab[:, s, :].rearrange("p (k n) -> p k n", k=KT),
                                 w_in[:, :, c0:c0 + 256]).then_inc(slab_landed[s], 16)
            sp.wait_ge(u_done, KT)
            sp.dma_start(d["spill_x"], xT[:, :, :].rearrange("p k n -> p (k n)")).then_inc(spilled, 16)
            sp.dma_start(d["spill_u"], uT[:, :, :].rearrange("p k n -> p (k n)")).then_inc(spilled, 16)
            sp.wait_ge(row_dve, 11)
            sp.wait_ge(row_act, 10)
            for i in range(2):
                tok = slice(P * i, P * i + P)
                sp.dma_start(d["moba_kv_prompt"][tok, :], rows_p[:, i, RKA:RKC]).then_inc(stored, 16)
                sp.dma_start(d["nsa_kv_prompt"][tok, :], rows_p[:, i, RKC:RKW]).then_inc(stored, 16)
                sp.dma_start(d["nsa_win_prompt"][tok, :], rows_p[:, i, RKW:ROWW]).then_inc(stored, 16)
            sp.dma_start(d["moba_kv_sample"], rows_s[:, RKA:RKC]).then_inc(stored, 16)
            sp.dma_start(d["nsa_kv_sample"], rows_s[:, RKC:RKW]).then_inc(stored, 16)
            for b in range(NB):
                sp.dma_start(d["nsa_win_sample"][b, WIN - T:WIN, :],
                             rows_s[T * b:T * b + T, RKW:ROWW]).then_inc(stored, 16)
            sp.wait_ge(stored, 16 * (6 + 2 + NB))
            sp.wait_ge(spilled, 32)

        @block.gpsimd
        def _(pool):
            for i, (t0, n) in enumerate(T_TILES):
                src = d["x_sample"] if i == 2 else d["x_prompt"][t0:t0 + n, :]
                pool.dma_start(xn[0:n, i, :], src).then_inc(x_loaded, 16)
            pool.dma_start(vecn[V_ADA:V_GA, :], d["b_ada"].rearrange("(r c) -> r c", c=P)).then_inc(loaded, 16)
            pool.dma_start(vecn[V_GA:V_GF, :], d["g_attn"].rearrange("(r c) -> r c", c=P)).then_inc(loaded, 16)
            pool.dma_start(vecn[V_GF:V_GZ, :], d["g_ffn"].rearrange("(r c) -> r c", c=P)).then_inc(loaded, 16)
            pool.dma_start(vecn[V_GZ:V_B1, :], d["g_final"].rearrange("(r c) -> r c", c=P)).then_inc(loaded, 16)
            pool.dma_start(vecn[V_B1:V_PE, :], d["cmp_b1"].rearrange("w (r c) -> (w r) c", c=P)).then_inc(loaded, 16)
            pool.dma_start(vecn[V_PE:V_B2, :],
                           d["cmp_pe"].rearrange("w (r two) e -> (w r) (two e)", two=2)).then_inc(loaded, 16)
            for kv in range(KV):
                pool.dma_start(vecn[V_B2:NVEC, DH * kv:DH * kv + DH], d["cmp_b2"][0:1, :]).then_inc(loaded, 16)
            pool.dma_start(ones[:, :], d["c_ones"]).then_inc(loaded, 16)
            table = d["page_table"].rearrange("b g -> g b")
            for s in range(PAGE // SEG):
                pool.dma_start(t["table"][s:P:PAGE // SEG, :], table, allow_slow_non_contiguous=True).then_inc(table_landed, 16)
            pool.dma_start(t["seg_col"][:, :], d["c_seg"]).then_inc(table_landed, 16)
            pool.dma_start(t["cp"][:, :], d["c_p"]).then_inc(later_loaded, 16)
            pool.dma_start(t["c64"][:, :], d["c_64"]).then_inc(later_loaded, 16)
            pool.dma_start(t["wgn"][:, :].rearrange("p (k n) -> p k n", k=KT),
                           d["w_in"].rearrange("(k p) n -> p k n", p=P)[:, :, GN:GN + 24]).then_inc(table_landed, 16)
            pool.dma_start(d["nsa_win_sample"][:, 0:WIN - T, :], d["cache_nsa_win"][:, T:WIN, :]).then_inc(later_loaded, 16)
            pool.wait_ge(later_loaded, 48)

        @block.tensor
        def _(pe):
            pe.wait_ge(c_loaded, 48)
            pe.wait_ge(silu_done, 1)
            for k in range(KT):
                last = pe.transpose(ps[5][:, 9 * k:9 * k + 9], cn[0:9, P * k:P * k + P], ident[0:9, 0:9])
            last.then_inc(c_tr, 1)
            pe.wait_ge(cT_done, 1)
            pe.wait_ge(x_loaded, 48)
            for k in range(KT):
                if k >= 4:
                    pe.wait_ge(xT_dve if k % 2 == 0 else xT_act, k // 2 - 1)
                for i, (t0, n) in enumerate(T_TILES):
                    last = pe.transpose(ps[k % 4][:, t0:t0 + n], xn[0:n, i, P * k:P * k + P], ident[0:n, 0:n])
                last.then_inc(x_tr, 1)
            pe.wait_ge(loaded, 16 * 9)
            pe.transpose(ps[4][:, 0:NVEC], vecn[0:NVEC, :], ident[0:NVEC, 0:NVEC]).then_inc(vec_tr, 1)
            for k in range(KT):
                pe.wait_ge(sq_done, k + 1)
                last = pe.matmul(ps[7][:, 0:TOK], ones[:, :], sq[:, k, :], start=k == 0, stop=k == KT - 1)
            last.then_inc(ss_mm, 1)

            def ada(it):
                for g in range(2):
                    pe.wait_ge(modn_done, it * 2 + g - 1 + OPEN)
                    for half in range(2):
                        s = 2 * g + half
                        pe.wait_ge(slab_landed[s], it * 16 + 16)
                        for k in range(4):
                            c0 = 9 * (4 * half + k)
                            last = pe.matmul(ps[5 + g][0:9, :], cT[:, c0:c0 + 9], slab[:, s, 512 * k:512 * k + 512],
                                             start=s % 2 == 0 and k == 0, stop=s % 2 == 1 and k == 3)
                        last.then_inc(slab_used[s], 1)

            def mod_transposes(bank, first, n):
                pe.wait_ge(modn_done, (first + n) // 4 + OPEN)
                for i in range(n):
                    last = pe.transpose(bank[:, 9 * i:9 * i + 9], modn[:, P * (first + i):P * (first + i) + P],
                                        ident[0:9, 0:9])
                last.then_inc(mod_tr, 1)

            for nothing_yet in slab_used:
                pe.sem_inc(nothing_yet, OPEN)
            with pe.Fori(0, 2) as it:
                ada(it)
            mod_transposes(ps[0], 0, 16)
            with pe.Fori(2, NADA) as it:
                ada(it)
            mod_transposes(ps[1], 16, 32)
            pe.wait_ge(u_done, KT)
            for m in range(8):
                s, ct = m // 2, m % 2
                if ct == 0:
                    pe.wait_ge(slab_landed[s], 16 * NADA + (16 if s < 2 else 64))
                if m == 0:
                    pe.wait_ge(mod_done, 2)
                if m >= 2:
                    pe.wait_ge(q_dve if m % 2 == 0 else q_act, m - 1 if m % 2 else m)
                for k in range(KT):
                    w = slab[:, s, 256 * k + P * ct:256 * k + P * ct + P]
                    last = pe.matmul(ps[m % 2][:, 0:TOK], w, uT[:, k, :], start=k == 0, stop=k == KT - 1)
                last.then_inc(q_mm, 1)
                if ct == 1:
                    pe.wait_ge(q_mm, m + 1)
                    pe.sem_inc(slab_used[s], 1)
            pe.wait_ge(table_landed, 16 * (PAGE // SEG + 2))
            for k in range(KT):
                last = pe.matmul(ps[7][0:24, 0:TOK], t["wgn"][:, 24 * k:24 * k + 24], uT[:, k, :],
                                 start=k == 0, stop=k == KT - 1)
            last.then_inc(gn_mm, 1)
            for j in range(4, 11):
                s = j % SLOTS
                pe.wait_ge(slab_landed[s], 16 * (NADA + j // SLOTS + 1) + (48 if s in (2, 3) else 0))
                for i, (t0, n) in enumerate(T_TILES):
                    r = 3 * (j - 4) + i
                    if r >= 4:
                        pe.wait_ge(row_dve if r % 2 == 0 else row_act, r // 2 - 1)
                    for k in range(KT):
                        last = pe.matmul(ps[2 + r % 4][0:n, 0:256], uT[:, k, t0:t0 + n],
                                         slab[:, s, 256 * k:256 * k + 256], start=k == 0, stop=k == KT - 1)
                    last.then_inc(row_mm, 1)
                pe.wait_ge(row_mm, 3 * (j - 3))
                pe.sem_inc(slab_used[s], 1)
            pe.wait_ge(row_dve, 11)
            pe.wait_ge(row_act, 10)
            pe.wait_ge(q_dve, 8)
            pe.wait_ge(q_act, 8)
            for g, c0 in enumerate([RKA, RKA + 128, RKA + 256, RKA + 384, RKS, RKW]):
                if g >= 2:
                    pe.wait_ge(kt_dve if g % 2 == 0 else kt_act, 2 * (g // 2))
                for i, (t0, n) in enumerate(T_TILES):
                    src = rows_s[:, c0:c0 + P] if i == 2 else rows_p[:, i, c0:c0 + P]
                    last = pe.transpose(ps[g % 2][:, t0:t0 + n], src, ident[0:n, 0:n])
                last.then_inc(kt_tr, 1)

        def kT_dst(g):
            if g < 4:
                return t["kaT_p"][:, g, :], t["kaT_s"][:, g, 0:NS]
            return t["ksT_p" if g == 4 else "kwT_p"][:, :], t["ksT_s" if g == 4 else "kwT_s"][:, 0:NS]

        def q_dst(m):
            n = "qaT" if m < 4 else "qbT"
            return t[n + "_p"][:, m % 4, :], t[n + "_s"][:, m % 4, 0:NS]

        def row_dst(r):
            j, i = r // 3, r % 3
            return rows_s[:, 256 * j:256 * j + 256] if i == 2 else rows_p[:, i, 256 * j:256 * j + 256]

        @block.scalar
        def _(act):
            act.sem_inc(modn_done, OPEN)
            act.wait_ge(c_loaded, 48)
            act.activation(cn[0:9, :], cn[0:9, :], ACT.Silu).then_inc(silu_done, 1)
            for k in range(1, KT, 2):
                act.wait_ge(x_tr, k + 1)
                act.activation(xT[:, k, :], ps[k % 4][:, 0:TOK], ACT.Copy).then_inc(xT_act, 1)
            act.wait_ge(xT_dve, 4)
            act.wait_ge(xT_act, 4)
            for k in range(KT):
                act.activation(sq[:, k, :], xT[:, k, :], ACT.Square).then_inc(sq_done, 1)
            act.wait_ge(ss_mm, 1)
            act.activation(t["root"][:, :], ps[7][:, 0:TOK], ACT.Sqrt, bias=t["eps"][:, 0:1], scale=1.0 / D)\
               .then_inc(root_done, 1)
            with act.Fori(0, NADA) as it:
                for g in range(2):
                    act.wait_ge(slab_used[2 * g + 1], it + 1 + OPEN)
                    act.activation(modn[:, bass.ds(it * D + 512 * g, 512)], ps[5 + g][0:9, :], ACT.Copy)\
                       .then_inc(modn_done, 1)
            for m in range(1, 8, 2):
                p_out, s_out = q_dst(m)
                act.wait_ge(q_mm, m + 1)
                act.activation(p_out, ps[1][:, 0:SEQ], ACT.Copy).then_inc(q_act, 1)
                act.activation(s_out, ps[1][:, SEQ:TOK], ACT.Copy).then_inc(q_act, 1)
            act.wait_ge(gn_mm, 1)
            act.activation(t["gn"][:, :], ps[7][0:24, 0:TOK], ACT.Sigmoid).then_inc(gn_done, 1)
            for r in range(1, NROWJ, 2):
                n = T_TILES[r % 3][1]
                act.wait_ge(row_mm, r + 1)
                act.activation(row_dst(r), ps[2 + r % 4][0:n, 0:256], ACT.Copy).then_inc(row_act, 1)
            for g in range(1, 6, 2):
                p_out, s_out = kT_dst(g)
                act.wait_ge(kt_tr, g + 1)
                act.activation(p_out, ps[1][:, 0:SEQ], ACT.Copy).then_inc(kt_act, 1)
                act.activation(s_out, ps[1][:, SEQ:TOK], ACT.Copy).then_inc(kt_act, 1)

        @block.vector
        def _(dve):
            steps = Steps(dve, dve_step)
            steps.do(dve.memset(t["eps"][:, :], EPS))
            for n in ("qaT_s", "qbT_s"):
                steps.do(dve.memset(t[n][:, :, NS:NS + T], 0.0))
            dve.wait_ge(c_tr, 1)
            dve.tensor_copy(cT[:, :], ps[5][:, 0:72]).then_inc(cT_done, 1)
            for k in range(0, KT, 2):
                dve.wait_ge(x_tr, k + 1)
                dve.tensor_copy(xT[:, k, :], ps[k % 4][:, 0:TOK]).then_inc(xT_dve, 1)
            dve.wait_ge(vec_tr, 1)
            dve.tensor_copy(vecT[:, :], ps[4][:, 0:NVEC]).then_inc(vecT_done, 1)
            dve.wait_ge(table_landed, 16 * (PAGE // SEG + 2))
            steps.do(dve.tensor_scalar(t["index"][:, :], t["table"][:, :], float(PAGE // SEG), t["seg_col"][:, 0:1],
                                       ALU.mult, ALU.add))
            dve.wait_ge(vecT_done, 1)
            dve.wait_ge(root_done, 1)
            dve.wait_ge(xT_act, 4)
            steps.do(dve.reciprocal(t["root"][:, :], t["root"][:, :]))

            def vectors(bank, first, n, which, scale, g0):
                bias = vecT[:, V_ADA + first:V_ADA + first + n].unsqueeze(2).to_broadcast([P, n, 9])
                dve.wait_ge(mod_tr, which + 1)
                dve.tensor_tensor(mod[:, first:first + n, :], bank[:, 0:9 * n].rearrange("p (a b) -> p a b", b=9),
                                  bias, ALU.add).then_inc(mod_done, 1)
                dve.wait_ge(mod_done, which + 1)
                g = vecT[:, g0:g0 + KT].unsqueeze(2).to_broadcast([P, KT, 9])
                steps.do(dve.scalar_tensor_tensor(t["amp"][:, which, :, :], mod[:, scale:scale + KT, :], 1.0, g,
                                                  ALU.add, ALU.mult))

            vectors(ps[0], 0, 16, 0, 8, V_GA)
            modulate(dve, t, 0, 0, u_pre, u_mid, u_done)
            vectors(ps[1], 16, 32, 1, 32, V_GF)
            for m in range(0, 8, 2):
                p_out, s_out = q_dst(m)
                dve.wait_ge(q_mm, m + 1)
                dve.tensor_copy(p_out, ps[0][:, 0:SEQ]).then_inc(q_dve, 1)
                dve.tensor_copy(s_out, ps[0][:, SEQ:TOK]).then_inc(q_dve, 1)
            for r in range(0, NROWJ, 2):
                n = T_TILES[r % 3][1]
                dve.wait_ge(row_mm, r + 1)
                dve.tensor_copy(row_dst(r), ps[2 + r % 4][0:n, 0:256]).then_inc(row_dve, 1)
            for g in range(0, 6, 2):
                p_out, s_out = kT_dst(g)
                dve.wait_ge(kt_tr, g + 1)
                dve.tensor_copy(p_out, ps[0][:, 0:SEQ]).then_inc(kt_dve, 1)
                dve.tensor_copy(s_out, ps[0][:, SEQ:TOK]).then_inc(kt_dve, 1)


def modulate(dve, t, which, shift, pre, mid, done, high=None, split=None):
    xT, uT, amp, mod = t["xT"], t["uT"], t["amp"], t["mod"]
    for step in range(KT + (3 if high else 2)):
        if step < KT:
            dve.tensor_tensor(uT[:, step, :], xT[:, step, :], t["root"][:, :], ALU.mult).then_inc(pre, 1)
        k = step - 1
        if 0 <= k < KT:
            dve.wait_ge(pre, k + 1)
            dve.tensor_scalar(uT[:, k, 0:SEQ], uT[:, k, 0:SEQ], amp[:, which, k, 0:1], mod[:, shift + k, 0:1],
                              ALU.mult, ALU.add)
            u = uT[:, k, SEQ:TOK].rearrange("p (b t) -> p b t", t=T)
            dve.tensor_tensor(u, u, amp[:, which, k, 1:9].unsqueeze(2).to_broadcast([P, NB, T]), ALU.mult)\
               .then_inc(mid, 1)
        k = step - 2
        if 0 <= k < KT:
            dve.wait_ge(mid, k + 1)
            u = uT[:, k, SEQ:TOK].rearrange("p (b t) -> p b t", t=T)
            dve.tensor_tensor(u, u, mod[:, shift + k, 1:9].unsqueeze(2).to_broadcast([P, NB, T]), ALU.add)\
               .then_inc(done, 1)
        k = step - 3
        if high and k >= 0:
            dve.wait_ge(high, k + 1)
            dve.tensor_tensor(t["uL"][:, k, :], uT[:, k, :], t["uH"][:, k, :], ALU.subtract).then_inc(split, 1)


UNITS = [(br, qt) for br in (0, 2, 3) for qt in range(2)]
BR_MOBA, BR_CMP, BR_SEL, BR_WIN = range(4)


def head_at(branch, half, tile):
    return 2 * tile + half if branch == BR_MOBA else G * half + tile


def score_banks(u):
    return 4 if UNITS[u][1] else 2


def prompt_block(nc, sem, t, d, ps):
    w1_landed, segs_landed = sem("p_w1"), sem("p_segs")
    seg_tr, segs_done, hidn_done, hid_tr, hbias_done = (sem("p_seg_tr"), sem("p_segs_done"), sem("p_hidn"),
                                                        sem("p_hid_tr"), sem("p_hbias"))
    conv_mm, gelu_done, ckcv_mm, ck_done, cv_done = (sem("p_conv_mm"), sem("p_gelu"), sem("p_ckcv_mm"), sem("p_ck"),
                                                     sem("p_cv"))
    cs_mm, csub_done, cexp_done, cp_ready = sem("p_cs_mm"), sem("p_csub"), sem("p_cexp"), sem("p_cprob")
    scores_mm, scores_taken, max_done, exp_done, p_ready = (sem("p_scores_mm"), sem("p_scores_taken"), sem("p_max"),
                                                            sem("p_exp"), sem("p_prob"))
    pt_tr, pt_dve, pt_act, pv_mm, pv_taken = (sem("p_pt_tr"), sem("p_pt_dve"), sem("p_pt_act"), sem("p_pv_mm"),
                                              sem("p_pv_taken"))
    dve_step, spilled = sem("p_dve_step"), sem("p_spilled")
    w1 = t["slab"][:, :, :].rearrange("p (w a) (b n) -> p w (a b) n", w=2, n=256)
    segs, XT, hid, ckT, cv = t["segs"], t["XTp"], t["hid_p"], t["ckT_p"], t["cv_p"]
    S, PT, Sc, PTc, cp, oT = t["S_p"], t["PT_p"], t["Sc_p"], t["PTc_p"], t["cp"], t["oT_p"]
    ident, vecT, hbias, rows = t["ident"], t["vecT"], t["hbias"], t["rows_p"]
    hidn = t["hidn"]
    NU = len(UNITS)
    jobs_of = [2 * (qt + 1) for _, qt in UNITS]
    first_job = [sum(jobs_of[:u]) for u in range(NU)]
    first_cmp_job = sum(jobs_of)

    with nc.Block() as block:

        @block.sync
        def _(sp):
            src = d["nsa_kv_prompt"].rearrange("(s lp l2) c -> s lp l2 c", lp=8, l2=2)
            for c in range(4):
                for l2 in range(2):
                    sp.dma_start(segs[:, :, c, l2, :], src[:, :, l2, DH * c:DH * c + DH]).then_inc(segs_landed, 16)
            for w in range(2):
                sp.dma_start(w1[:, w, :, :], d["cmp_w1"][w].rearrange("(lp p) n -> p lp n", p=P)).then_inc(w1_landed, 16)
                sp.dma_start(t["w2"][:, w, :, :], d["cmp_w2"][w].rearrange("(h p) e -> p h e", p=P)).then_inc(w1_landed, 16)
            sp.dma_start(t["b2v"][:, :], d["cmp_b2"][1:2, :]).then_inc(w1_landed, 16)
            sp.wait_ge(pv_taken, NU + 2)
            sp.dma_start(d["spill_o"], oT[:, :, :, :].rearrange("p b g t -> p (b g t)")).then_inc(spilled, 16)
            sp.wait_ge(spilled, 16)

        @block.tensor
        def _(pe):
            def scores(u):
                br, qt = UNITS[u]
                nk = P * (qt + 1)
                before = sum(score_banks(v) for v in range(u))
                if u:
                    pe.wait_ge(scores_taken, before)
                for slot in range(H):
                    half, tile = slot // 4, slot % 4
                    rows64 = slice(DH * half, DH * half + DH)
                    qT = t["qaT_p" if br == BR_MOBA else "qbT_p"][rows64, tile, P * qt:P * qt + P]
                    kT = (t["kaT_p"][rows64, tile, 0:nk] if br == BR_MOBA
                          else t["ksT_p" if br == BR_SEL else "kwT_p"][rows64, 0:nk])
                    col = slot * nk
                    last = pe.matmul(ps[col // 512][:, col % 512:col % 512 + nk], qT, kT, start=True, stop=True)
                    if (col + nk) % 512 == 0:
                        last.then_inc(scores_mm, 1)

            def staging(job):
                if job >= 2:
                    pe.wait_ge(pt_dve if job % 2 == 0 else pt_act, job // 2)
                return ps[4 + job % 2]

            def attend(u):
                br, qt = UNITS[u]
                pe.wait_ge(p_ready, u + 1)
                for i in range(jobs_of[u]):
                    bank = staging(first_job[u] + i)
                    kt, h0 = i // 2, 4 * (i % 2)
                    for h in range(h0, h0 + 4):
                        col = h * P * (qt + 1) + P * kt
                        last = pe.transpose(bank[:, P * (h - h0):P * (h - h0) + P], S[:, u % 3, col:col + P], ident[:, :])
                    last.then_inc(pt_tr, 1)
                done = first_job[u] + jobs_of[u]
                pe.wait_ge(pt_dve, done // 2)
                pe.wait_ge(pt_act, done // 2)
                if u:
                    pe.wait_ge(pv_taken, u)
                if u == 5:
                    pe.wait_ge(csub_done, 1)
                for slot in range(H):
                    half, tile = slot // 4, slot % 4
                    h = head_at(br, half, tile)
                    c0 = {BR_MOBA: RVA + h * DH, BR_SEL: RVS + half * DH, BR_WIN: RVW + half * DH}[br]
                    for kt in range(qt + 1):
                        last = pe.matmul(ps[6][DH * half:DH * half + DH, P * tile:P * tile + P],
                                         rows[:, kt, c0:c0 + DH], PT[:, u % 2, kt, slot, :], start=kt == 0, stop=kt == qt)
                last.then_inc(pv_mm, 1)

            def segment_transposes():
                pe.wait_ge(segs_landed, 16 * 8)
                for lp in range(8):
                    for c in range(4):
                        last = pe.transpose(ps[7][:, (c * 8 + lp) * PSEG:(c * 8 + lp + 1) * PSEG],
                                            segs[:, lp, c, :, :].rearrange("s a e -> s (a e)"), ident[0:PSEG, 0:PSEG])
                last.then_inc(seg_tr, 1)

            def hidden_layer():
                pe.wait_ge(w1_landed, 16 * 5)
                pe.wait_ge(segs_done, 5)
                for w in range(2):
                    for part in range(2):
                        for lp in range(8):
                            last = pe.matmul(ps[7][0:PC1, 256 * w:256 * w + 256], XT[:, w, part, lp, :],
                                             w1[:, w, 8 * part + lp, :], start=part == 0 and lp == 0,
                                             stop=part == 1 and lp == 7)
                last.then_inc(conv_mm, 1)

            def hidden_transposes():
                pe.wait_ge(hidn_done, 1)
                for c in range(4):
                    last = pe.transpose(ps[7][:, 32 * c:32 * c + PC1], hidn[:, P * c:P * c + P], ident[0:PC1, 0:PC1])
                last.then_inc(hid_tr, 1)

            def keys_and_values():
                pe.wait_ge(gelu_done, 4)
                compressed_keys(pe, ps[7], t, hid, 0, PCMP)
                last = compressed_values(pe, ps[7][:, P:2 * P], t, hid, 0, PCMP)
                last.then_inc(ckcv_mm, 1)

            def compressed_scores():
                pe.wait_ge(ck_done, 2)
                pe.wait_ge(cv_done, 2)
                pe.wait_ge(pv_taken, 5)
                for qt in range(2):
                    for slot in range(H):
                        half, g = slot // 4, slot % 4
                        rows64 = slice(DH * half, DH * half + DH)
                        col = (qt * G + g) * PSEG
                        last = pe.matmul(ps[6 if half else 7][:, col:col + PSEG],
                                         t["qbT_p"][rows64, g, P * qt:P * qt + P], ckT[rows64, :], start=True, stop=True)
                last.then_inc(cs_mm, 1)

            between = [segment_transposes, hidden_layer, hidden_transposes, keys_and_values, compressed_scores, None]
            scores(0)
            scores(1)
            for u in range(NU):
                if u + 2 < NU:
                    scores(u + 2)
                attend(u)
                if between[u]:
                    between[u]()
            pe.wait_ge(cp_ready, 2)
            for j in range(4):
                bank = staging(first_cmp_job + j)
                for i in range(4):
                    n = 4 * j + i
                    last = pe.transpose(bank[0:PSEG, P * i:P * i + P], Sc[:, n * PSEG:n * PSEG + PSEG], ident[:, :])
                last.then_inc(pt_tr, 1)
            for qt in range(2):
                pe.wait_ge(pt_act, first_cmp_job // 2 + qt + 1)
                pe.wait_ge(pt_dve, first_cmp_job // 2 + qt + 1)
                pe.wait_ge(pv_taken, NU + qt)
                for h in range(H):
                    half, g = h // 4, h % 4
                    last = pe.matmul(ps[6][DH * half:DH * half + DH, P * g:P * g + P], cv[:, DH * half:DH * half + DH],
                                     PTc[:, qt * H + h, :], start=True, stop=True)
                last.then_inc(pv_mm, 1)

        def pt_dst(job):
            if job >= first_cmp_job:
                j = job - first_cmp_job
                return PTc[:, 4 * j:4 * j + 4, :].rearrange("p a b -> p (a b)")
            u = max(v for v in range(NU) if first_job[v] <= job)
            i = job - first_job[u]
            return PT[:, u % 2, i // 2, 4 * (i % 2):4 * (i % 2) + 4, :].rearrange("p a b -> p (a b)")

        def pt_rows(job):
            return PSEG if job >= first_cmp_job else P

        @block.scalar
        def _(act):
            def pt_copy(job):
                act.wait_ge(pt_tr, job + 1)
                act.activation(pt_dst(job), ps[4 + job % 2][0:pt_rows(job), :], ACT.Copy).then_inc(pt_act, 1)

            def pv_copy(n, br, qt):
                act.wait_ge(pv_mm, n + 1)
                act.activation(oT[:, br, :, P * qt:P * qt + P], ps[6][:, :].rearrange("p (g q) -> p g q", g=4),
                               ACT.Copy).then_inc(pv_taken, 1)

            def exps(u):
                qt = UNITS[u][1]
                nk = P * (qt + 1)
                act.wait_ge(max_done, u + 1)
                for h in range(H):
                    act.activation(S[:, u % 3, h * nk:h * nk + nk], S[:, u % 3, h * nk:h * nk + nk], ACT.Exp,
                                   bias=t["nmax_p"][:, u % 3, h:h + 1], accum_out=t["sum_p"][:, u % 3, h:h + 1])\
                       .then_inc(exp_done, 1)

            def hidden_copy():
                act.wait_ge(conv_mm, 1)
                act.activation(hidn[:, :], ps[7][0:PC1, :], ACT.Copy).then_inc(hidn_done, 1)

            def gelu():
                act.wait_ge(hbias_done, 1)
                for w in range(2):
                    for ht in range(2):
                        c = 2 * w + ht
                        act.activation(hid[:, w, ht, :], ps[7][:, 32 * c:32 * c + 2 * PCMP], ACT.Gelu_apprx_tanh,
                                       bias=hbias[:, c:c + 1]).then_inc(gelu_done, 1)

            def keys_and_values():
                act.wait_ge(ckcv_mm, 1)
                act.wait_ge(ck_done, 1)
                act.activation(ckT[:, 0:PCMP], ps[7][:, 0:PCMP], ACT.Identity, bias=vecT[:, V_B2:V_B2 + 1])\
                   .then_inc(ck_done, 1)
                act.wait_ge(cv_done, 1)
                act.activation(cv[0:PCMP, :], ps[7][0:PCMP, P:2 * P], ACT.Copy).then_inc(cv_done, 1)

            def compressed_exps():
                act.wait_ge(csub_done, 1)
                act.activation(Sc[:, :], Sc[:, :], ACT.Exp).then_inc(cexp_done, 1)

            between = [None, hidden_copy, gelu, keys_and_values, compressed_exps, None]
            exps(0)
            exps(1)
            for u, (br, qt) in enumerate(UNITS):
                for job in range(first_job[u] + 1, first_job[u] + jobs_of[u], 2):
                    pt_copy(job)
                if u + 2 < NU:
                    exps(u + 2)
                pv_copy(u, br, qt)
                if between[u]:
                    between[u]()
            for j in (1, 3):
                pt_copy(first_cmp_job + j)
            for qt in range(2):
                pv_copy(NU + qt, BR_CMP, qt)

        @block.vector
        def _(dve):
            steps = Steps(dve, dve_step)

            def pt_copy(job):
                dve.wait_ge(pt_tr, job + 1)
                dve.tensor_copy(pt_dst(job), ps[4 + job % 2][0:pt_rows(job), :]).then_inc(pt_dve, 1)

            def biased(u):
                qt = UNITS[u][1]
                nk = P * (qt + 1)
                before = sum(score_banks(v) for v in range(u))
                c0 = C_BP1 if qt else C_BP0
                if u >= 3:
                    dve.wait_ge(pt_tr, first_job[u - 3] + jobs_of[u - 3])
                bias = cp[:, c0:c0 + H * nk].rearrange("p (h k) -> p h k", h=H)
                n = 512 // nk
                for b in range(score_banks(u)):
                    h0 = head_at(UNITS[u][0], n * b // 4, n * b % 4)
                    step = 2 if UNITS[u][0] == BR_MOBA else 1
                    dve.wait_ge(scores_mm, before + b + 1)
                    dve.scalar_tensor_tensor(S[:, u % 3, 512 * b:512 * b + 512].rearrange("p (h k) -> p h k", h=n),
                                             ps[b][:, :].rearrange("p (h k) -> p h k", h=n), SCALE,
                                             bias[:, h0:h0 + step * (n - 1) + 1:step, :], ALU.mult, ALU.add)\
                       .then_inc(scores_taken, 1)
                dve.wait_ge(scores_taken, before + score_banks(u))
                dve.tensor_reduce(t["nmax_p"][:, u % 3, :], S[:, u % 3, 0:H * nk].rearrange("p (h k) -> p h k", h=H),
                                  AX.X, ALU.max, negate=True).then_inc(max_done, 1)

            def normed(u):
                qt = UNITS[u][1]
                nk = P * (qt + 1)
                dve.wait_ge(exp_done, H * (u + 1))
                steps.do(dve.reciprocal(t["rsum_p"][:, :], t["sum_p"][:, u % 3, :]))
                s = S[:, u % 3, 0:H * nk].rearrange("p (h k) -> p h k", h=H)
                dve.tensor_tensor(s, s, t["rsum_p"][:, :].unsqueeze(2).to_broadcast([P, H, nk]), ALU.mult)\
                   .then_inc(p_ready, 1)

            def segment_copies():
                dve.wait_ge(seg_tr, 1)
                for w in range(2):
                    for part in range(2):
                        dve.tensor_copy(XT[:, w, part, :, 0:2 * PCMP].rearrange("p l (v n) -> p v l n", v=KV),
                                        ps[7][:, 256 * w:256 * w + 256].rearrange("p (v l s) -> p v l s", v=KV, l=8)
                                        [:, :, :, part:part + PCMP]).then_inc(segs_done, 1)
                dve.tensor_copy(XT[:, :, :, :, :].rearrange("p w a l n -> p (w a l) n")[:, :, 2 * PCMP],
                                vecT[:, V_PE:V_B2]).then_inc(segs_done, 1)

            def hidden_bias():
                dve.wait_ge(hid_tr, 1)
                dve.tensor_tensor(hbias[:, :], ps[7][:, 2 * PCMP:P:32], vecT[:, V_B1:V_PE], ALU.add)\
                   .then_inc(hbias_done, 1)

            s3 = Sc[:, :].rearrange("p (r n) -> p r n", n=PSEG)
            stat = t["cstat_p"]

            def compressed_scores():
                dve.wait_ge(cs_mm, 1)
                for qt, half in [(0, 0), (0, 1), (1, 0), (1, 1)]:
                    m = cp[:, C_MADD + PSEG * qt:C_MADD + PSEG * qt + PSEG].unsqueeze(1).to_broadcast([P, G, PSEG])
                    c = slice(P * qt + 64 * half, P * qt + 64 * half + 64)
                    raw = ps[6 if half else 7][:, 64 * qt:64 * qt + 64]
                    last = dve.scalar_tensor_tensor(Sc[:, c].rearrange("p (h n) -> p h n", h=G),
                                                    raw.rearrange("p (h n) -> p h n", h=G), SCALE, m,
                                                    ALU.mult, ALU.add)
                steps.do(last)
                steps.do(dve.tensor_reduce(stat[:, :], s3, AX.X, ALU.max))
                dve.tensor_tensor(s3, s3, stat[:, :].unsqueeze(2).to_broadcast([P, 2 * H, PSEG]), ALU.subtract)\
                   .then_inc(csub_done, 1)

            def compressed_probs():
                dve.wait_ge(cexp_done, 1)
                for qt in range(2):
                    m = cp[:, C_MMUL + PSEG * qt:C_MMUL + PSEG * qt + PSEG].unsqueeze(1).to_broadcast([P, H, PSEG])
                    s = Sc[:, P * qt:P * qt + P].rearrange("p (h n) -> p h n", h=H)
                    last = dve.tensor_tensor(s, s, m, ALU.mult)
                steps.do(last)
                steps.do(dve.tensor_reduce(stat[:, :], s3, AX.X, ALU.add))
                steps.do(dve.tensor_scalar(stat[:, :], stat[:, :], 1e-30, None, ALU.max))
                steps.do(dve.reciprocal(stat[:, :], stat[:, :]))
                for qt in range(2):
                    s = Sc[:, P * qt:P * qt + P].rearrange("p (h n) -> p h n", h=H)
                    dve.tensor_tensor(s, s, stat[:, H * qt:H * qt + H].unsqueeze(2).to_broadcast([P, H, PSEG]), ALU.mult)\
                       .then_inc(cp_ready, 1)

            dve.memset(ckT[:, :], 0.0).then_inc(ck_done, 1)
            dve.memset(cv[:, :], 0.0).then_inc(cv_done, 1)
            between = [segment_copies, None, hidden_bias, None, compressed_scores, compressed_probs]
            biased(0)
            biased(1)
            for u in range(NU):
                normed(u)
                if u + 2 < NU:
                    biased(u + 2)
                for job in range(first_job[u], first_job[u] + jobs_of[u], 2):
                    pt_copy(job)
                if between[u]:
                    between[u]()
            for j in (0, 2):
                pt_copy(first_cmp_job + j)


def compress(pe, out, w1, XT, w, ht, n):
    for part in range(2):
        for lp in range(8):
            last = pe.matmul(out, w1[:, w, 8 * part + lp, P * ht:P * ht + P], XT[:, w, :, lp, part:part + n],
                             start=part == 0 and lp == 0, stop=part == 1 and lp == 7)
    return last


def compressed_keys(pe, bank, t, hid, w, n):
    for kv in range(KV):
        for ht in range(2):
            last = pe.matmul(bank[DH * kv:DH * kv + DH, 0:n], t["w2"][:, 0, ht, :], hid[:, 0, ht, n * kv:n * kv + n],
                             start=ht == 0, stop=ht == 1)
    return last


def compressed_values(pe, bank, t, hid, w, n):
    for kv in range(KV):
        out = bank[0:n, DH * kv:DH * kv + DH]
        for ht in range(2):
            pe.matmul(out, hid[:, 1, ht, n * kv:n * kv + n], t["w2"][:, 1, ht, :], start=ht == 0, stop=False)
        last = pe.matmul(out, t["ones"][0:1, 0:n], t["b2v"][:, :], start=False, stop=True)
    return last


GROUPS = ([grp for q in range(4) for grp in [("cmp", q, 0), ("cmp", q, 1), ("sel", q, 0)]
           + [("moba", q, hp) for hp in range(4)]] + [("win", 0, 0)])
NG = len(GROUPS)
SCORED = [g for g in range(NG) if GROUPS[g][0] != "cmp"]
NM = len(SCORED)
EVEN, ODD = (NG + 1) // 2, NG // 2
N_SCORE = 9
N_RING, N_SMALL, N_OUT = 13, 4, 3
DVE_STEPS = 20
V_SLOTS = 12
E_MOBA, E_WIN, E_CMP, E_SEL = range(4)


def bank_of_scores(g):
    kind, q, _ = GROUPS[g]
    return {"sel": 2 * q, "moba": 2 * q + 1, "win": 8}[kind]


def last_group(s):
    return max(g for g in SCORED if bank_of_scores(g) == s)


def transposed(kind, q):
    return max(g for g in range(NG) if GROUPS[g][:2] == (kind, q)) + 1


def decode_block(nc, sem, t, d, ps):
    k_landed = [sem(f"d_k{s}") for s in range(2)]
    v_landed = [sem(f"d_v{s}") for s in range(V_SLOTS // 4)]
    nsa_landed = [sem(f"d_nsa{s}") for s in range(2)]
    win_landed, mask_zeroed, staged_index = sem("d_win"), sem("d_mask_zeroed"), sem("d_staged_index")
    q_zeroed, q_staged, relaid, kept = sem("d_q_zeroed"), sem("d_q_staged"), sem("d_relaid"), sem("d_kept")
    tr, copied_dve, copied_act, scored, scores_taken = (sem("d_tr"), sem("d_copied_dve"), sem("d_copied_act"),
                                                        sem("d_scored"), sem("d_scores_taken"))
    ring_mm, ring_taken, small_mm, small_taken = sem("d_ring_mm"), sem("d_ring_taken"), sem("d_small_mm"), sem("d_small_taken")
    out_mm, out_taken, v_used = sem("d_out_mm"), sem("d_out_taken"), sem("d_v_used")
    max_done, exp_done, pc_ready, dve_step = sem("d_max"), sem("d_exp"), sem("d_pc"), sem("d_dve_step")
    pe_turns, pool_turns = sem("d_pe_turns"), sem("d_pool_turns")
    w1 = t["slab"][:, :, :].rearrange("p (w a) (b n) -> p w (a b) n", w=2, n=256)
    Kr, Vr, nsa, relay, vsel, XT, KTr = t["Kr"], t["Vr"], t["nsa"], t["relay"], t["vsel"], t["XT"], t["KTr"]
    Sm, Ss, Sw, Sc, PTm, PTs, PTw = t["Sm"], t["Ss"], t["Sw"], t["Sc"], t["PTm"], t["PTs"], t["PTw"]
    hid, ckT, cv, wkv, qa, qb = t["hid"], t["ckT"], t["cv"], t["wkv"], t["qa_cur"], t["qb_cur"]
    c64, ident, rows, oT = t["c64"], t["ident"], t["rows_s"], t["oT_s"]
    ident64 = ident[0:64, 0:64]
    OWN = PAST

    with nc.Block() as block:

        @block.sync
        def _(sp):
            with sp.Fori(0, NB) as it:
                sp.wait_ge(out_mm, it * N_OUT + OPEN)
                sp.dma_start(wkv[:, :, :].rearrange("p c x -> p (c x)"),
                             d["cache_nsa_win"].rearrange("b (p c) x -> p b (c x)", c=4)[:, bass.ds(it, 1), :]
                             .rearrange("p b x -> p (b x)")).then_inc(win_landed, 16)

        @block.gpsimd
        def _(pool):
            def gather(dst, src, which, offset, landed):
                pool.indirect_dma_start(out=dst, out_offset=None, in_=src,
                                        in_offset=bass.IndirectOffsetOnAxis(ap=t["index_now"][:, which:which + 1], axis=0),
                                        element_offset=offset).then_inc(landed, 16)

            def gather_k(lq, which):
                for l in range(4 * lq, 4 * lq + 4):
                    gather(Kr[:, l % 8, :], d["cache_moba_kv"], which, l * 1024, k_landed[lq % 2])

            def gather_v(lq, which):
                for l in range(4 * lq, 4 * lq + 4):
                    s = l % V_SLOTS
                    gather(Vr[:, s, :], d["cache_moba_kv"], which, l * 1024 + 512, v_landed[s // 4])

            def gather_nsa(q, which):
                gather(nsa[:, q % 2, :], d["cache_nsa_kv"], which, q * 2048, nsa_landed[q % 2])

            def stage_index(which, column):
                pool.tensor_copy(t["index_now"][:, which:which + 1], t["index"][:, column]).then_inc(staged_index, 1)

            def gather_nsa_after(it, q, quarter, which):
                pool.wait_ge(kept, it * 4 + q + 1)
                pool.wait_ge(relaid, it * 8 + 2 * q + 2)
                gather_after(tr, it * NG + transposed("sel", q) + OPEN, gather_nsa, quarter, which)

            def gather_k_after(it, q, quarter, which):
                gather_after(tr, it * NG + transposed("moba", q) + OPEN, gather_k, quarter, which)

            def sequence(it, odd, more):
                for q in range(2):
                    gather_nsa_after(it, q, q + 2, odd)
                    gather_k_after(it, q, q + 2, odd)
                if more:
                    pool.wait_ge(v_used, it * 4 + OPEN)
                    stage_index(1 - odd, bass.ds(it + 1, 1))
                    pool.wait_ge(staged_index, it + 2)
                    for q in range(2, 4):
                        gather_nsa_after(it, q, q - 2, 1 - odd)
                        gather_k_after(it, q, q - 2, 1 - odd)
                gather_after(v_used, it * 4 + 1 + OPEN, gather_v, 3, odd)
                if more:
                    for q in (1, 2, 0):
                        gather_after(v_used, it * 4 + (q + 1 if q else 4) + OPEN, gather_v, q, 1 - odd)

            def gather_after(used, count, gather_quarter, q, which):
                pool.wait_ge(used, count)
                apart(pool, pool_turns)
                gather_quarter(q, which)

            stage_index(0, slice(0, 1))
            pool.wait_ge(staged_index, 1)
            for q in range(2):
                gather_nsa(q, 0)
                gather_k(q, 0)
            for q in range(3):
                gather_v(q, 0)
            with pool.Fori(0, NB - 2, 2) as it:
                sequence(it, 0, True)
                sequence(it + 1, 1, True)
            sequence(NB - 2, 0, True)
            sequence(NB - 1, 1, False)

        @block.tensor
        def _(pe):
            def transposes(it, g):
                kind, q, i = GROUPS[g]
                if g % 2 == 0:
                    pe.wait_ge(copied_dve, it * EVEN + g // 2 + OPEN)
                else:
                    pe.wait_ge(copied_act, it * ODD + g // 2 + OPEN)
                if kind == "moba":
                    if i == 0:
                        pe.wait_ge(k_landed[q % 2], it * 128 + 64 * (q // 2 + 1))
                    srcs = [Kr[:, l % 8, P * i:P * i + P] for l in range(4 * q, 4 * q + 4)]
                elif kind == "cmp":
                    pe.wait_ge(relaid, it * 8 + 2 * q + i + 1)
                    srcs = [relay[:, i, P * c:P * c + P] for c in range(4)]
                elif kind == "sel":
                    pe.wait_ge(nsa_landed[q % 2], it * 32 + 16 * (q // 2 + 1))
                    srcs = [nsa[:, q % 2, 512 * l + 256:512 * l + 384] for l in range(4)]
                else:
                    pe.wait_ge(win_landed, it * 16 + 16)
                    srcs = [wkv[:, c, 0:P] for c in range(4)]
                for n, src in enumerate(srcs):
                    last = pe.transpose(ps[g % 2][:, P * n:P * n + P], src, ident[:, :])
                last.then_inc(tr, 1)

            def score(it, g):
                kind, q, i = GROUPS[g]
                s, m = bank_of_scores(g), SCORED.index(g)
                if g % 2 == 0:
                    pe.wait_ge(copied_dve, it * EVEN + g // 2 + 1 + OPEN)
                else:
                    pe.wait_ge(copied_act, it * ODD + g // 2 + 1 + OPEN)
                if i == 0:
                    pe.wait_ge(scores_taken, it * N_SCORE + s - 1 + OPEN)
                lhsT = qa[:, 64 * i:64 * i + 64] if kind == "moba" else qb[:, :]
                pe.matmul(ps[2 + s % 2][0:64, :], lhsT, KTr[:, m % 4, :], start=i == 0,
                          stop=kind != "moba" or i == 3).then_inc(scored, 1)

            def ring_bank(it, r):
                pe.wait_ge(ring_taken, it * N_RING + r - 1 + OPEN)
                return ps[4 + r % 2]

            def prob_transposes(it, S, r):
                for n in range(2):
                    bank = ring_bank(it, r + n)
                    for i in range(8):
                        c0 = P * (8 * n + i)
                        if i == 0:
                            apart(pe, pe_turns)
                        last = pe.transpose(bank[:, 64 * i:64 * i + 64], S[:, c0:c0 + P], ident64)
                    last.then_inc(ring_mm, 1)
                bank = ring_bank(it, r + 2)
                apart(pe, pe_turns)
                pe.transpose(bank[0:64, 0:64], S[:, OWN:OWN + 64], ident64).then_inc(ring_mm, 1)

            def sequence(it):
                pe.wait_ge(q_staged, it * 4 + 4)
                pe.wait_ge(small_taken, it * N_SMALL + OPEN)
                for hp in range(4):
                    pe.matmul(ps[7][0:64, 0:64], qa[:, 64 * hp:64 * hp + 64], t["kaT_s"][:, hp, :],
                              start=hp == 0, stop=hp == 3)
                pe.matmul(ps[7][0:64, 64:128], qb[:, :], t["ksT_s"][:, :], start=True, stop=True)
                pe.matmul(ps[7][0:64, 128:192], qb[:, :], t["kwT_s"][:, :], start=True, stop=True).then_inc(small_mm, 1)
                for g in range(NG):
                    transposes(it, g)
                    if g >= 2 and g - 2 in SCORED:
                        score(it, g - 2)
                score(it, NG - 2)
                score(it, NG - 1)
                last_cmp = transposed("cmp", 3) - 1
                pe.wait_ge(copied_dve, it * EVEN + last_cmp // 2 + 1 + OPEN)
                pe.wait_ge(copied_act, it * ODD + (last_cmp + 1) // 2 + OPEN)
                for w in range(2):
                    for ht in range(2):
                        out = ring_bank(it, 2 * w + ht)[:, 0:2 * NCMP]
                        compress(pe, out, w1, XT, w, ht, NCMP).then_inc(ring_mm, 1)
                bank = ring_bank(it, 4)
                compressed_keys(pe, bank, t, hid, 0, NCMP).then_inc(ring_mm, 1)
                bank = ring_bank(it, 5)
                compressed_values(pe, bank, t, hid, 0, NCMP).then_inc(ring_mm, 1)
                pe.wait_ge(ring_taken, it * N_RING + 5 + OPEN)
                pe.wait_ge(small_taken, it * N_SMALL + 1 + OPEN)
                pe.matmul(ps[7][0:64, 0:NCMP], qb[:, :], ckT[:, 0:NCMP], start=True, stop=True).then_inc(small_mm, 1)
                pe.wait_ge(exp_done, it * 4 + E_MOBA + 1)
                prob_transposes(it, Sm, 6)
                pe.wait_ge(out_taken, it * N_OUT + OPEN)
                for l in range(SEG):
                    if l % 8 == 0:
                        pe.wait_ge(ring_taken, it * N_RING + 7 + l // 8 + OPEN)
                    if l == 8:
                        pe.wait_ge(pc_ready, it + 1)
                        pe.wait_ge(small_taken, it * N_SMALL + 2 + OPEN)
                        apart(pe, pe_turns)
                        pe.matmul(ps[7][0:64, 0:NCMP], c64[:, C_GSUM:C_GSUM + 64], Sc[:, 0:NCMP], start=True, stop=True)\
                          .then_inc(small_mm, 1)
                    vs = l % V_SLOTS
                    if l % 4 == 0:
                        pe.wait_ge(v_landed[vs // 4], it * (64 if vs else 128) + 64 * (l // V_SLOTS + 1))
                    last = pe.matmul(ps[6][0:64, :], PTm[:, l, :], Vr[:, vs, :], start=l == 0, stop=False)
                    if l % 4 == 3:
                        last.then_inc(v_used, 1)
                pe.wait_ge(ring_taken, it * N_RING + 9 + OPEN)
                apart(pe, pe_turns)
                pe.matmul(ps[6][0:64, :], PTm[0:64, SEG, :], rows[:, RVA:RVA + 512], start=False, stop=True)\
                  .then_inc(out_mm, 1)
                pe.wait_ge(exp_done, it * 4 + E_WIN + 1)
                bank = ring_bank(it, 9)
                apart(pe, pe_turns)
                pe.transpose(bank[0:NCMP, 0:64], Sc[:, 0:NCMP], ident64)
                for c in range(4):
                    pe.transpose(bank[:, 64 * (1 + c):64 * (2 + c)], Sw[:, P * c:P * c + P], ident64)
                pe.transpose(bank[0:64, 320:384], Sw[:, WIN:WIN + 64], ident64).then_inc(ring_mm, 1)
                pe.wait_ge(ring_taken, it * N_RING + 10 + OPEN)
                pe.wait_ge(out_taken, it * N_OUT + 1 + OPEN)
                pe.matmul(ps[6][0:64, 0:P], PTw[0:NCMP, 0, :], cv[0:NCMP, :], start=True, stop=True)
                for c in range(4):
                    pe.matmul(ps[6][0:64, P:2 * P], PTw[:, 1 + c, :], wkv[:, c, P:2 * P], start=c == 0, stop=False)
                pe.matmul(ps[6][0:64, P:2 * P], PTw[0:64, 5, :], rows[:, RVW:RVW + P], start=False, stop=True)\
                  .then_inc(out_mm, 1)
                pe.wait_ge(exp_done, it * 4 + E_SEL + 1)
                prob_transposes(it, Ss, 10)
                pe.wait_ge(out_taken, it * N_OUT + 2 + OPEN)
                pe.wait_ge(kept, it * 4 + 4)
                for l in range(SEG):
                    if l % 8 == 0:
                        pe.wait_ge(ring_taken, it * N_RING + 11 + l // 8 + OPEN)
                    pe.matmul(ps[6][0:64, 0:P], PTs[:, l, :], vsel[:, l, :], start=l == 0, stop=False)
                pe.wait_ge(ring_taken, it * N_RING + 13 + OPEN)
                apart(pe, pe_turns)
                pe.matmul(ps[6][0:64, 0:P], PTs[0:64, SEG, :], rows[:, RVS:RVS + P], start=False, stop=True)\
                  .then_inc(out_mm, 1)
                pe.wait_ge(out_taken, it * N_OUT + 3 + OPEN)
                pe.wait_ge(small_taken, it * N_SMALL + 3 + OPEN)
                apart(pe, pe_turns)
                for n in range(4):
                    pe.transpose(ps[7][:, 64 * n:64 * n + 64], t["Om"][:, P * n:P * n + P], ident64)
                for n in range(3):
                    last = pe.transpose(ps[7][:, 256 + 64 * n:320 + 64 * n], t["On"][:, n, :], ident64)
                last.then_inc(small_mm, 1)

            for nothing_yet in (tr, scored, ring_mm, out_mm, v_used):
                pe.sem_inc(nothing_yet, OPEN)
            with pe.Fori(0, NB) as it:
                sequence(it)

        def group_copy(eng, copy, it, g, done):
            kind, q, i = GROUPS[g]
            eng.wait_ge(tr, it * NG + g + 1 + OPEN)
            if kind == "cmp":
                eng.wait_ge(ring_mm, it * N_RING + OPEN)
                dst = XT[:, :, :, 2 * q + i, :].rearrange("p w v s -> p (w v) s")
                copy(dst, ps[g % 2][:, :].rearrange("p (c s) -> p c s", c=4)).then_inc(done, 1)
            else:
                m = SCORED.index(g)
                eng.wait_ge(scored, it * NM + m - 3 + OPEN)
                copy(KTr[:, m % 4, :], ps[g % 2][:, :]).then_inc(done, 1)

        @block.scalar
        def _(act):
            def copy(dst, src):
                return act.activation(dst, src, ACT.Copy)

            def stage_queries(b):
                cols = bass.ds(b * T, T) if not isinstance(b, int) else slice(b * T, b * T + T)
                for half in range(2):
                    rows64 = slice(DH * half, DH * half + DH)
                    copy(qa[rows64, 8 * half:8 * half + 320].rearrange("p (g c) -> p g c", c=80)[:, :, 0:T],
                         t["qaT_s"][rows64, :, cols]).then_inc(q_staged, 1)
                    copy(qb[rows64, 32 * half:32 * half + 32].rearrange("p (g c) -> p g c", c=T),
                         t["qbT_s"][rows64, :, cols]).then_inc(q_staged, 1)

            def exp(it, which, S, n):
                act.wait_ge(max_done, it * 4 + which + 1)
                act.activation(S[:, 0:n], S[:, 0:n], ACT.Exp, bias=t["nmax"][:, which:which + 1],
                               accum_out=t["sums"][:, which:which + 1]).then_inc(exp_done, 1)

            def prob_copies(it, PT, r):
                for n in range(2):
                    act.wait_ge(ring_mm, it * N_RING + r + n + 1 + OPEN)
                    copy(PT[:, 8 * n:8 * n + 8, :].rearrange("p l r -> p (l r)"), ps[4 + (r + n) % 2][:, :])\
                        .then_inc(ring_taken, 1)
                act.wait_ge(ring_mm, it * N_RING + r + 3 + OPEN)
                copy(PT[0:64, SEG, :], ps[4 + r % 2][0:64, 0:64]).then_inc(ring_taken, 1)

            def relay_quarter(it, q):
                act.wait_ge(nsa_landed[q % 2], it * 32 + 16 * (q // 2 + 1))
                act.wait_ge(tr, it * NG + (transposed("cmp", q - 1) if q else 0) + OPEN)
                src = nsa[:, q % 2, :].rearrange("p (a b x) -> p a b x", a=2, b=2)
                for a in range(2):
                    copy(relay[:, a, :].rearrange("p (c b e) -> p c b e", c=4, b=2),
                         src[:, a, :, 0:256].rearrange("p b (c e) -> p c b e", c=4)).then_inc(relaid, 1)
                if q == 0:
                    act.wait_ge(out_mm, it * N_OUT + OPEN)
                copy(vsel[:, 4 * q:4 * q + 4, :],
                     nsa[:, q % 2, :].rearrange("p (l x) -> p l x", l=4)[:, :, 384:512]).then_inc(kept, 1)

            act.sem_inc(copied_act, OPEN)
            act.sem_inc(ring_taken, OPEN)
            act.wait_ge(q_zeroed, 2)
            stage_queries(0)
            with act.Fori(0, NB) as it:
                relay_quarter(it, 0)
                for g in range(1, NG, 2):
                    group_copy(act, copy, it, g, copied_act)
                    for q in range(1, 4):
                        if g in (transposed("cmp", q - 1) + 1, transposed("cmp", q - 1) + 2):
                            relay_quarter(it, q)
                exp(it, E_MOBA, Sm, PAST + 64)
                exp(it, E_WIN, Sw, WIN + 64)
                for w in range(2):
                    for ht in range(2):
                        r = 2 * w + ht
                        act.wait_ge(ring_mm, it * N_RING + r + 1 + OPEN)
                        act.activation(hid[:, w, ht, :], ps[4 + r % 2][:, 0:2 * NCMP], ACT.Gelu_apprx_tanh,
                                       bias=t["hbias"][:, r:r + 1]).then_inc(ring_taken, 1)
                act.wait_ge(ring_mm, it * N_RING + 5 + OPEN)
                act.activation(ckT[:, 0:NCMP], ps[4][:, 0:NCMP], ACT.Identity, bias=t["vecT"][:, V_B2:V_B2 + 1])\
                   .then_inc(ring_taken, 1)
                act.wait_ge(ring_mm, it * N_RING + 6 + OPEN)
                copy(cv[0:NCMP, :], ps[5][0:NCMP, 0:P]).then_inc(ring_taken, 1)
                prob_copies(it, PTm, 6)
                exp(it, E_CMP, Sc, NCMP)
                act.wait_ge(ring_mm, it * N_RING + 10 + OPEN)
                copy(PTw[0:NCMP, 0, :], ps[5][0:NCMP, 0:64])
                copy(PTw[:, 1:5, :].rearrange("p c r -> p (c r)"), ps[5][:, 64:320])
                copy(PTw[0:64, 5, :], ps[5][0:64, 320:384]).then_inc(ring_taken, 1)
                exp(it, E_SEL, Ss, PAST + 64)
                prob_copies(it, PTs, 10)
                act.wait_ge(small_mm, it * N_SMALL + 2)
                stage_queries(it + 1)

        @block.vector
        def _(dve):
            def ranks(steps, value, n, above, equal, tie, rank):
                one = value.unsqueeze(1).to_broadcast([64, n, n])
                other = value.unsqueeze(2).to_broadcast([64, n, n])
                steps.do(dve.tensor_tensor(above, one, other, ALU.is_gt))
                steps.do(dve.tensor_tensor(equal, one, other, ALU.is_equal))
                steps.do(dve.tensor_tensor(equal, equal, tie.rearrange("p (j i) -> p j i", i=n), ALU.mult))
                steps.do(dve.tensor_tensor(above, above, equal, ALU.add))
                steps.do(dve.tensor_reduce(rank, above, AX.X, ALU.add))

            def take_scores(it, s):
                bank = ps[2 + s % 2][0:64, :]
                dve.wait_ge(scored, it * NM + SCORED.index(last_group(s)) + 1 + OPEN)
                q = s // 2
                c0 = 512 * q
                if s == 8:
                    dst, bias = Sw[:, 0:WIN], c64[:, C_BWIN:C_BWIN + WIN]
                elif s % 2:
                    dve.tensor_reduce(t["gates4"][:, :, q], bank.rearrange("p (l n s) -> p n l s", l=4, n=NMB),
                                      AX.XY, ALU.add)
                    dst, bias = Sm[:, c0:c0 + 512], c64[:, C_BDEC + c0:C_BDEC + c0 + 512]
                else:
                    dst, bias = Ss[:, c0:c0 + 512], c64[:, C_BDEC + c0:C_BDEC + c0 + 512]
                dve.scalar_tensor_tensor(dst, bank, SCALE, bias, ALU.mult, ALU.add).then_inc(scores_taken, 1)

            def row_max(which, S, n):
                dve.tensor_reduce(t["nmax"][:, which:which + 1], S[:, 0:n], AX.X, ALU.max, negate=True)\
                   .then_inc(max_done, 1)

            def inverse(it, steps, which):
                dve.wait_ge(exp_done, it * 4 + which + 1)
                steps.do(dve.reciprocal(t["inv"][:, which:which + 1], t["sums"][:, which:which + 1]))

            for nothing_yet in (copied_dve, scores_taken, small_taken, out_taken):
                dve.sem_inc(nothing_yet, OPEN)
            dve.memset(qa[:, :], 0.0).then_inc(q_zeroed, 1)
            dve.memset(qb[:, :], 0.0).then_inc(q_zeroed, 1)
            dve.memset(t["sel_mask"][:, :], 0.0).then_inc(mask_zeroed, 1)
            dve.wait_ge(mask_zeroed, 1)
            with dve.Fori(0, NB) as it:
                steps = Steps(dve, dve_step, it * DVE_STEPS)
                dve.wait_ge(small_mm, it * N_SMALL + 1)
                own = c64[:, C_BOWN:C_BOWN + 512].rearrange("p (b u) -> p b u", u=64)[:, bass.ds(it, 1), :]\
                    .rearrange("p b u -> p (b u)")
                for n, dst in enumerate([Sm[:, OWN:OWN + 64], Ss[:, OWN:OWN + 64], Sw[:, WIN:WIN + 64]]):
                    last = dve.scalar_tensor_tensor(dst, ps[7][0:64, 64 * n:64 * n + 64], SCALE, own, ALU.mult, ALU.add)
                last.then_inc(small_taken, 1)
                after = {(last_group(s) + 2) // 2 * 2: s for s in range(8)}
                for g in range(0, NG, 2):
                    group_copy(dve, dve.tensor_copy, it, g, copied_dve)
                    if g in after:
                        take_scores(it, after[g])
                take_scores(it, 8)
                dve.wait_ge(scores_taken, it * N_SCORE + 9 + OPEN)
                steps.do(dve.tensor_reduce(t["gate"][:, :], t["gates4"][:, :, :], AX.X, ALU.add))
                ranks(steps, t["gate"][:, :], NMB, t["above8"][:, :, :], t["equal8"][:, :, :],
                      c64[:, C_TIE8:C64W], t["rank"][:, 0:NMB])
                steps.do(dve.tensor_scalar(t["mb_mask"][:, :], t["rank"][:, 0:NMB], float(MTOP), NEG, ALU.is_ge, ALU.mult))
                s4 = Sm[:, 0:PAST].rearrange("p (l n s) -> p l n s", l=SEG, n=NMB)
                steps.do(dve.tensor_tensor(s4, s4, t["mb_mask"][:, :].unsqueeze(1).unsqueeze(3)
                                           .to_broadcast([64, SEG, NMB, SEG]), ALU.add))
                row_max(E_MOBA, Sm, PAST + 64)
                row_max(E_WIN, Sw, WIN + 64)
                dve.wait_ge(small_mm, it * N_SMALL + 2)
                dve.tensor_scalar(Sc[:, 0:NCMP], ps[7][0:64, 0:NCMP], SCALE, None, ALU.mult).then_inc(small_taken, 1)
                dve.wait_ge(small_taken, it * N_SMALL + 2 + OPEN)
                row_max(E_CMP, Sc, NCMP)
                inverse(it, steps, E_CMP)
                dve.tensor_scalar(Sc[:, 0:NCMP], Sc[:, 0:NCMP], t["inv"][:, E_CMP:E_CMP + 1], None, ALU.mult)\
                   .then_inc(pc_ready, 1)
                dve.wait_ge(small_mm, it * N_SMALL + 3)
                steps.do(dve.tensor_reduce(t["imp"][:, :], ps[7][0:64, 4:4 + 4 * CAND].rearrange("p (j n) -> p j n", n=4),
                                           AX.X, ALU.add))
                dve.tensor_tensor(t["imp"][:, :], t["imp"][:, :], ps[7][0:64, 3:3 + 4 * CAND:4], ALU.add)\
                   .then_inc(small_taken, 1)
                dve.wait_ge(small_taken, it * N_SMALL + 3 + OPEN)
                above, equal = [Sm[:, c:c + CAND * CAND].rearrange("p (j i) -> p j i", i=CAND)
                                for c in (0, CAND * CAND)]
                ranks(steps, t["imp"][:, :], CAND, above, equal,
                      c64[:, C_TIE:C_TIE8], t["rank"][:, :])
                steps.do(dve.tensor_scalar(t["sel_mask"][:, 1:1 + CAND], t["rank"][:, :], float(STOP), NEG,
                                           ALU.is_ge, ALU.mult))
                s4 = Ss[:, 0:PAST].rearrange("p (l j s) -> p l j s", l=SEG, j=NSB)
                steps.do(dve.tensor_tensor(s4, s4, t["sel_mask"][:, :].unsqueeze(1).unsqueeze(3)
                                           .to_broadcast([64, SEG, NSB, 4]), ALU.add))
                row_max(E_SEL, Ss, PAST + 64)
                inverse(it, steps, E_MOBA)
                dve.wait_ge(out_mm, it * N_OUT + 1 + OPEN)
                dve.tensor_scalar(t["Om"][:, :], ps[6][0:64, :], t["inv"][:, E_MOBA:E_MOBA + 1], None, ALU.mult)\
                   .then_inc(out_taken, 1)
                inverse(it, steps, E_WIN)
                dve.wait_ge(out_mm, it * N_OUT + 2 + OPEN)
                dve.tensor_copy(t["On"][:, 0, :], ps[6][0:64, 0:P])
                dve.tensor_scalar(t["On"][:, 2, :], ps[6][0:64, P:2 * P], t["inv"][:, E_WIN:E_WIN + 1], None, ALU.mult)\
                   .then_inc(out_taken, 1)
                inverse(it, steps, E_SEL)
                dve.wait_ge(out_mm, it * N_OUT + 3 + OPEN)
                dve.tensor_scalar(t["On"][:, 1, :], ps[6][0:64, 0:P], t["inv"][:, E_SEL:E_SEL + 1], None, ALU.mult)\
                   .then_inc(out_taken, 1)
                dve.wait_ge(small_mm, it * N_SMALL + 4)
                for half in range(2):
                    rows64 = slice(DH * half, DH * half + DH)
                    dve.tensor_copy(oT[rows64, BR_MOBA, :, bass.ds(it * T, T)],
                                    ps[7][rows64, 8 * half:8 * half + 320].rearrange("p (g c) -> p g c", c=80)[:, :, 0:T])
                    last = dve.tensor_copy(oT[rows64, BR_CMP:, :, bass.ds(it * T, T)],
                                           ps[7][rows64, 256:448].rearrange("p (c v g t) -> p c v g t", c=3, v=KV, g=G)
                                           [:, :, half, :, :])
                last.then_inc(small_taken, 1)
                assert steps.n == DVE_STEPS, steps.n
            dve.wait_ge(small_taken, NB * N_SMALL + OPEN)


def square_norm(pe, ones, sq, bank, sq_done, first, ss_mm):
    for k in range(KT):
        pe.wait_ge(sq_done, first + k + 1)
        last = pe.matmul(bank[:, 0:TOK], ones[:, :], sq[:, k, :], start=k == 0, stop=k == KT - 1)
    last.then_inc(ss_mm, 1)


def split_matmul(pe, out, w_high, w_low, x_high, x_low, start, stop, **kw):
    pe.matmul(out, w_high, x_high, start=start, stop=False, **kw)
    pe.matmul(out, w_high, x_low, start=False, stop=False, **kw)
    return pe.matmul(out, w_low, x_high, start=False, stop=stop, **kw)


def back_block(nc, sem, t, d, ps):
    slab_landed = [sem(f"b_slab_landed{s}") for s in range(SLOTS)]
    w_high, w_split, sp_turns = sem("b_w_high"), sem("b_w_split"), sem("b_sp_turns")
    u_back, x_back, o_back, exp_landed, o_whole = (sem("b_u_back"), sem("b_x_back"), sem("b_o_back"), sem("b_expand"),
                                                   sem("b_o_whole"))
    u_high, u_split, o_split, ge_mm, ge_taken, ob_done = (sem("b_u_high"), sem("b_u_split"), sem("b_o_split"),
                                                          sem("b_ge_mm"), sem("b_ge"), sem("b_ob"))
    gate_mm, gate_done, y_mm, z_part, z_step, z_done = (sem("b_gate_mm"), sem("b_gate"), sem("b_y_mm"),
                                                        sem("b_z_part"), sem("b_z_step"), sem("b_z"))
    mix_mm, x_done = sem("b_mix_mm"), sem("b_x")
    sq_done, ss_mm, root_done = sem("b_sq"), sem("b_ss_mm"), sem("b_root")
    h_pre, h_mid, h_done, h_high, h_split = (sem("b_h_pre"), sem("b_h_mid"), sem("b_h"), sem("b_h_high"),
                                             sem("b_h_split"))
    a_mm, b_mm, silu_done, f_step, f_done = sem("b_a_mm"), sem("b_b_mm"), sem("b_silu"), sem("b_f_step"), sem("b_f")
    down_mm, y_done, y_tr, y_act, y_dve, dve_step, stored = (sem("b_down_mm"), sem("b_y"), sem("b_y_tr"), sem("b_y_act"),
                                                             sem("b_y_dve"), sem("b_dve_step"), sem("b_stored"))
    slab, slabH, slabL, xT, uT, uH = t["slab"], t["slabH"], t["slabL"], t["xT"], t["uT"], t["uH"]
    ex = xT[0:24, :, :].rearrange("p k n -> p (k n)")[:, 0:12 * P]
    uL, sq, gn, gates, prod = t["uL"], t["sq"], t["gn"], t["gates"], t["prod"]
    oT, oH, oL, bH, bL, zH, zL, GH, GL, yn = (t["oT"], t["oH"], t["oL"], t["bH"], t["bL"], t["zH"], t["zL"],
                                              t["GH"], t["GL"], t["yn"])
    mod, ident = t["mod"], t["ident"]
    N_OUT, N_GU, N_DOWN, N_END = 16, 20, 42, 53
    HALF = 1024

    with nc.Block() as block:

        @block.sync
        def _(sp):
            def load(n, it, dst, src):
                sp.wait_ge(w_split, it * 4 + n - 3 + OPEN)
                apart(sp, sp_turns)
                sp.dma_start(dst, src).then_inc(slab_landed[n % SLOTS], 16)

            def in_tiles(n, k, values=SLABW):
                return slab[:, n % SLOTS, 0:values].rearrange("p (k n) -> p k n", k=k)

            w_in = d["w_in"].rearrange("(k p) n -> p k n", p=P)
            sp.dma_start(uT[:, :, :].rearrange("p k n -> p (k n)"), d["spill_u"]).then_inc(u_back, 16)
            w_pa = d["w_pa"].rearrange("(k p) n -> p k n", p=P)
            w_pb = d["w_pb"].rearrange("(v g e) n -> v e g n", v=KV, g=G)
            with sp.Fori(0, 4) as it:
                cols = bass.ds(it * 256, 256)
                load(0, it, in_tiles(0, KT), w_in[:, :, bass.ds(it * 256 + GA, 256)])
                load(1, it, in_tiles(1, KT), w_in[:, :, bass.ds(it * 256 + GB, 256)])
                load(2, it, in_tiles(2, 4, HALF), w_pa[:, :, cols])
                sp.wait_ge(w_split, it * 4 + OPEN)
                apart(sp, sp_turns)
                for v in range(KV):
                    sp.dma_start(slab[DH * v:DH * v + DH, 3, 0:HALF].rearrange("p (k n) -> p k n", k=4),
                                 w_pb[v][:, :, cols]).then_inc(slab_landed[3], 16)
            sp.wait_ge(ge_mm, 12)
            sp.dma_start(xT[:, :, :].rearrange("p k n -> p (k n)"), d["spill_x"]).then_inc(x_back, 16)
            w_out = d["w_out"].rearrange("(k p) n -> p k n", p=P)
            for i in range(4):
                load(N_OUT + i, 0, in_tiles(i, KT), w_out[:, :, 256 * i:256 * i + 256])
            w_gu = d["w_gu"].rearrange("(k p) n -> p k n", p=P)
            with sp.Fori(0, 5) as it:
                for i in range(4):
                    load(N_GU + i, it, in_tiles(i, KT),
                         w_gu[:, :, bass.ds(it * 512 + 256 * (i // 2) + FF * (i % 2), 256)])
            for i in range(2):
                load(N_GU + 20 + i, 0, in_tiles(i, KT), w_gu[:, :, 2560 + FF * i:2816 + FF * i])
            w_down = d["w_down"].rearrange("(f p) n -> p f n", p=P)
            with sp.Fori(0, 2) as it:
                for i in range(4):
                    load(N_DOWN + i, it, in_tiles(N_DOWN + i, 2), w_down[:, bass.ds(it * 8 + 2 * i, 2), :])
            for i in range(8, 11):
                load(N_DOWN + i, 0, in_tiles(N_DOWN + i, 2), w_down[:, 2 * i:2 * i + 2, :])
            for i, (t0, n) in enumerate(T_TILES):
                sp.wait_ge(y_act, i + 1)
                sp.wait_ge(y_dve, i + 1)
                dst = d["y_sample"] if i == 2 else d["y_prompt"][t0:t0 + n, :]
                sp.dma_start(dst, yn[0:n, i, :]).then_inc(stored, 16)
            sp.wait_ge(stored, 48)

        @block.gpsimd
        def _(pool):
            def low_part(n, it, values=SLABW):
                s = n % SLOTS
                pool.wait_ge(w_high, it * 4 + n + 1)
                pool.tensor_tensor(slabL[:, s, 0:values], slab[:, s, 0:values], slabH[:, s, 0:values].bitcast(F32),
                                   ALU.subtract).then_inc(w_split, 1)

            pool.sem_inc(w_split, OPEN)
            pool.dma_start(ex, d["c_expand"]).then_inc(exp_landed, 16)
            for br in range(4):
                pool.dma_start(oT[:, br, :, 0:SEQ],
                               d["spill_o"][:, br * 4 * SEQ:(br + 1) * 4 * SEQ].rearrange("p (g t) -> p g t", g=4))\
                    .then_inc(o_back, 16)
            for br in range(4):
                pool.tensor_copy(oT[:, br, :, SEQ:TOK], t["oT_s"][:, br, :, :]).then_inc(o_whole, 1)
            with pool.Fori(0, 4) as it:
                for i in range(4):
                    low_part(i, it, SLABW if i < 2 else HALF)
            with pool.Fori(4, N_END // 4) as it:
                for i in range(4):
                    low_part(i, it)
            for n in range(N_END // 4 * 4, N_END):
                low_part(n, 0)
            pool.wait_ge(exp_landed, 16)

        @block.tensor
        def _(pe):
            def split(n, it=0):
                pe.wait_ge(w_split, it * 4 + n + 1 + OPEN)

            def weights(n, c0):
                return slabH[:, n % SLOTS, c0:c0 + P], slabL[:, n % SLOTS, c0:c0 + P]

            for nothing_yet in (gate_mm, y_mm, a_mm, b_mm):
                pe.sem_inc(nothing_yet, OPEN)
            pe.wait_ge(exp_landed, 16)
            for n in range(12):
                c, g = n // 4, n % 4
                if n >= 4:
                    pe.wait_ge(ge_taken, n - 3)
                pe.matmul(ps[n % 4][:, 0:TOK], ex[:, (c * 4 + g) * P:(c * 4 + g) * P + P], gn[:, :],
                          start=True, stop=True).then_inc(ge_mm, 1)
            pe.wait_ge(ge_taken, 12)
            pe.wait_ge(u_split, 1)
            with pe.Fori(0, 4) as it:
                for i in range(4):
                    split(i, it)
                    for m in range(2):
                        bank = ps[4 * m + i]
                        if i < 2:
                            pe.wait_ge(gate_done, it * 4 + 2 * i + m - 3 + OPEN)
                        else:
                            pe.wait_ge(z_part, it * 4 + 2 * m + (i - 2) - 3 + OPEN)
                        if i == 2:
                            pe.wait_ge(o_split, 1)
                        if i == 3:
                            pe.wait_ge(ob_done, 1)
                        for k in range(KT if i < 2 else 4):
                            high, low = {0: (uH, uL), 1: (uH, uL), 2: (oH, oL), 3: (bH, bL)}[i]
                            last = split_matmul(pe, bank[:, 0:TOK], *weights(i, 256 * k + P * m), high[:, k, :],
                                                low[:, k, :], k == 0, k == (KT if i < 2 else 4) - 1)
                        last.then_inc(gate_mm if i < 2 else y_mm, 1)
            pe.wait_ge(z_done, 8 + OPEN)
            for m in range(KT):
                n = N_OUT + m // 2
                if m % 2 == 0:
                    split(n)
                if m >= 2:
                    pe.wait_ge(x_done, m - 1)
                for k in range(KT):
                    last = split_matmul(pe, ps[m % 2][:, 0:TOK], *weights(n, 256 * k + P * (m % 2)), zH[:, k, :],
                                        zL[:, k, :], k == 0, k == KT - 1)
                last.then_inc(mix_mm, 1)
            square_norm(pe, t["ones"], sq, ps[7], sq_done, 0, ss_mm)

            def up(it, group):
                for f in range(2):
                    pe.wait_ge(f_done, it * 4 + 2 * group + f - 3 + OPEN)
                    for half in range(2):
                        n = N_GU + 2 * group + half
                        if f == 0:
                            split(n, it)
                        bank = ps[4 * group + 2 * f + half]
                        for k in range(KT):
                            if group == f == half == 0:
                                pe.wait_ge(h_split, k + 1)
                            last = split_matmul(pe, bank[:, 0:TOK], *weights(n, 256 * k + P * f), uH[:, k, :],
                                                uL[:, k, :], k == 0, k == KT - 1)
                        last.then_inc(b_mm if half else a_mm, 1)

            with pe.Fori(0, 5) as it:
                for group in range(2):
                    up(it, group)
            up(5, 0)

            def down(n, it, tile, first=False, final=False):
                split(n, it)
                for f in range(2):
                    for m in (4, 5, 6, 7, 0, 1, 2, 3):
                        if first and f == 0 and m % 4 == 0:
                            pe.wait_ge(f_done, (FT - 2 if m else FT) + OPEN)
                        high, low = [g[:, tile + f, :] if isinstance(tile, int) else
                                     g[:, bass.ds(tile + f, 1), :].rearrange("p a b -> p (a b)") for g in (GH, GL)]
                        last = split_matmul(pe, ps[m][:, 0:TOK], *weights(n, D * f + P * m), high, low,
                                            first and f == 0, final and f == 1, skip_group_check=True)
                last.then_inc(down_mm, 1)

            down(N_DOWN, 0, 0, first=True)
            with pe.Fori(0, 2) as it:
                for i in range(4):
                    down(N_DOWN + 1 + i, it, it * 8 + 2 + 2 * i)
            down(N_DOWN + 9, 0, 18)
            down(N_DOWN + 10, 0, 20, final=True)
            pe.wait_ge(x_done, 2 * KT)
            square_norm(pe, t["ones"], sq, ps[7], sq_done, KT, ss_mm)
            for j in range(6):
                i, half = j // 2, j % 2
                pe.wait_ge(y_done, 4 * half + 4)
                t0, n = T_TILES[i]
                if j >= 2:
                    pe.wait_ge(y_dve if half else y_act, i)
                for k in range(4):
                    last = pe.transpose(ps[half][0:n, P * k:P * k + P], uT[:, 4 * half + k, t0:t0 + n], ident[:, :])
                last.then_inc(y_tr, 1)

        @block.scalar
        def _(act):
            def high_part(n, it, used, count, values=SLABW):
                s = n % SLOTS
                act.wait_ge(used, count)
                per = 32 if values == HALF and s == 3 else 16
                before = 16 * 4 if values == SLABW and s == 3 else 0
                act.wait_ge(slab_landed[s], it * per + per * (n // SLOTS + 1) + before)
                act.activation(slabH[:, s, 0:values], slab[:, s, 0:values], ACT.Copy).then_inc(w_high, 1)

            def high_mix(i, it):
                high_part(i, it, gate_mm if i < 2 else y_mm, it * 4 + 2 * (i % 2) - 2 + OPEN, SLABW if i < 2 else HALF)

            def high_out(i):
                high_part(N_OUT + i, 0, gate_mm if i < 2 else y_mm, 14 + 2 * (i % 2) + OPEN)

            def high_gu(i, it):
                act.wait_ge(mix_mm, 2 * i + 2)
                high_part(N_GU + i, it, b_mm if i % 2 else a_mm, it * 4 + 2 * (i // 2) - 2 + OPEN)

            def square(n, k):
                act.wait_ge(x_done, (n - 1) * KT + k + 1)
                act.activation(sq[:, k, :], xT[:, k, :], ACT.Square).then_inc(sq_done, 1)

            def root(n):
                act.wait_ge(ss_mm, n)
                act.activation(t["root"][:, :], ps[7][:, 0:TOK], ACT.Sqrt, bias=t["eps"][:, 0:1], scale=1.0 / D)\
                   .then_inc(root_done, 1)

            def sigmoids(i, it):
                for m in range(2):
                    act.wait_ge(z_done, it * 2 + m - 1 + OPEN)
                    act.wait_ge(gate_mm, it * 4 + 2 * i + m + 1 + OPEN)
                    act.activation(gates[:, m, i, :], ps[4 * m + i][:, 0:TOK], ACT.Sigmoid).then_inc(gate_done, 1)

            act.sem_inc(gate_done, OPEN)
            act.wait_ge(u_back, 16)
            act.activation(uH[:, :, :], uT[:, :, :], ACT.Copy).then_inc(u_high, 1)
            for i in range(4):
                high_mix(i, 0)
            with act.Fori(0, 3) as it:
                for i in range(4):
                    high_mix(i, it + 1)
                    if i < 2:
                        sigmoids(i, it)
            for i in range(4):
                high_out(i)
                if i < 2:
                    sigmoids(i, 3)
            for i in range(2):
                high_gu(i, 0)
            for k in range(KT):
                square(1, k)
            root(1)
            for k in range(KT):
                act.wait_ge(h_done, k + 1)
                act.activation(uH[:, k, :], uT[:, k, :], ACT.Copy).then_inc(h_high, 1)

            def silu(f, it):
                act.wait_ge(f_done, it * 4 + f - 3 + OPEN)
                act.wait_ge(a_mm, it * 4 + f + 1 + OPEN)
                act.activation(gates[:, f % 4 // 2, f % 2, :], ps[2 * (f % 4)][:, 0:TOK], ACT.Silu).then_inc(silu_done, 1)

            with act.Fori(0, 5) as it:
                high_gu(2, it)
                high_gu(3, it)
                silu(0, it)
                silu(1, it)
                high_gu(0, it + 1)
                high_gu(1, it + 1)
                silu(2, it)
                silu(3, it)
            high_part(N_DOWN, 0, a_mm, 20 + OPEN)
            high_part(N_DOWN + 1, 0, b_mm, 20 + OPEN)
            silu(20, 0)
            silu(21, 0)
            high_part(N_DOWN + 2, 0, a_mm, 22 + OPEN)
            high_part(N_DOWN + 3, 0, b_mm, 22 + OPEN)
            for i in range(4, 11):
                high_part(N_DOWN + i, 0, down_mm, i - 3)
            for k in range(KT):
                square(2, k)
            root(2)
            for i, (t0, n) in enumerate(T_TILES):
                act.wait_ge(y_tr, 2 * i + 1)
                act.activation(yn[0:n, i, 0:512], ps[0][0:n, :], ACT.Copy).then_inc(y_act, 1)

        @block.vector
        def _(dve):
            steps = Steps(dve, dve_step)
            for nothing_yet in (z_part, z_done, f_done):
                dve.sem_inc(nothing_yet, OPEN)
            dve.wait_ge(u_high, 1)
            dve.tensor_tensor(uL[:, :, :], uT[:, :, :], uH[:, :, :], ALU.subtract).then_inc(u_split, 1)
            dve.wait_ge(o_back, 64)
            dve.wait_ge(o_whole, 4)
            for n in range(12):
                c, g = n // 4, n % 4
                dve.wait_ge(ge_mm, n + 1)
                dve.tensor_tensor(oT[:, 1 + c, g, :], oT[:, 1 + c, g, :], ps[n % 4][:, 0:TOK], ALU.mult)\
                   .then_inc(ge_taken, 1)
            dve.wait_ge(ge_taken, 12)
            steps.do(dve.tensor_copy(oH[:, :, :], oT[:, 0, :, :]))
            dve.tensor_tensor(oL[:, :, :], oT[:, 0, :, :], oH[:, :, :], ALU.subtract).then_inc(o_split, 1)
            steps.do(dve.tensor_tensor(oT[:, 1, :, :], oT[:, 1, :, :], oT[:, 2, :, :], ALU.add))
            steps.do(dve.tensor_tensor(oT[:, 1, :, :], oT[:, 1, :, :], oT[:, 3, :, :], ALU.add))
            steps.do(dve.tensor_copy(bH[:, :, :], oT[:, 1, :, :]))
            dve.tensor_tensor(bL[:, :, :], oT[:, 1, :, :], bH[:, :, :], ALU.subtract).then_inc(ob_done, 1)

            def tile(x, n):
                return x[:, n, :] if isinstance(n, int) else x[:, bass.ds(n, 1), :].rearrange("p a b -> p (a b)")

            with dve.Fori(0, 4) as it:
                for m in range(2):
                    dve.wait_ge(z_done, it * 2 + m + OPEN)
                    for i in range(2):
                        dve.wait_ge(gate_done, it * 4 + 2 * i + m + 1 + OPEN)
                        dve.wait_ge(y_mm, it * 4 + 2 * i + m + 1 + OPEN)
                        dve.tensor_tensor(prod[:, i, :], gates[:, m, i, :], ps[4 * m + 2 + i][:, 0:TOK], ALU.mult)\
                           .then_inc(z_part, 1)
                    dve.wait_ge(z_part, it * 4 + 2 * m + 2 + OPEN)
                    dve.tensor_tensor(prod[:, 0, :], prod[:, 0, :], prod[:, 1, :], ALU.add).then_inc(z_step, 1)
                    dve.wait_ge(z_step, it * 4 + 2 * m + 1)
                    dve.tensor_copy(tile(zH, it * 2 + m), prod[:, 0, :]).then_inc(z_step, 1)
                    dve.wait_ge(z_step, it * 4 + 2 * m + 2)
                    dve.tensor_tensor(tile(zL, it * 2 + m), prod[:, 0, :], tile(zH, it * 2 + m), ALU.subtract)\
                       .then_inc(z_done, 1)

            def residual(m, bank, gate, before):
                dve.wait_ge(x_done, m + before)
                dve.scalar_tensor_tensor(xT[:, m, 0:SEQ], bank[:, 0:SEQ], mod[:, gate + m, 0:1], xT[:, m, 0:SEQ],
                                         ALU.mult, ALU.add)
                y = bank[:, SEQ:TOK].rearrange("p (b t) -> p b t", t=T)
                steps.do(dve.tensor_tensor(prod[:, 0, 0:NS].rearrange("p (b t) -> p b t", t=T), y,
                                           mod[:, gate + m, 1:9].unsqueeze(2).to_broadcast([P, NB, T]), ALU.mult))
                dve.tensor_tensor(xT[:, m, SEQ:TOK], xT[:, m, SEQ:TOK], prod[:, 0, 0:NS], ALU.add).then_inc(x_done, 1)

            dve.wait_ge(x_back, 16)
            for m in range(KT):
                dve.wait_ge(mix_mm, m + 1)
                residual(m, ps[m % 2], 16, 0)
            dve.wait_ge(root_done, 1)
            steps.do(dve.reciprocal(t["root"][:, :], t["root"][:, :]))
            modulate(dve, t, 1, 24, h_pre, h_mid, h_done, h_high, h_split)

            def product(f, it, col):
                buf = prod[:, f % 2, :]
                dve.wait_ge(f_done, it * 4 + f - 1 + OPEN)
                dve.wait_ge(silu_done, it * 4 + f + 1)
                dve.wait_ge(b_mm, it * 4 + f + 1 + OPEN)
                dve.tensor_tensor(buf, gates[:, f % 4 // 2, f % 2, :], ps[2 * (f % 4) + 1][:, 0:TOK], ALU.mult)\
                   .then_inc(f_step, 1)
                dve.wait_ge(f_step, it * 8 + 2 * f + 1)
                dve.tensor_copy(tile(GH, col), buf).then_inc(f_step, 1)
                dve.wait_ge(f_step, it * 8 + 2 * f + 2)
                dve.tensor_tensor(tile(GL, col), buf, tile(GH, col), ALU.subtract).then_inc(f_done, 1)

            with dve.Fori(0, 5) as it:
                for f in range(4):
                    product(f, it, it * 4 + f)
            for f in range(20, 22):
                product(f, 0, f)
            dve.wait_ge(down_mm, 11)
            for m in range(KT):
                residual(m, ps[m], 40, KT)
            dve.wait_ge(root_done, 2)
            steps.do(dve.reciprocal(t["root"][:, :], t["root"][:, :]))
            for k in range(KT):
                dve.scalar_tensor_tensor(uT[:, k, :], xT[:, k, :], t["vecT"][:, V_GZ + k:V_GZ + k + 1], t["root"][:, :],
                                         ALU.mult, ALU.mult).then_inc(y_done, 1)
            for i, (t0, n) in enumerate(T_TILES):
                dve.wait_ge(y_tr, 2 * i + 2)
                dve.tensor_copy(yn[0:n, i, 512:1024], ps[1][0:n, :]).then_inc(y_dve, 1)


def build(nc, d):
    with ExitStack() as persist:
        def sb(stack, name, shape, dt=F32):
            return stack.enter_context(nc.sbuf_tensor("t_" + name, shape, dt))

        def sem(name):
            return persist.enter_context(nc.semaphore(name))

        t = {}
        for name, shape in [("slab", [P, SLOTS, SLABW]), ("ident", [P, P]), ("ones", [P, P]),
                            ("vecT", [P, NVEC]), ("mod", [P, 48, 9]), ("amp", [P, 2, KT, 9]), ("eps", [P, 1]),
                            ("gn", [24, TOK])]:
            t[name] = sb(persist, name, shape)
        to_back, to_decode = ExitStack(), ExitStack()
        t["oT_s"] = sb(to_back, "oT_s", [P, 4, 4, NS])
        t["table"], t["index"] = sb(to_decode, "table", [P, NB], I32), sb(to_decode, "index", [P, NB], U32)
        ps = [persist.enter_context(nc.psum_tensor(f"ps{i}", [P, 512], F32)) for i in range(8)]
        for name, shape in [("hbias", [P, 4]), ("w2", [P, 2, 2, DH]), ("b2v", [1, DH]), ("seg_col", [P, 1]),
                            ("c64", [64, C64W]), ("qaT_s", [P, 4, NS + T]), ("qbT_s", [P, 4, NS + T]),
                            ("kaT_s", [P, 4, NS]), ("ksT_s", [P, NS]), ("kwT_s", [P, NS]), ("rows_s", [NS, ROWW])]:
            t[name] = sb(to_decode, name, shape)
        with ExitStack() as early:
            for name, shape in [("rows_p", [P, 2, ROWW]), ("qaT_p", [P, 4, SEQ]), ("qbT_p", [P, 4, SEQ]),
                                ("kaT_p", [P, 4, SEQ]), ("ksT_p", [P, SEQ]), ("kwT_p", [P, SEQ]),
                                ("cp", [P, CPW])]:
                t[name] = sb(early, name, shape)
            with ExitStack() as temps:
                for name, shape in [("root", [P, TOK]), ("wgn", [P, KT * 24]), ("xn", [P, 3, D]), ("cn", [9, D]), ("modn", [9, NADA * D]), ("vecn", [P, P]), ("cT", [P, 72]),
                                    ("xT", [P, KT, TOK]), ("uT", [P, KT, TOK]), ("sq", [P, KT, TOK])]:
                    t[name] = sb(temps, name, shape)
                front_block(nc, sem, t, d, ps)
            with ExitStack() as temps:
                for name, shape in [("segs", [PSEG, 8, 4, 2, DH]), ("XTp", [P, 2, 2, 8, PC1]),
                                    ("hidn", [PC1, 512]), ("hid_p", [P, 2, 2, 2 * PCMP]), ("ckT_p", [P, PSEG]), ("cv_p", [PSEG, P]),
                                    ("S_p", [P, 3, 2048]), ("PT_p", [P, 2, 2, H, P]),
                                    ("Sc_p", [P, 256]), ("PTc_p", [PSEG, 2 * H, P]), ("oT_p", [P, 4, 4, SEQ]),
                                    ("nmax_p", [P, 3, H]), ("sum_p", [P, 3, H]), ("rsum_p", [P, H]),
                                    ("cstat_p", [P, 2 * H])]:
                    t[name] = sb(temps, name, shape)
                prompt_block(nc, sem, t, d, ps)
        with ExitStack() as mid:
            for name, shape, dt in [("Kr", [P, 8, 512], F32), ("Vr", [P, V_SLOTS, 512], F32), ("nsa", [P, 2, 2048], F32),
                                    ("relay", [P, 2, 512], F32), ("vsel", [P, SEG, P], F32),
                                    ("XT", [P, 2, KV, 8, NSEG], F32), ("KTr", [P, 4, 512], F32),
                                    ("Sm", [64, PAST + 64], F32), ("Ss", [64, PAST + 64], F32), ("Sw", [64, WIN + 64], F32),
                                    ("Sc", [64, P], F32), ("PTm", [P, SEG + 1, 64], F32), ("PTs", [P, SEG + 1, 64], F32),
                                    ("PTw", [P, 6, 64], F32), ("hid", [P, 2, 2, 2 * NCMP], F32), ("ckT", [P, P], F32),
                                    ("cv", [P, P], F32), ("wkv", [P, 4, 256], F32), ("qa_cur", [P, 328], F32),
                                    ("qb_cur", [P, 64], F32), ("above8", [64, NMB, NMB], F32),
                                    ("equal8", [64, NMB, NMB], F32), ("gates4", [64, NMB, 4], F32), ("gate", [64, NMB], F32),
                                    ("rank", [64, CAND], F32), ("mb_mask", [64, NMB], F32), ("sel_mask", [64, NSB], F32),
                                    ("imp", [64, CAND], F32), ("nmax", [64, 4], F32), ("sums", [64, 4], F32),
                                    ("inv", [64, 4], F32), ("Om", [64, 512], F32), ("On", [64, 3, P], F32),
                                    ("index_now", [P, 2], U32)]:
                t[name] = sb(mid, name, shape, dt)
            decode_block(nc, sem, t, d, ps)
        to_decode.close()
        to_back.close()
        with ExitStack() as late:
            def place(stack, tensors):
                for name, shape, dt in tensors:
                    t[name] = stack.enter_context(nc.sbuf_tensor("b_" + name, shape, dt))

            def overlaid(*sets):
                for tensors in sets[:-1]:
                    with ExitStack() as here:
                        place(here, tensors)
                place(late, sets[-1])

            place(late, [("gates", [P, 2, 2, TOK], F32), ("root", [P, TOK], F32), ("xT", [P, KT, TOK], F32),
                         ("uT", [P, KT, TOK], F32), ("uL", [P, KT, TOK], F32R), ("slabH", [P, SLOTS, SLABW], F32R),
                         ("slabL", [P, SLOTS, SLABW], F32R), ("prod", [P, 2, TOK], F32)])
            overlaid([("sq", [P, KT, TOK], F32)], [("uH", [P, KT, TOK], F32R)])
            overlaid([("oT", [P, 4, 4, TOK], F32), ("oH", [P, 4, TOK], F32R), ("oL", [P, 4, TOK], F32R),
                      ("zH", [P, KT, TOK], F32R), ("zL", [P, KT, TOK], F32R)],
                     [("below", [P, 2, 4, TOK], F32), ("bH", [P, 4, TOK], F32R), ("bL", [P, 4, TOK], F32R)],
                     [("yn", [P, 3, D], F32)],
                     [("GH", [P, FT, TOK], F32R), ("GL", [P, FT, TOK], F32R)])
            back_block(nc, sem, t, d, ps)


_OUTS = [("y_prompt", (1, 256, 1024)), ("y_sample", (8, 8, 1024)), ("moba_kv_prompt", (1, 256, 2, 8, 64)),
         ("nsa_kv_prompt", (1, 256, 4, 2, 64)), ("nsa_win_prompt", (1, 256, 2, 2, 64)),
         ("moba_kv_sample", (8, 8, 2, 8, 64)), ("nsa_kv_sample", (8, 8, 4, 2, 64)),
         ("nsa_win_sample", (8, 512, 2, 2, 64))]


def constants():
    import numpy as np
    slope = 2.0 ** -(np.arange(H) + 1.0)
    ident = np.eye(P)
    ones = np.ones((P, P))
    row_h, row_t = np.repeat(np.arange(H), T), np.tile(np.arange(T), H)
    row_kv = row_h // G
    c64 = np.zeros((64, C64W))
    c64[:, C_GSUM:C_BDEC] = (row_kv[:, None] == row_kv) & (row_t[:, None] == row_t)
    kpos = SEG * np.arange(NSEG)[None, :] + np.arange(SEG)[:, None]
    c64[:, C_BDEC:C_BOWN] = -slope[row_h][:, None] * (PAST + row_t[:, None] - kpos.reshape(1, -1))
    own = np.full((64, NB, NB, T), NEG)
    for r in range(64):
        for b in range(NB):
            for u in range(row_t[r] + 1):
                own[r, b, b, u] = -slope[row_h[r]] * (row_t[r] - u)
    c64[:, C_BOWN:C_BWIN] = own.reshape(64, -1)
    wpos = PAST - WIN + (4 * np.arange(128)[None, :] + np.arange(4)[:, None]).reshape(1, -1)
    qpos = PAST + row_t[:, None]
    c64[:, C_BWIN:C_TIE] = np.where(wpos > qpos - WIN, -slope[row_h][:, None] * (qpos - wpos), NEG)
    c64[:, C_TIE:C_TIE8] = (np.arange(CAND)[None, :] < np.arange(CAND)[:, None]).reshape(1, -1)
    c64[:, C_TIE8:C64W] = (np.arange(NMB)[None, :] < np.arange(NMB)[:, None]).reshape(1, -1)
    cp = np.zeros((P, CPW))
    q, k = np.arange(P)[:, None, None], np.arange(256)[None, None, :]
    for qt, c0, nk in [(0, C_BP0, 128), (1, C_BP1, 256)]:
        dist = q + P * qt - k[:, :, :nk]
        cp[:, c0:c0 + 8 * nk] = np.where(dist >= 0, -slope[None, :, None] * dist, NEG).reshape(P, -1)
    n = np.arange(PSEG)[None, None, :]
    seen = (SEG * n + 2 * SEG - 1 <= np.arange(P)[:, None, None] + P * np.arange(2)[None, :, None]) & (n < PCMP)
    cp[:, C_MADD:C_MMUL] = np.where(seen, 0.0, NEG).reshape(P, -1)
    cp[:, C_MMUL:CPW] = seen.reshape(P, -1)
    expand = np.zeros((24, 3, 4, P))
    for kv in range(KV):
        for g in range(G):
            for c in range(3):
                expand[(kv * G + g) * 3 + c, c, g, DH * kv:DH * kv + DH] = 1.0
    return {"c_ident": ident, "c_ones": ones, "c_64": c64, "c_p": cp, "c_expand": expand.reshape(24, -1),
            "c_seg": np.arange(P)[:, None] % (PAGE // SEG)}


def kernel(**inputs):
    import numpy as np
    import concourse.bacc as bacc
    from concourse.bass_utils import run_bass_kernel_spmd

    nc = bacc.Bacc("TRN2", target_bir_lowering=False, num_devices=1)
    arrays, d = {}, {}
    shapes = {
        "x_prompt": (256, 1024), "x_sample": (64, 1024), "cache_moba_kv": (160 * 8, 16 * 1024),
        "cache_nsa_kv": (160 * 8, 16 * 512), "cache_nsa_win": (8, 512, 256)}
    for name, a in inputs.items():
        arrays[name] = np.ascontiguousarray(a)
    for name, a in constants().items():
        arrays[name] = np.ascontiguousarray(a.astype(np.float32))
    for name, a in arrays.items():
        if name in shapes:
            arrays[name] = a = a.reshape(shapes[name])
        d[name] = nc.dram_tensor(name, a.shape, mybir.dt.from_np(a.dtype), kind="ExternalInput").ap()
    flat = {"y_prompt": (256, 1024), "y_sample": (64, 1024), "moba_kv_prompt": (256, 1024), "nsa_kv_prompt": (256, 512),
            "nsa_win_prompt": (256, 256), "moba_kv_sample": (64, 1024), "nsa_kv_sample": (64, 512),
            "nsa_win_sample": (8, 512, 256)}
    for name, _ in _OUTS:
        d[name] = nc.dram_tensor(name, flat[name], F32, kind="ExternalOutput").ap()
    for name, shape in [("spill_x", (P, KT * TOK)), ("spill_u", (P, KT * TOK)), ("spill_o", (P, 16 * SEQ))]:
        d[name] = nc.dram_tensor(name, shape, F32, kind="Internal").ap()
    build(nc, d)
    r = run_bass_kernel_spmd(nc, [arrays], core_ids=[0]).results[0]
    return tuple(np.asarray(r[name]).reshape(shape) for name, shape in _OUTS)
```

```python
from contextlib import ExitStack

import concourse.bass as bass
from concourse import mybir

F32 = mybir.dt.float32
F32R = mybir.dt.float32r
I32 = mybir.dt.int32
U32 = mybir.dt.uint32
ALU = mybir.AluOpType
ACT = mybir.ActivationFunctionType
AX = mybir.AxisListType

P = 128
D = 1024
KT = D // P
SEQ = 256
NB = 8
T = 8
NS = NB * T
TOK = SEQ + NS
PAST = 2048
PAGE = 128
DH = 64
H = 8
KV = 2
G = H // KV
SEG = 16
NSEG = PAST // SEG
NCMP = NSEG - 1
PSEG = SEQ // SEG
PCMP = PSEG - 1
PC1 = 2 * PCMP + 1
MB = 256
NMB = PAST // MB
MTOP = 3
SB = 64
NSB = PAST // SB
CAND = NSB - 2
STOP = 16 - 3
WIN = 512
FF = 2816
FT = FF // P
NADA = 6
EPS = 1e-6
NEG = -1e30
SCALE = DH ** -0.5
QA, KA, VA, QB, KC, GN, GA, GB = 0, 512, 1024, 1536, 2048, 2816, 2840, 3864
RKA, RVA, RKC, RKS, RVS, RKW, RVW, ROWW = 0, 512, 1024, 1280, 1408, 1536, 1664, 1792
SLOTS = 4
OPEN = 4
SLABW = 2048
V_ADA, V_GA, V_GF, V_GZ, V_B1, V_PE, V_B2, NVEC = 0, 48, 56, 64, 72, 76, 108, 109
C_GSUM, C_BDEC, C_BOWN, C_BWIN, C_TIE, C_TIE8 = 0, 64, 64 + PAST, 64 + PAST + 512, 64 + PAST + 1024, 64 + PAST + 1024 + CAND * CAND
C64W = C_TIE8 + 64
C_BP0, C_BP1, C_MADD, C_MMUL, CPW = 0, 1024, 3072, 3104, 3136
T_TILES = [(0, 128), (128, 128), (256, 64)]


class Steps:

    def __init__(self, eng, sem, base=0):
        self.eng, self.sem, self.base, self.n = eng, sem, base, 0

    def do(self, ins):
        self.n += 1
        ins.then_inc(self.sem, 1)
        self.eng.wait_ge(self.sem, self.base + self.n)


def apart(eng, turns):
    eng.sem_inc(turns, 1)


def split_matmul(pe, out, w_high, w_low, x_high, x_low, start, stop, **kw):
    pe.matmul(out, w_high, x_high, start=start, stop=False, **kw)
    pe.matmul(out, w_high, x_low, start=False, stop=False, **kw)
    return pe.matmul(out, w_low, x_high, start=False, stop=stop, **kw)


def front_block(nc, sem, t, d, ps):
    w_high, w_split, u_high, u_split = sem("f_w_high"), sem("f_w_split"), sem("f_u_high"), sem("f_u_split")
    slabH, slabL, uH, uL = [t["f_H0"], t["f_H1"]], [t["f_L0"], t["f_L1"]], t["uH"], t["uL"]
    NW = 11
    loaded, x_loaded, c_loaded = sem("f_loaded"), sem("f_x_loaded"), sem("f_c_loaded")
    slab_landed = [sem(f"f_slab_landed{s}") for s in range(SLOTS)]
    slab_used = [sem(f"f_slab_used{s}") for s in range(SLOTS)]
    silu_done, x_tr, vec_tr, c_tr = sem("f_silu"), sem("f_x_tr"), sem("f_vec_tr"), sem("f_c_tr")
    xT_dve, xT_act, vecT_done, cT_done = sem("f_xT_dve"), sem("f_xT_act"), sem("f_vecT"), sem("f_cT")
    mod_done, sq_done, ss_mm, root_done = sem("f_mod"), sem("f_sq"), sem("f_ss_mm"), sem("f_root")
    u_done, q_mm, q_dve, q_act = sem("f_u"), sem("f_q_mm"), sem("f_q_dve"), sem("f_q_act")
    row_mm, row_dve, row_act = sem("f_row_mm"), sem("f_row_dve"), sem("f_row_act")
    kt_tr, kt_dve, kt_act = sem("f_kt_tr"), sem("f_kt_dve"), sem("f_kt_act")
    dve_step, stored, spilled = sem("f_dve_step"), t["rows_stored"], sem("f_spilled")
    u_pre, u_mid, modn_done, mod_tr = sem("f_u_pre"), sem("f_u_mid"), sem("f_modn"), sem("f_mod_tr")
    modn = t["modn"]
    table_landed, gn_mm = sem("f_table"), sem("f_gn_mm")
    slab, xn, cn, vecn = t["slab"], t["xn"], t["cn"], t["vecn"]
    xT, uT, sq, cT, vecT, mod = t["xT"], t["uT"], t["sq"], t["cT"], t["vecT"], t["mod"]
    ident, ones = t["ident"], t["ones"]
    rows_p, rows_s = t["rows_p"], t["rows_s"]
    NROWJ = 21

    with nc.Block() as block:

        @block.sync
        def _(sp):
            sp.dma_start(ident[:, :], d["c_ident"]).then_inc(c_loaded, 16)
            sp.dma_start(cn[0:1, :], d["c_prompt"]).then_inc(c_loaded, 16)
            sp.dma_start(cn[1:1 + NB, :], d["c_sample"]).then_inc(c_loaded, 16)
            w_ada = d["w_ada"].rearrange("(k p) n -> p k n", p=P)
            with sp.Fori(0, NADA) as it:
                for s in range(SLOTS):
                    sp.wait_ge(slab_used[s], it + OPEN)
                    half = 4 * (s % 2)
                    sp.dma_start(slab[:, s, :].rearrange("p (k n) -> p k n", k=4),
                                 w_ada[:, half:half + 4, bass.ds(it * D + 512 * (s // 2), 512)])\
                      .then_inc(slab_landed[s], 16)
            w_in = d["w_in"].rearrange("(k p) n -> p k n", p=P)
            for j in range(NW):
                s = j % SLOTS
                if j < SLOTS:
                    sp.wait_ge(slab_used[s], NADA + OPEN)
                else:
                    sp.wait_ge(w_split, j - SLOTS + 1)
                if j in (2, 3):
                    for n, (g, kv) in enumerate([(g, kv) for g in range(2) for kv in range(KV)]):
                        c0 = QB + kv * 256 + (2 * (j - 2) + g) * DH
                        sp.dma_start(slab[:, s, :].rearrange("p (k n) -> p k n", k=KT)[:, :, n * DH:n * DH + DH],
                                     w_in[:, :, c0:c0 + DH]).then_inc(slab_landed[s], 16)
                else:
                    c0 = [QA, QA + 256, 0, 0, KA, KA + 256, VA, VA + 256, KC, KC + 256, KC + 512][j]
                    sp.dma_start(slab[:, s, :].rearrange("p (k n) -> p k n", k=KT),
                                 w_in[:, :, c0:c0 + 256]).then_inc(slab_landed[s], 16)
            table = d["page_table"].rearrange("b g -> g b")
            for s in range(PAGE // SEG):
                sp.dma_start(t["table"][s:P:PAGE // SEG, :], table, allow_slow_non_contiguous=True).then_inc(table_landed, 16)
            sp.dma_start(t["seg_col"][:, :], d["c_seg"]).then_inc(table_landed, 16)
            sp.dma_start(t["cp"][:, :], d["c_p"]).then_inc(table_landed, 16)
            sp.dma_start(t["c64"][:, :], d["c_64"]).then_inc(table_landed, 16)
            sp.dma_start(t["wgn"][:, :].rearrange("p (k n) -> p k n", k=KT),
                           d["w_in"].rearrange("(k p) n -> p k n", p=P)[:, :, GN:GN + 24]).then_inc(table_landed, 16)
            sp.wait_ge(u_done, KT)
            sp.dma_start(d["spill_x"], xT[:, :, :].rearrange("p k n -> p (k n)")).then_inc(spilled, 16)
            sp.dma_start(d["spill_u"], uT[:, :, :].rearrange("p k n -> p (k n)")).then_inc(spilled, 16)
            sp.wait_ge(row_dve, 11)
            sp.wait_ge(row_act, 10)
            for i in range(2):
                tok = slice(P * i, P * i + P)
                sp.dma_start(d["moba_kv_prompt"][tok, :], rows_p[:, i, RKA:RKC]).then_inc(stored, 16)
                sp.dma_start(d["nsa_kv_prompt"][tok, :], rows_p[:, i, RKC:RKW]).then_inc(stored, 16)
                sp.dma_start(d["nsa_win_prompt"][tok, :], rows_p[:, i, RKW:ROWW]).then_inc(stored, 16)
            sp.dma_start(d["moba_kv_sample"], rows_s[:, RKA:RKC]).then_inc(stored, 16)
            sp.dma_start(d["nsa_kv_sample"], rows_s[:, RKC:RKW]).then_inc(stored, 16)
            for b in range(NB):
                sp.dma_start(d["nsa_win_sample"][b, WIN - T:WIN, :],
                             rows_s[T * b:T * b + T, RKW:ROWW]).then_inc(stored, 16)
            sp.wait_ge(spilled, 32)

        @block.gpsimd
        def _(pool):
            for i, (t0, n) in enumerate(T_TILES):
                src = d["x_sample"] if i == 2 else d["x_prompt"][t0:t0 + n, :]
                pool.dma_start(xn[0:n, i, :], src).then_inc(x_loaded, 16)
            pool.dma_start(vecn[V_ADA:V_GA, :], d["b_ada"].rearrange("(r c) -> r c", c=P)).then_inc(loaded, 16)
            pool.dma_start(vecn[V_GA:V_GF, :], d["g_attn"].rearrange("(r c) -> r c", c=P)).then_inc(loaded, 16)
            pool.dma_start(vecn[V_GF:V_GZ, :], d["g_ffn"].rearrange("(r c) -> r c", c=P)).then_inc(loaded, 16)
            pool.dma_start(vecn[V_GZ:V_B1, :], d["g_final"].rearrange("(r c) -> r c", c=P)).then_inc(loaded, 16)
            pool.dma_start(vecn[V_B1:V_PE, :], d["cmp_b1"].rearrange("w (r c) -> (w r) c", c=P)).then_inc(loaded, 16)
            pool.dma_start(vecn[V_PE:V_B2, :],
                           d["cmp_pe"].rearrange("w (r two) e -> (w r) (two e)", two=2)).then_inc(loaded, 16)
            for kv in range(KV):
                pool.dma_start(vecn[V_B2:NVEC, DH * kv:DH * kv + DH], d["cmp_b2"][0:1, :]).then_inc(loaded, 16)
            pool.dma_start(ones[:, :], d["c_ones"]).then_inc(loaded, 16)

            def low_part(j):
                pool.wait_ge(w_high, j + 1)
                pool.tensor_tensor(slabL[j % 2][:, :], slab[:, j % SLOTS, :], slabH[j % 2][:, :].bitcast(F32),
                                   ALU.subtract).then_inc(w_split, 1)

            for j in range(NW):
                low_part(j)

        @block.tensor
        def _(pe):
            pe.wait_ge(c_loaded, 48)
            pe.wait_ge(silu_done, 1)
            for k in range(KT):
                last = pe.transpose(ps[5][:, 9 * k:9 * k + 9], cn[0:9, P * k:P * k + P], ident[0:9, 0:9])
            last.then_inc(c_tr, 1)
            pe.wait_ge(cT_done, 1)
            pe.wait_ge(x_loaded, 48)
            for k in range(KT):
                if k >= 4:
                    pe.wait_ge(xT_dve if k % 2 == 0 else xT_act, k // 2 - 1)
                for i, (t0, n) in enumerate(T_TILES):
                    last = pe.transpose(ps[k % 4][:, t0:t0 + n], xn[0:n, i, P * k:P * k + P], ident[0:n, 0:n])
                last.then_inc(x_tr, 1)

            def ada(it):
                for g in range(2):
                    pe.wait_ge(modn_done, it * 2 + g - 1 + OPEN)
                    for half in range(2):
                        s = 2 * g + half
                        pe.wait_ge(slab_landed[s], it * 16 + 16)
                        for k in range(4):
                            c0 = 9 * (4 * half + k)
                            last = pe.matmul(ps[5 + g][0:9, :], cT[:, c0:c0 + 9], slab[:, s, 512 * k:512 * k + 512],
                                             start=s % 2 == 0 and k == 0, stop=s % 2 == 1 and k == 3)
                        last.then_inc(slab_used[s], 1)

            def mod_transposes(bank, first, n):
                pe.wait_ge(modn_done, (first + n) // 4 + OPEN)
                for i in range(n):
                    last = pe.transpose(bank[:, 9 * i:9 * i + 9], modn[:, P * (first + i):P * (first + i) + P],
                                        ident[0:9, 0:9])
                last.then_inc(mod_tr, 1)

            for nothing_yet in slab_used:
                pe.sem_inc(nothing_yet, OPEN)
            with pe.Fori(0, 2) as it:
                ada(it)
            pe.wait_ge(loaded, 16 * 9)
            pe.transpose(ps[4][:, 0:NVEC], vecn[0:NVEC, :], ident[0:NVEC, 0:NVEC]).then_inc(vec_tr, 1)
            for k in range(KT):
                pe.wait_ge(sq_done, k + 1)
                last = pe.matmul(ps[7][:, 0:TOK], ones[:, :], sq[:, k, :], start=k == 0, stop=k == KT - 1)
            last.then_inc(ss_mm, 1)
            pe.wait_ge(xT_dve, 4)
            mod_transposes(ps[0], 0, 16)
            with pe.Fori(2, NADA) as it:
                ada(it)
            mod_transposes(ps[1], 16, 32)
            pe.wait_ge(u_split, KT)
            pe.wait_ge(mod_done, 2)
            for m in range(8):
                j, ct = m // 2, m % 2
                if ct == 0:
                    pe.wait_ge(w_split, j + 1)
                if m >= 2:
                    pe.wait_ge(q_dve if m % 2 == 0 else q_act, m - 1 if m % 2 else m)
                for k in range(KT):
                    c = slice(256 * k + P * ct, 256 * k + P * ct + P)
                    last = split_matmul(pe, ps[m % 2][:, 0:TOK], slabH[j % 2][:, c], slabL[j % 2][:, c], uH[:, k, :],
                                        uL[:, k, :], k == 0, k == KT - 1)
                last.then_inc(q_mm, 1)
            for j in range(4, NW):
                pe.wait_ge(w_split, j + 1)
                for i, (t0, n) in enumerate(T_TILES):
                    r = 3 * (j - 4) + i
                    if r >= 4:
                        pe.wait_ge(row_dve if r % 2 == 0 else row_act, r // 2 - 1)
                    for k in range(KT):
                        c = slice(256 * k, 256 * k + 256)
                        last = split_matmul(pe, ps[2 + r % 4][0:n, 0:256], uH[:, k, t0:t0 + n], uL[:, k, t0:t0 + n],
                                            slabH[j % 2][:, c], slabL[j % 2][:, c], k == 0, k == KT - 1)
                    last.then_inc(row_mm, 1)
            pe.wait_ge(table_landed, 16 * (PAGE // SEG + 4))
            for k in range(KT):
                last = pe.matmul(ps[7][0:24, 0:TOK], t["wgn"][:, 24 * k:24 * k + 24], uT[:, k, :],
                                 start=k == 0, stop=k == KT - 1)
            last.then_inc(gn_mm, 1)
            pe.wait_ge(row_dve, 11)
            pe.wait_ge(row_act, 10)
            pe.wait_ge(q_dve, 8)
            pe.wait_ge(q_act, 8)
            for g, c0 in enumerate([RKA, RKA + 128, RKA + 256, RKA + 384, RKS, RKW]):
                if g >= 2:
                    pe.wait_ge(kt_dve if g % 2 == 0 else kt_act, 2 * (g // 2))
                for i, (t0, n) in enumerate(T_TILES):
                    src = rows_s[:, c0:c0 + P] if i == 2 else rows_p[:, i, c0:c0 + P]
                    last = pe.transpose(ps[g % 2][:, t0:t0 + n], src, ident[0:n, 0:n])
                last.then_inc(kt_tr, 1)

        def kT_dst(g):
            if g < 4:
                return t["kaT_p"][:, g, :], t["kaT_s"][:, g, 0:NS]
            return t["ksT_p" if g == 4 else "kwT_p"][:, :], t["ksT_s" if g == 4 else "kwT_s"][:, 0:NS]

        def q_dst(m):
            n = "qaT" if m < 4 else "qbT"
            return t[n + "_p"][:, m % 4, :], t[n + "_s"][:, m % 4, 0:NS]

        def row_dst(r):
            j, i = r // 3, r % 3
            return rows_s[:, 256 * j:256 * j + 256] if i == 2 else rows_p[:, i, 256 * j:256 * j + 256]

        @block.scalar
        def _(act):
            act.sem_inc(modn_done, OPEN)
            act.wait_ge(c_loaded, 48)
            act.activation(cn[0:9, :], cn[0:9, :], ACT.Silu).then_inc(silu_done, 1)
            for k in range(1, KT, 2):
                act.wait_ge(x_tr, k + 1)
                act.activation(xT[:, k, :], ps[k % 4][:, 0:TOK], ACT.Copy).then_inc(xT_act, 1)
            act.wait_ge(xT_dve, 4)
            act.wait_ge(xT_act, 4)
            for k in range(KT):
                act.activation(sq[:, k, :], xT[:, k, :], ACT.Square).then_inc(sq_done, 1)

            def vector_copies(it):
                for g in range(2):
                    act.wait_ge(slab_used[2 * g + 1], it + 1 + OPEN)
                    act.activation(modn[:, bass.ds(it * D + 512 * g, 512)], ps[5 + g][0:9, :], ACT.Copy)\
                       .then_inc(modn_done, 1)

            with act.Fori(0, 2) as it:
                vector_copies(it)
            act.wait_ge(ss_mm, 1)
            act.activation(t["root"][:, :], ps[7][:, 0:TOK], ACT.Sqrt, bias=t["eps"][:, 0:1], scale=1.0 / D)\
               .then_inc(root_done, 1)
            for k in range(KT):
                act.wait_ge(u_done, k + 1)
                act.activation(uH[:, k, :], uT[:, k, :], ACT.Copy).then_inc(u_high, 1)
            with act.Fori(2, NADA) as it:
                vector_copies(it)

            def high_part(j):
                if j == 0:
                    act.wait_ge(x_tr, KT)
                if j == 1:
                    act.wait_ge(mod_tr, 2)
                if j >= 2:
                    if j < 6:
                        act.wait_ge(q_mm, 2 * (j - 1))
                    else:
                        act.wait_ge(row_mm, 3 * (j - 5))
                s = j % SLOTS
                act.wait_ge(slab_landed[s], 16 * (NADA + j // SLOTS + 1) + (48 if s in (2, 3) else 0))
                act.activation(slabH[j % 2][:, :], slab[:, s, :], ACT.Copy).then_inc(w_high, 1)

            high_part(0)
            high_part(1)
            for m in range(1, 8, 2):
                p_out, s_out = q_dst(m)
                act.wait_ge(q_mm, m + 1)
                act.activation(p_out, ps[1][:, 0:SEQ], ACT.Copy).then_inc(q_act, 1)
                act.activation(s_out, ps[1][:, SEQ:TOK], ACT.Copy).then_inc(q_act, 1)
                high_part(m // 2 + 2)
            for r in range(1, NROWJ, 2):
                n = T_TILES[r % 3][1]
                act.wait_ge(row_mm, r + 1)
                act.activation(row_dst(r), ps[2 + r % 4][0:n, 0:256], ACT.Copy).then_inc(row_act, 1)
                for j in range(6, NW):
                    if r - 2 < 3 * (j - 5) - 1 <= r:
                        high_part(j)
            act.wait_ge(gn_mm, 1)
            act.activation(t["gn"][:, :], ps[7][0:24, 0:TOK], ACT.Sigmoid)
            for g in range(1, 6, 2):
                p_out, s_out = kT_dst(g)
                act.wait_ge(kt_tr, g + 1)
                act.activation(p_out, ps[1][:, 0:SEQ], ACT.Copy).then_inc(kt_act, 1)
                act.activation(s_out, ps[1][:, SEQ:TOK], ACT.Copy).then_inc(kt_act, 1)

        @block.vector
        def _(dve):
            steps = Steps(dve, dve_step)
            steps.do(dve.memset(t["eps"][:, :], EPS))
            for n in ("qaT_s", "qbT_s"):
                steps.do(dve.memset(t[n][:, :, NS:NS + T], 0.0))
            dve.wait_ge(c_tr, 1)
            dve.tensor_copy(cT[:, :], ps[5][:, 0:72]).then_inc(cT_done, 1)
            for k in range(0, KT, 2):
                dve.wait_ge(x_tr, k + 1)
                dve.tensor_copy(xT[:, k, :], ps[k % 4][:, 0:TOK]).then_inc(xT_dve, 1)
            dve.wait_ge(vec_tr, 1)
            dve.tensor_copy(vecT[:, :], ps[4][:, 0:NVEC]).then_inc(vecT_done, 1)
            dve.wait_ge(vecT_done, 1)
            dve.wait_ge(root_done, 1)
            dve.wait_ge(xT_act, 4)
            steps.do(dve.reciprocal(t["root"][:, :], t["root"][:, :]))

            def vectors(bank, first, n, which, scale, g0):
                bias = vecT[:, V_ADA + first:V_ADA + first + n].unsqueeze(2).to_broadcast([P, n, 9])
                dve.wait_ge(mod_tr, which + 1)
                dve.tensor_tensor(mod[:, first:first + n, :], bank[:, 0:9 * n].rearrange("p (a b) -> p a b", b=9),
                                  bias, ALU.add).then_inc(mod_done, 1)
                dve.wait_ge(mod_done, which + 1)
                g = vecT[:, g0:g0 + KT].unsqueeze(2).to_broadcast([P, KT, 9])
                steps.do(dve.scalar_tensor_tensor(t["amp"][:, which, :, :], mod[:, scale:scale + KT, :], 1.0, g,
                                                  ALU.add, ALU.mult))

            vectors(ps[0], 0, 16, 0, 8, V_GA)
            modulate(dve, t, 0, 0, u_pre, u_mid, u_done, u_high, u_split)
            vectors(ps[1], 16, 32, 1, 32, V_GF)
            for m in range(0, 8, 2):
                p_out, s_out = q_dst(m)
                dve.wait_ge(q_mm, m + 1)
                dve.tensor_copy(p_out, ps[0][:, 0:SEQ]).then_inc(q_dve, 1)
                dve.tensor_copy(s_out, ps[0][:, SEQ:TOK]).then_inc(q_dve, 1)
            for r in range(0, NROWJ, 2):
                n = T_TILES[r % 3][1]
                dve.wait_ge(row_mm, r + 1)
                dve.tensor_copy(row_dst(r), ps[2 + r % 4][0:n, 0:256]).then_inc(row_dve, 1)
            for g in range(0, 6, 2):
                p_out, s_out = kT_dst(g)
                dve.wait_ge(kt_tr, g + 1)
                dve.tensor_copy(p_out, ps[0][:, 0:SEQ]).then_inc(kt_dve, 1)
                dve.tensor_copy(s_out, ps[0][:, SEQ:TOK]).then_inc(kt_dve, 1)
            dve.wait_ge(table_landed, 16 * (PAGE // SEG + 4))
            steps.do(dve.tensor_scalar(t["index"][:, :], t["table"][:, :], float(PAGE // SEG), t["seg_col"][:, 0:1],
                                       ALU.mult, ALU.add))


def modulate(dve, t, which, shift, pre, mid, done, high=None, split=None):
    xT, uT, amp, mod = t["xT"], t["uT"], t["amp"], t["mod"]
    for step in range(KT + (3 if high else 2)):
        if step < KT:
            dve.tensor_tensor(uT[:, step, :], xT[:, step, :], t["root"][:, :], ALU.mult).then_inc(pre, 1)
        k = step - 1
        if 0 <= k < KT:
            dve.wait_ge(pre, k + 1)
            dve.tensor_scalar(uT[:, k, 0:SEQ], uT[:, k, 0:SEQ], amp[:, which, k, 0:1], mod[:, shift + k, 0:1],
                              ALU.mult, ALU.add)
            u = uT[:, k, SEQ:TOK].rearrange("p (b t) -> p b t", t=T)
            dve.tensor_tensor(u, u, amp[:, which, k, 1:9].unsqueeze(2).to_broadcast([P, NB, T]), ALU.mult)\
               .then_inc(mid, 1)
        k = step - 2
        if 0 <= k < KT:
            dve.wait_ge(mid, k + 1)
            u = uT[:, k, SEQ:TOK].rearrange("p (b t) -> p b t", t=T)
            dve.tensor_tensor(u, u, mod[:, shift + k, 1:9].unsqueeze(2).to_broadcast([P, NB, T]), ALU.add)\
               .then_inc(done, 1)
        k = step - 3
        if high and k >= 0:
            dve.wait_ge(high, k + 1)
            dve.tensor_tensor(t["uL"][:, k, :], uT[:, k, :], t["uH"][:, k, :], ALU.subtract).then_inc(split, 1)


UNITS = [(br, qt) for br in (0, 2, 3) for qt in range(2)]
BR_MOBA, BR_CMP, BR_SEL, BR_WIN = range(4)


def head_at(branch, half, tile):
    return 2 * tile + half if branch == BR_MOBA else G * half + tile


def score_banks(u):
    return 4 if UNITS[u][1] else 2


def prompt_block(nc, sem, t, d, ps):
    w1_landed, segs_landed, window_kept = sem("p_w1"), sem("p_segs"), sem("p_window")
    seg_tr, segs_done, hidn_done, hid_tr, hbias_done = (sem("p_seg_tr"), sem("p_segs_done"), sem("p_hidn"),
                                                        sem("p_hid_tr"), sem("p_hbias"))
    conv_mm, gelu_done, ckcv_mm, ck_done, cv_done = (sem("p_conv_mm"), sem("p_gelu"), sem("p_ckcv_mm"), sem("p_ck"),
                                                     sem("p_cv"))
    cs_mm, csub_done, cexp_done, cp_ready = sem("p_cs_mm"), sem("p_csub"), sem("p_cexp"), sem("p_cprob")
    scores_mm, scores_taken, max_done, exp_done, p_ready = (sem("p_scores_mm"), sem("p_scores_taken"), sem("p_max"),
                                                            sem("p_exp"), sem("p_prob"))
    pt_tr, pt_dve, pt_act, pv_mm, pv_taken = (sem("p_pt_tr"), sem("p_pt_dve"), sem("p_pt_act"), sem("p_pv_mm"),
                                              sem("p_pv_taken"))
    dve_step, spilled = sem("p_dve_step"), sem("p_spilled")
    w1 = t["slab"][:, :, :].rearrange("p (w a) (b n) -> p w (a b) n", w=2, n=256)
    segs, XT, hid, ckT, cv = t["segs"], t["XTp"], t["hid_p"], t["ckT_p"], t["cv_p"]
    S, PT, Sc, PTc, cp, oT = t["S_p"], t["PT_p"], t["Sc_p"], t["PTc_p"], t["cp"], t["oT_p"]
    ident, vecT, hbias, rows = t["ident"], t["vecT"], t["hbias"], t["rows_p"]
    hidn = t["hidn"]
    NU = len(UNITS)
    jobs_of = [2 * (qt + 1) for _, qt in UNITS]
    first_cmp_job = sum(jobs_of[:NU - 1])
    first_job = [sum(jobs_of[:u]) + (4 if u == NU - 1 else 0) for u in range(NU)]
    output_of = [u + (2 if u == NU - 1 else 0) for u in range(NU)]
    CMP_OUT = NU - 1

    with nc.Block() as block:

        @block.sync
        def _(sp):
            sp.wait_ge(t["rows_stored"], 16 * (6 + 2 + NB))
            src = d["nsa_kv_prompt"].rearrange("(s lp l2) c -> s lp l2 c", lp=8, l2=2)
            for c in range(4):
                for l2 in range(2):
                    sp.dma_start(segs[:, :, c, l2, :], src[:, :, l2, DH * c:DH * c + DH]).then_inc(segs_landed, 16)
            for w in range(2):
                sp.dma_start(w1[:, w, :, :], d["cmp_w1"][w].rearrange("(lp p) n -> p lp n", p=P)).then_inc(w1_landed, 16)
                sp.dma_start(t["w2"][:, w, :, :], d["cmp_w2"][w].rearrange("(h p) e -> p h e", p=P)).then_inc(w1_landed, 16)
            sp.dma_start(t["b2v"][:, :], d["cmp_b2"][1:2, :]).then_inc(w1_landed, 16)
            sp.dma_start(d["nsa_win_sample"][:, 0:WIN - T, :], d["cache_nsa_win"][:, T:WIN, :]).then_inc(window_kept, 16)
            sp.wait_ge(window_kept, 16)
            for br, outputs in ((BR_MOBA, 2), (BR_SEL, 4), (BR_CMP, CMP_OUT + 2), (BR_WIN, NU + 2)):
                sp.wait_ge(pv_taken, outputs)
                sp.dma_start(d["spill_o"][:, br * 4 * SEQ:(br + 1) * 4 * SEQ],
                             oT[:, br, :, :].rearrange("p g t -> p (g t)")).then_inc(spilled, 16)
            sp.wait_ge(spilled, 64)

        @block.tensor
        def _(pe):
            def scores(u):
                br, qt = UNITS[u]
                nk = P * (qt + 1)
                before = sum(score_banks(v) for v in range(u))
                if u:
                    pe.wait_ge(scores_taken, before)
                for slot in range(H):
                    half, tile = slot // 4, slot % 4
                    rows64 = slice(DH * half, DH * half + DH)
                    qT = t["qaT_p" if br == BR_MOBA else "qbT_p"][rows64, tile, P * qt:P * qt + P]
                    kT = (t["kaT_p"][rows64, tile, 0:nk] if br == BR_MOBA
                          else t["ksT_p" if br == BR_SEL else "kwT_p"][rows64, 0:nk])
                    col = slot * nk
                    last = pe.matmul(ps[col // 512][:, col % 512:col % 512 + nk], qT, kT, start=True, stop=True)
                    if (col + nk) % 512 == 0:
                        last.then_inc(scores_mm, 1)

            def staging(job):
                if job >= 2:
                    pe.wait_ge(pt_dve if job % 2 == 0 else pt_act, job // 2)
                return ps[4 + job % 2]

            def attend(u):
                br, qt = UNITS[u]
                pe.wait_ge(p_ready, u + 1)
                for i in range(jobs_of[u]):
                    bank = staging(first_job[u] + i)
                    kt, h0 = i // 2, 4 * (i % 2)
                    for h in range(h0, h0 + 4):
                        col = h * P * (qt + 1) + P * kt
                        last = pe.transpose(bank[:, P * (h - h0):P * (h - h0) + P], S[:, u % 3, col:col + P], ident[:, :])
                    last.then_inc(pt_tr, 1)
                done = first_job[u] + jobs_of[u]
                pe.wait_ge(pt_dve, done // 2)
                pe.wait_ge(pt_act, done // 2)
                if u:
                    pe.wait_ge(pv_taken, output_of[u])
                if u == 4:
                    pe.wait_ge(csub_done, 1)
                for slot in range(H):
                    half, tile = slot // 4, slot % 4
                    h = head_at(br, half, tile)
                    c0 = {BR_MOBA: RVA + h * DH, BR_SEL: RVS + half * DH, BR_WIN: RVW + half * DH}[br]
                    for kt in range(qt + 1):
                        last = pe.matmul(ps[6][DH * half:DH * half + DH, P * tile:P * tile + P],
                                         rows[:, kt, c0:c0 + DH], PT[:, u % 2, kt, slot, :], start=kt == 0, stop=kt == qt)
                last.then_inc(pv_mm, 1)

            def segment_transposes():
                pe.wait_ge(segs_landed, 16 * 8)
                for lp in range(8):
                    for c in range(4):
                        last = pe.transpose(ps[7][:, (c * 8 + lp) * PSEG:(c * 8 + lp + 1) * PSEG],
                                            segs[:, lp, c, :, :].rearrange("s a e -> s (a e)"), ident[0:PSEG, 0:PSEG])
                last.then_inc(seg_tr, 1)

            def hidden_layer():
                pe.wait_ge(w1_landed, 16 * 5)
                pe.wait_ge(segs_done, 5)
                for w in range(2):
                    for part in range(2):
                        for lp in range(8):
                            last = pe.matmul(ps[7][0:PC1, 256 * w:256 * w + 256], XT[:, w, part, lp, :],
                                             w1[:, w, 8 * part + lp, :], start=part == 0 and lp == 0,
                                             stop=part == 1 and lp == 7)
                last.then_inc(conv_mm, 1)

            def hidden_transposes():
                pe.wait_ge(hidn_done, 1)
                for c in range(4):
                    last = pe.transpose(ps[7][:, 32 * c:32 * c + PC1], hidn[:, P * c:P * c + P], ident[0:PC1, 0:PC1])
                last.then_inc(hid_tr, 1)

            def keys_and_values():
                pe.wait_ge(gelu_done, 4)
                compressed_keys(pe, ps[7], t, hid, 0, PCMP)
                last = compressed_values(pe, ps[7][:, P:2 * P], t, hid, 0, PCMP)
                last.then_inc(ckcv_mm, 1)

            def compressed_scores():
                pe.wait_ge(ck_done, 2)
                pe.wait_ge(cv_done, 2)
                pe.wait_ge(pv_taken, 4)
                for qt in range(2):
                    for slot in range(H):
                        half, g = slot // 4, slot % 4
                        rows64 = slice(DH * half, DH * half + DH)
                        col = (qt * G + g) * PSEG
                        last = pe.matmul(ps[6 if half else 7][:, col:col + PSEG],
                                         t["qbT_p"][rows64, g, P * qt:P * qt + P], ckT[rows64, :], start=True, stop=True)
                last.then_inc(cs_mm, 1)

            def compressed_attention():
                pe.wait_ge(cp_ready, 2)
                for j in range(4):
                    bank = staging(first_cmp_job + j)
                    for i in range(4):
                        n = 4 * j + i
                        last = pe.transpose(bank[0:PSEG, P * i:P * i + P], Sc[:, n * PSEG:n * PSEG + PSEG], ident[:, :])
                    last.then_inc(pt_tr, 1)
                for qt in range(2):
                    pe.wait_ge(pt_act, first_cmp_job // 2 + qt + 1)
                    pe.wait_ge(pt_dve, first_cmp_job // 2 + qt + 1)
                    pe.wait_ge(pv_taken, CMP_OUT + qt)
                    for h in range(H):
                        half, g = h // 4, h % 4
                        last = pe.matmul(ps[6][DH * half:DH * half + DH, P * g:P * g + P],
                                         cv[:, DH * half:DH * half + DH], PTc[:, qt * H + h, :], start=True, stop=True)
                    last.then_inc(pv_mm, 1)

            between = [(segment_transposes, hidden_layer), (hidden_transposes,), (keys_and_values,),
                       (compressed_scores,), (compressed_attention,), ()]
            scores(0)
            scores(1)
            for u in range(NU):
                if u + 2 < NU:
                    scores(u + 2)
                attend(u)
                for step in between[u]:
                    step()

        def pt_dst(job):
            if pt_rows(job) == PSEG:
                j = job - first_cmp_job
                return PTc[:, 4 * j:4 * j + 4, :].rearrange("p a b -> p (a b)")
            u = max(v for v in range(NU) if first_job[v] <= job)
            i = job - first_job[u]
            return PT[:, u % 2, i // 2, 4 * (i % 2):4 * (i % 2) + 4, :].rearrange("p a b -> p (a b)")

        def pt_rows(job):
            return PSEG if first_cmp_job <= job < first_cmp_job + 4 else P

        @block.scalar
        def _(act):
            def pt_copy(job):
                act.wait_ge(pt_tr, job + 1)
                act.activation(pt_dst(job), ps[4 + job % 2][0:pt_rows(job), :], ACT.Copy).then_inc(pt_act, 1)

            def pv_copy(n, br, qt):
                act.wait_ge(pv_mm, n + 1)
                act.activation(oT[:, br, :, P * qt:P * qt + P], ps[6][:, :].rearrange("p (g q) -> p g q", g=4),
                               ACT.Copy).then_inc(pv_taken, 1)

            def exps(u):
                qt = UNITS[u][1]
                nk = P * (qt + 1)
                act.wait_ge(max_done, u + 1)
                for h in range(H):
                    act.activation(S[:, u % 3, h * nk:h * nk + nk], S[:, u % 3, h * nk:h * nk + nk], ACT.Exp,
                                   bias=t["nmax_p"][:, u % 3, h:h + 1], accum_out=t["sum_p"][:, u % 3, h:h + 1])\
                       .then_inc(exp_done, 1)

            def hidden_copy():
                act.wait_ge(conv_mm, 1)
                act.activation(hidn[:, :], ps[7][0:PC1, :], ACT.Copy).then_inc(hidn_done, 1)

            def gelu():
                act.wait_ge(hbias_done, 1)
                for w in range(2):
                    for ht in range(2):
                        c = 2 * w + ht
                        act.activation(hid[:, w, ht, :], ps[7][:, 32 * c:32 * c + 2 * PCMP], ACT.Gelu_apprx_tanh,
                                       bias=hbias[:, c:c + 1]).then_inc(gelu_done, 1)

            def keys_and_values():
                act.wait_ge(ckcv_mm, 1)
                act.wait_ge(ck_done, 1)
                act.activation(ckT[:, 0:PCMP], ps[7][:, 0:PCMP], ACT.Identity, bias=vecT[:, V_B2:V_B2 + 1])\
                   .then_inc(ck_done, 1)
                act.wait_ge(cv_done, 1)
                act.activation(cv[0:PCMP, :], ps[7][0:PCMP, P:2 * P], ACT.Copy).then_inc(cv_done, 1)

            def compressed_exps():
                act.wait_ge(csub_done, 1)
                act.activation(Sc[:, :], Sc[:, :], ACT.Exp).then_inc(cexp_done, 1)

            def compressed_outputs():
                for j in (1, 3):
                    pt_copy(first_cmp_job + j)
                for qt in range(2):
                    pv_copy(CMP_OUT + qt, BR_CMP, qt)

            between = [hidden_copy, gelu, keys_and_values, compressed_exps, compressed_outputs, None]
            exps(0)
            exps(1)
            for u, (br, qt) in enumerate(UNITS):
                for job in range(first_job[u] + 1, first_job[u] + jobs_of[u], 2):
                    pt_copy(job)
                if u + 2 < NU:
                    exps(u + 2)
                pv_copy(output_of[u], br, qt)
                if between[u]:
                    between[u]()

        @block.vector
        def _(dve):
            steps = Steps(dve, dve_step)

            def pt_copy(job):
                dve.wait_ge(pt_tr, job + 1)
                dve.tensor_copy(pt_dst(job), ps[4 + job % 2][0:pt_rows(job), :]).then_inc(pt_dve, 1)

            def biased(u):
                qt = UNITS[u][1]
                nk = P * (qt + 1)
                before = sum(score_banks(v) for v in range(u))
                c0 = C_BP1 if qt else C_BP0
                if u >= 3:
                    dve.wait_ge(pt_tr, first_job[u - 3] + jobs_of[u - 3])
                bias = cp[:, c0:c0 + H * nk].rearrange("p (h k) -> p h k", h=H)
                n = 512 // nk
                for b in range(score_banks(u)):
                    h0 = head_at(UNITS[u][0], n * b // 4, n * b % 4)
                    step = 2 if UNITS[u][0] == BR_MOBA else 1
                    dve.wait_ge(scores_mm, before + b + 1)
                    dve.scalar_tensor_tensor(S[:, u % 3, 512 * b:512 * b + 512].rearrange("p (h k) -> p h k", h=n),
                                             ps[b][:, :].rearrange("p (h k) -> p h k", h=n), SCALE,
                                             bias[:, h0:h0 + step * (n - 1) + 1:step, :], ALU.mult, ALU.add)\
                       .then_inc(scores_taken, 1)
                dve.wait_ge(scores_taken, before + score_banks(u))
                dve.tensor_reduce(t["nmax_p"][:, u % 3, :], S[:, u % 3, 0:H * nk].rearrange("p (h k) -> p h k", h=H),
                                  AX.X, ALU.max, negate=True).then_inc(max_done, 1)

            def normed(u):
                qt = UNITS[u][1]
                nk = P * (qt + 1)
                dve.wait_ge(exp_done, H * (u + 1))
                steps.do(dve.reciprocal(t["rsum_p"][:, :], t["sum_p"][:, u % 3, :]))
                s = S[:, u % 3, 0:H * nk].rearrange("p (h k) -> p h k", h=H)
                dve.tensor_tensor(s, s, t["rsum_p"][:, :].unsqueeze(2).to_broadcast([P, H, nk]), ALU.mult)\
                   .then_inc(p_ready, 1)

            def segment_copies():
                dve.wait_ge(seg_tr, 1)
                for w in range(2):
                    for part in range(2):
                        dve.tensor_copy(XT[:, w, part, :, 0:2 * PCMP].rearrange("p l (v n) -> p v l n", v=KV),
                                        ps[7][:, 256 * w:256 * w + 256].rearrange("p (v l s) -> p v l s", v=KV, l=8)
                                        [:, :, :, part:part + PCMP]).then_inc(segs_done, 1)
                dve.tensor_copy(XT[:, :, :, :, :].rearrange("p w a l n -> p (w a l) n")[:, :, 2 * PCMP],
                                vecT[:, V_PE:V_B2]).then_inc(segs_done, 1)

            def hidden_bias():
                dve.wait_ge(hid_tr, 1)
                dve.tensor_tensor(hbias[:, :], ps[7][:, 2 * PCMP:P:32], vecT[:, V_B1:V_PE], ALU.add)\
                   .then_inc(hbias_done, 1)

            s3 = Sc[:, :].rearrange("p (r n) -> p r n", n=PSEG)
            stat = t["cstat_p"]

            def compressed_scores():
                dve.wait_ge(cs_mm, 1)
                for qt, half in [(0, 0), (0, 1), (1, 0), (1, 1)]:
                    m = cp[:, C_MADD + PSEG * qt:C_MADD + PSEG * qt + PSEG].unsqueeze(1).to_broadcast([P, G, PSEG])
                    c = slice(P * qt + 64 * half, P * qt + 64 * half + 64)
                    raw = ps[6 if half else 7][:, 64 * qt:64 * qt + 64]
                    last = dve.scalar_tensor_tensor(Sc[:, c].rearrange("p (h n) -> p h n", h=G),
                                                    raw.rearrange("p (h n) -> p h n", h=G), SCALE, m,
                                                    ALU.mult, ALU.add)
                steps.do(last)
                steps.do(dve.tensor_reduce(stat[:, :], s3, AX.X, ALU.max))
                dve.tensor_tensor(s3, s3, stat[:, :].unsqueeze(2).to_broadcast([P, 2 * H, PSEG]), ALU.subtract)\
                   .then_inc(csub_done, 1)

            def compressed_probs():
                dve.wait_ge(cexp_done, 1)
                for qt in range(2):
                    m = cp[:, C_MMUL + PSEG * qt:C_MMUL + PSEG * qt + PSEG].unsqueeze(1).to_broadcast([P, H, PSEG])
                    s = Sc[:, P * qt:P * qt + P].rearrange("p (h n) -> p h n", h=H)
                    last = dve.tensor_tensor(s, s, m, ALU.mult)
                steps.do(last)
                steps.do(dve.tensor_reduce(stat[:, :], s3, AX.X, ALU.add))
                steps.do(dve.tensor_scalar(stat[:, :], stat[:, :], 1e-30, None, ALU.max))
                steps.do(dve.reciprocal(stat[:, :], stat[:, :]))
                for qt in range(2):
                    s = Sc[:, P * qt:P * qt + P].rearrange("p (h n) -> p h n", h=H)
                    dve.tensor_tensor(s, s, stat[:, H * qt:H * qt + H].unsqueeze(2).to_broadcast([P, H, PSEG]), ALU.mult)\
                       .then_inc(cp_ready, 1)

            dve.memset(ckT[:, :], 0.0).then_inc(ck_done, 1)
            dve.memset(cv[:, :], 0.0).then_inc(cv_done, 1)
            def compressed_outputs():
                compressed_probs()
                for j in (0, 2):
                    pt_copy(first_cmp_job + j)

            between = [segment_copies, hidden_bias, None, compressed_scores, compressed_outputs, None]
            biased(0)
            biased(1)
            for u in range(NU):
                normed(u)
                if u + 2 < NU:
                    biased(u + 2)
                for job in range(first_job[u], first_job[u] + jobs_of[u], 2):
                    pt_copy(job)
                if between[u]:
                    between[u]()


def compress(pe, out, w1, XT, w, ht, n, parts=(0, 1)):
    for part in parts:
        for lp in range(8):
            last = pe.matmul(out, w1[:, w, 8 * part + lp, P * ht:P * ht + P], XT[:, w, :, lp, part:part + n],
                             start=part == 0 and lp == 0, stop=part == 1 and lp == 7)
    return last


def compressed_keys(pe, bank, t, hid, w, n):
    for kv in range(KV):
        for ht in range(2):
            last = pe.matmul(bank[DH * kv:DH * kv + DH, 0:n], t["w2"][:, 0, ht, :], hid[:, 0, ht, n * kv:n * kv + n],
                             start=ht == 0, stop=ht == 1)
    return last


def compressed_values(pe, bank, t, hid, w, n):
    for kv in range(KV):
        out = bank[0:n, DH * kv:DH * kv + DH]
        for ht in range(2):
            pe.matmul(out, hid[:, 1, ht, n * kv:n * kv + n], t["w2"][:, 1, ht, :], start=ht == 0, stop=False)
        last = pe.matmul(out, t["ones"][0:1, 0:n], t["b2v"][:, :], start=False, stop=True)
    return last


GROUPS = ([grp for q in range(4) for grp in [("cmp", q, 0), ("cmp", q, 1), ("sel", q, 0)]
           + [("moba", q, hp) for hp in range(4)]] + [("win", 0, 0)])
NG = len(GROUPS)
SCORED = [g for g in range(NG) if GROUPS[g][0] != "cmp"]
NM = len(SCORED)
EVEN, ODD = (NG + 1) // 2, NG // 2
N_SCORE = 9
N_RING, N_SMALL, N_OUT = 13, 4, 3
T_BANKS = (0, 1, 4, 5)
LAG = 3
R_HID_K0, R_HID_K1, R_HID_V0, R_KEYS, R_HID_V1, R_VALUES, R_PTM, R_PTW, R_PTS = 0, 1, 2, 3, 4, 5, 6, 9, 10
DVE_STEPS = 19
V_SLOTS = 12
E_MOBA, E_WIN, E_CMP, E_SEL = range(4)


def bank_of_scores(g):
    kind, q, _ = GROUPS[g]
    return {"sel": 2 * q, "moba": 2 * q + 1, "win": 8}[kind]


def last_group(s):
    return max(g for g in SCORED if bank_of_scores(g) == s)


def transposed(kind, q):
    return max(g for g in range(NG) if GROUPS[g][:2] == (kind, q)) + 1


def mix_slab(sp, d, slab, i, it, landed):
    w = d["w_in"].rearrange("(k p) n -> p k n", p=P)
    dst = slab[:, i, :].rearrange("p (k n) -> p k n", k=KT)

    def cols(c0=0):
        return slice(c0, c0 + 256) if isinstance(it, int) else bass.ds(it * 256 + c0, 256)

    if i < 2:
        sp.dma_start(dst, w[:, :, cols(GB if i else GA)]).then_inc(landed[i], 16)
    elif i == 2:
        sp.dma_start(dst[:, 0:4, :], d["w_pa"].rearrange("(k p) n -> p k n", p=P)[:, :, cols()]).then_inc(landed[i], 16)
    else:
        w_pb = d["w_pb"].rearrange("(v g e) n -> v e g n", v=KV, g=G)
        for v in range(KV):
            sp.dma_start(dst[DH * v:DH * v + DH, 0:4, :], w_pb[v][:, :, cols()]).then_inc(landed[i], 16)


def decode_block(nc, sem, t, d, ps):
    k_landed = [sem(f"d_k{s}") for s in range(2)]
    v_landed = [sem(f"d_v{s}") for s in range(V_SLOTS // 4)]
    nsa_landed = [sem(f"d_nsa{s}") for s in range(2)]
    win_landed, mask_zeroed, staged_index = sem("d_win"), sem("d_mask_zeroed"), sem("d_staged_index")
    q_zeroed, q_staged, relaid, kept = sem("d_q_zeroed"), sem("d_q_staged"), sem("d_relaid"), sem("d_kept")
    tr, copied_dve, copied_act, scored, scores_taken = (sem("d_tr"), sem("d_copied_dve"), sem("d_copied_act"),
                                                        sem("d_scored"), sem("d_scores_taken"))
    ring_mm, ring_taken, small_mm, small_taken = sem("d_ring_mm"), sem("d_ring_taken"), sem("d_small_mm"), sem("d_small_taken")
    out_mm, out_taken, v_used = sem("d_out_mm"), sem("d_out_taken"), sem("d_v_used")
    max_done, exp_done, pc_ready, dve_step = sem("d_max"), sem("d_exp"), sem("d_pc"), sem("d_dve_step")
    pe_turns, pool_turns = sem("d_pe_turns"), sem("d_pool_turns")
    inv_ready, om_taken = sem("d_inv"), sem("d_om_taken")
    w1 = t["slab"][:, :, :].rearrange("p (w a) (b n) -> p w (a b) n", w=2, n=256)
    Kr, Vr, nsa, relay, vsel, XT, KTr = t["Kr"], t["Vr"], t["nsa"], t["relay"], t["vsel"], t["XT"], t["KTr"]
    Sm, Ss, Sw, Sc, PTm, PTs, PTw = t["Sm"], t["Ss"], t["Sw"], t["Sc"], t["PTm"], t["PTs"], t["PTw"]
    hid, ckT, cv, wkv, qa, qb = t["hid"], t["ckT"], t["cv"], t["wkv"], t["qa_cur"], t["qb_cur"]
    c64, ident, rows, oT = t["c64"], t["ident"], t["rows_s"], t["oT_s"]
    ident64 = ident[0:64, 0:64]
    OWN = PAST

    with nc.Block() as block:

        @block.sync
        def _(sp):
            sp.wait_ge(k_landed[0], 64)
            with sp.Fori(0, NB) as it:
                sp.wait_ge(out_mm, it * N_OUT + OPEN)
                sp.dma_start(wkv[:, :, :].rearrange("p c x -> p (c x)"),
                             d["cache_nsa_win"].rearrange("b (p c) x -> p b (c x)", c=4)[:, bass.ds(it, 1), :]
                             .rearrange("p b x -> p (b x)")).then_inc(win_landed, 16)

            sp.wait_ge(ring_mm, (NB - 1) * N_RING + R_HID_V1 + 1 + OPEN)
            for i in range(4):
                mix_slab(sp, d, t["slab"], i, 0, t["slab_landed"])

        @block.gpsimd
        def _(pool):
            def gather(dst, src, which, offset, landed):
                pool.indirect_dma_start(out=dst, out_offset=None, in_=src,
                                        in_offset=bass.IndirectOffsetOnAxis(ap=t["index_now"][:, which:which + 1], axis=0),
                                        element_offset=offset).then_inc(landed, 16)

            def gather_k(lq, which):
                for l in range(4 * lq, 4 * lq + 4):
                    gather(Kr[:, l % 8, :], d["cache_moba_kv"], which, l * 1024, k_landed[lq % 2])

            def gather_v(lq, which):
                for l in range(4 * lq, 4 * lq + 4):
                    s = l % V_SLOTS
                    gather(Vr[:, s, :], d["cache_moba_kv"], which, l * 1024 + 512, v_landed[s // 4])

            def gather_nsa(q, which):
                gather(nsa[:, q % 2, :], d["cache_nsa_kv"], which, q * 2048, nsa_landed[q % 2])

            def stage_index(which, column):
                pool.tensor_copy(t["index_now"][:, which:which + 1], t["index"][:, column]).then_inc(staged_index, 1)

            def gather_nsa_after(it, q, quarter, which):
                pool.wait_ge(kept, it * 4 + q + 1)
                pool.wait_ge(relaid, it * 8 + 2 * q + 2)
                gather_after(tr, it * NG + transposed("sel", q) + OPEN, gather_nsa, quarter, which)

            def gather_k_after(it, q, quarter, which):
                gather_after(tr, it * NG + transposed("moba", q) + OPEN, gather_k, quarter, which)

            def sequence(it, odd, more):
                for q in range(2):
                    gather_nsa_after(it, q, q + 2, odd)
                    gather_k_after(it, q, q + 2, odd)
                if more:
                    pool.wait_ge(v_used, it * 4 + OPEN)
                    stage_index(1 - odd, bass.ds(it + 1, 1))
                    pool.wait_ge(staged_index, it + 2)
                    for q in range(2, 4):
                        gather_nsa_after(it, q, q - 2, 1 - odd)
                        gather_k_after(it, q, q - 2, 1 - odd)
                gather_after(v_used, it * 4 + 1 + OPEN, gather_v, 3, odd)
                if more:
                    for q in (1, 2, 0):
                        gather_after(v_used, it * 4 + (q + 1 if q else 4) + OPEN, gather_v, q, 1 - odd)

            def gather_after(used, count, gather_quarter, q, which):
                pool.wait_ge(used, count)
                apart(pool, pool_turns)
                gather_quarter(q, which)

            stage_index(0, slice(0, 1))
            pool.wait_ge(staged_index, 1)
            for q in range(2):
                gather_nsa(q, 0)
                gather_k(q, 0)
            for q in range(3):
                gather_v(q, 0)
            with pool.Fori(0, NB - 2, 2) as it:
                sequence(it, 0, True)
                sequence(it + 1, 1, True)
            sequence(NB - 2, 0, True)
            sequence(NB - 1, 1, False)

        @block.tensor
        def _(pe):
            def transposes(it, g):
                kind, q, i = GROUPS[g]
                if g % 2 == 0:
                    pe.wait_ge(copied_dve, it * EVEN + g // 2 - (1 if g >= 4 else 0) + OPEN)
                else:
                    pe.wait_ge(copied_act, it * ODD + g // 2 - (1 if g >= 4 else 0) + OPEN)
                if g < 4:
                    pe.wait_ge(ring_taken, it * N_RING + OPEN)
                if kind == "moba":
                    if i == 0:
                        pe.wait_ge(k_landed[q % 2], it * 128 + 64 * (q // 2 + 1))
                    srcs = [Kr[:, l % 8, P * i:P * i + P] for l in range(4 * q, 4 * q + 4)]
                elif kind == "cmp":
                    pe.wait_ge(relaid, it * 8 + 2 * q + i + 1)
                    srcs = [relay[:, i, P * c:P * c + P] for c in range(4)]
                elif kind == "sel":
                    pe.wait_ge(nsa_landed[q % 2], it * 32 + 16 * (q // 2 + 1))
                    srcs = [nsa[:, q % 2, 512 * l + 256:512 * l + 384] for l in range(4)]
                else:
                    pe.wait_ge(win_landed, it * 16 + 16)
                    srcs = [wkv[:, c, 0:P] for c in range(4)]
                for n, src in enumerate(srcs):
                    last = pe.transpose(ps[T_BANKS[g % 4]][:, P * n:P * n + P], src, ident[:, :])
                last.then_inc(tr, 1)

            def score(it, g):
                kind, q, i = GROUPS[g]
                s, m = bank_of_scores(g), SCORED.index(g)
                if g % 2 == 0:
                    pe.wait_ge(copied_dve, it * EVEN + g // 2 + 1 + OPEN)
                else:
                    pe.wait_ge(copied_act, it * ODD + g // 2 + 1 + OPEN)
                if i == 0:
                    pe.wait_ge(scores_taken, it * N_SCORE + s - 1 + OPEN)
                lhsT = qa[:, 64 * i:64 * i + 64] if kind == "moba" else qb[:, :]
                pe.matmul(ps[2 + s % 2][0:64, :], lhsT, KTr[:, m % 4, :], start=i == 0,
                          stop=kind != "moba" or i == 3).then_inc(scored, 1)

            def ring_bank(it, r):
                pe.wait_ge(ring_taken, it * N_RING + r - 1 + OPEN)
                return ps[4 + r % 2]

            def prob_transposes(it, S, r):
                for n in range(2):
                    bank = ring_bank(it, r + n)
                    for i in range(8):
                        c0 = P * (8 * n + i)
                        if i == 0:
                            apart(pe, pe_turns)
                        last = pe.transpose(bank[:, 64 * i:64 * i + 64], S[:, c0:c0 + P], ident64)
                    last.then_inc(ring_mm, 1)
                bank = ring_bank(it, r + 2)
                apart(pe, pe_turns)
                pe.transpose(bank[0:64, 0:64], S[:, OWN:OWN + 64], ident64).then_inc(ring_mm, 1)

            def own_scores(it):
                pe.wait_ge(q_staged, it * 4 + 4)
                pe.wait_ge(small_taken, it * N_SMALL + OPEN)
                for hp in range(4):
                    pe.matmul(ps[7][0:64, 0:64], qa[:, 64 * hp:64 * hp + 64], t["kaT_s"][:, hp, :],
                              start=hp == 0, stop=hp == 3)
                pe.matmul(ps[7][0:64, 64:128], qb[:, :], t["ksT_s"][:, :], start=True, stop=True)
                pe.matmul(ps[7][0:64, 128:192], qb[:, :], t["kwT_s"][:, :], start=True, stop=True).then_inc(small_mm, 1)

            def sequence(it):
                for g in range(NG):
                    transposes(it, g)
                    if g == 1:
                        own_scores(it)
                    if g >= LAG and g - LAG in SCORED:
                        score(it, g - LAG)
                for g in range(NG - LAG, NG):
                    score(it, g)
                last_cmp = transposed("cmp", 3) - 1
                pe.wait_ge(copied_dve, it * EVEN + last_cmp // 2 + 1 + OPEN)
                pe.wait_ge(copied_act, it * ODD + (last_cmp + 1) // 2 + OPEN)

                def hidden(w, ht, r):
                    out = ring_bank(it, r)[:, 0:2 * NCMP]
                    compress(pe, out, w1, XT, w, ht, NCMP).then_inc(ring_mm, 1)

                hidden(0, 0, R_HID_K0)
                hidden(0, 1, R_HID_K1)
                hidden(1, 0, R_HID_V0)
                bank = ring_bank(it, R_KEYS)
                compressed_keys(pe, bank, t, hid, 0, NCMP).then_inc(ring_mm, 1)
                pe.wait_ge(ring_taken, it * N_RING + R_KEYS + 1 + OPEN)
                pe.wait_ge(small_taken, it * N_SMALL + 1 + OPEN)
                pe.matmul(ps[7][0:64, 0:NCMP], qb[:, :], ckT[:, 0:NCMP], start=True, stop=True).then_inc(small_mm, 1)
                out = ring_bank(it, R_HID_V1)[:, 0:2 * NCMP]
                compress(pe, out, w1, XT, 1, 1, NCMP, (0,))
                pe.wait_ge(pc_ready, it + 1)
                pe.wait_ge(small_taken, it * N_SMALL + 2 + OPEN)
                apart(pe, pe_turns)
                pe.matmul(ps[7][0:64, 0:NCMP], c64[:, C_GSUM:C_GSUM + 64], Sc[:, 0:NCMP], start=True, stop=True)\
                  .then_inc(small_mm, 1)
                compress(pe, out, w1, XT, 1, 1, NCMP, (1,)).then_inc(ring_mm, 1)
                pe.wait_ge(ring_taken, it * N_RING + R_HID_V1 + 1 + OPEN)
                compressed_values(pe, ps[4 + R_VALUES % 2], t, hid, 0, NCMP).then_inc(ring_mm, 1)
                pe.wait_ge(exp_done, it * 4 + E_MOBA + 1)
                prob_transposes(it, Sm, R_PTM)
                pe.wait_ge(out_taken, it * 2 + OPEN)
                for l in range(SEG):
                    if l % 8 == 0:
                        pe.wait_ge(ring_taken, it * N_RING + R_PTM + 1 + l // 8 + OPEN)
                    vs = l % V_SLOTS
                    if l % 4 == 0:
                        pe.wait_ge(v_landed[vs // 4], it * (64 if vs else 128) + 64 * (l // V_SLOTS + 1))
                    last = pe.matmul(ps[6][0:64, :], PTm[:, l, :], Vr[:, vs, :], start=l == 0, stop=False)
                    if l % 4 == 3:
                        last.then_inc(v_used, 1)
                pe.wait_ge(ring_taken, it * N_RING + 9 + OPEN)
                apart(pe, pe_turns)
                pe.matmul(ps[6][0:64, :], PTm[0:64, SEG, :], rows[:, RVA:RVA + 512], start=False, stop=True)\
                  .then_inc(out_mm, 1)
                pe.wait_ge(exp_done, it * 4 + E_WIN + 1)
                bank = ring_bank(it, R_PTW)
                apart(pe, pe_turns)
                pe.transpose(bank[0:NCMP, 0:64], Sc[:, 0:NCMP], ident64)
                for c in range(4):
                    pe.transpose(bank[:, 64 * (1 + c):64 * (2 + c)], Sw[:, P * c:P * c + P], ident64)
                pe.transpose(bank[0:64, 320:384], Sw[:, WIN:WIN + 64], ident64).then_inc(ring_mm, 1)
                pe.wait_ge(ring_taken, it * N_RING + 10 + OPEN)
                pe.wait_ge(om_taken, it + 1)
                pe.matmul(ps[6][0:64, 0:P], PTw[0:NCMP, 0, :], cv[0:NCMP, :], start=True, stop=True)
                for c in range(4):
                    pe.matmul(ps[6][0:64, P:2 * P], PTw[:, 1 + c, :], wkv[:, c, P:2 * P], start=c == 0, stop=False)
                pe.matmul(ps[6][0:64, P:2 * P], PTw[0:64, 5, :], rows[:, RVW:RVW + P], start=False, stop=True)\
                  .then_inc(out_mm, 1)
                pe.wait_ge(exp_done, it * 4 + E_SEL + 1)
                prob_transposes(it, Ss, R_PTS)
                pe.wait_ge(out_taken, it * 2 + 1 + OPEN)
                pe.wait_ge(kept, it * 4 + 4)
                for l in range(SEG):
                    if l % 8 == 0:
                        pe.wait_ge(ring_taken, it * N_RING + 11 + l // 8 + OPEN)
                    pe.matmul(ps[6][0:64, 0:P], PTs[:, l, :], vsel[:, l, :], start=l == 0, stop=False)
                pe.wait_ge(ring_taken, it * N_RING + 13 + OPEN)
                apart(pe, pe_turns)
                pe.matmul(ps[6][0:64, 0:P], PTs[0:64, SEG, :], rows[:, RVS:RVS + P], start=False, stop=True)\
                  .then_inc(out_mm, 1)
                pe.wait_ge(out_taken, it * 2 + 2 + OPEN)
                pe.wait_ge(small_taken, it * N_SMALL + 3 + OPEN)
                apart(pe, pe_turns)
                for n in range(4):
                    pe.transpose(ps[7][:, 64 * n:64 * n + 64], t["Om"][:, P * n:P * n + P], ident64)
                for n in range(3):
                    last = pe.transpose(ps[7][:, 256 + 64 * n:320 + 64 * n], t["On"][:, n, :], ident64)
                last.then_inc(small_mm, 1)

            for nothing_yet in (tr, scored, ring_mm, out_mm, v_used):
                pe.sem_inc(nothing_yet, OPEN)
            with pe.Fori(0, NB) as it:
                sequence(it)

        def group_copy(eng, copy, it, g, done):
            kind, q, i = GROUPS[g]
            eng.wait_ge(tr, it * NG + g + 1 + OPEN)
            if kind == "cmp":
                eng.wait_ge(ring_mm, it * N_RING + OPEN)
                dst = XT[:, :, :, 2 * q + i, :].rearrange("p w v s -> p (w v) s")
                copy(dst, ps[T_BANKS[g % 4]][:, :].rearrange("p (c s) -> p c s", c=4)).then_inc(done, 1)
            else:
                m = SCORED.index(g)
                eng.wait_ge(scored, it * NM + m - 3 + OPEN)
                copy(KTr[:, m % 4, :], ps[T_BANKS[g % 4]][:, :]).then_inc(done, 1)

        @block.scalar
        def _(act):
            def copy(dst, src):
                return act.activation(dst, src, ACT.Copy)

            def stage_queries(b):
                cols = bass.ds(b * T, T) if not isinstance(b, int) else slice(b * T, b * T + T)
                for half in range(2):
                    rows64 = slice(DH * half, DH * half + DH)
                    copy(qa[rows64, 8 * half:8 * half + 320].rearrange("p (g c) -> p g c", c=80)[:, :, 0:T],
                         t["qaT_s"][rows64, :, cols]).then_inc(q_staged, 1)
                    copy(qb[rows64, 32 * half:32 * half + 32].rearrange("p (g c) -> p g c", c=T),
                         t["qbT_s"][rows64, :, cols]).then_inc(q_staged, 1)

            def exp(it, which, S, n):
                act.wait_ge(max_done, it * 4 + which + 1)
                act.activation(S[:, 0:n], S[:, 0:n], ACT.Exp, bias=t["nmax"][:, which:which + 1],
                               accum_out=t["sums"][:, which:which + 1]).then_inc(exp_done, 1)

            def prob_copies(it, PT, r):
                for n in range(2):
                    act.wait_ge(ring_mm, it * N_RING + r + n + 1 + OPEN)
                    copy(PT[:, 8 * n:8 * n + 8, :].rearrange("p l r -> p (l r)"), ps[4 + (r + n) % 2][:, :])\
                        .then_inc(ring_taken, 1)
                act.wait_ge(ring_mm, it * N_RING + r + 3 + OPEN)
                copy(PT[0:64, SEG, :], ps[4 + r % 2][0:64, 0:64]).then_inc(ring_taken, 1)

            def relay_quarter(it, q):
                act.wait_ge(nsa_landed[q % 2], it * 32 + 16 * (q // 2 + 1))
                act.wait_ge(tr, it * NG + (transposed("cmp", q - 1) if q else 0) + OPEN)
                src = nsa[:, q % 2, :].rearrange("p (a b x) -> p a b x", a=2, b=2)
                for a in range(2):
                    copy(relay[:, a, :].rearrange("p (c b e) -> p c b e", c=4, b=2),
                         src[:, a, :, 0:256].rearrange("p b (c e) -> p c b e", c=4)).then_inc(relaid, 1)
                if q == 0:
                    act.wait_ge(out_mm, it * N_OUT + OPEN)
                copy(vsel[:, 4 * q:4 * q + 4, :],
                     nsa[:, q % 2, :].rearrange("p (l x) -> p l x", l=4)[:, :, 384:512]).then_inc(kept, 1)

            act.sem_inc(copied_act, OPEN)
            act.sem_inc(ring_taken, OPEN)
            act.wait_ge(q_zeroed, 2)
            stage_queries(0)
            with act.Fori(0, NB) as it:
                relay_quarter(it, 0)
                for g in range(1, NG, 2):
                    group_copy(act, copy, it, g, copied_act)
                    for q in range(1, 4):
                        if g in (transposed("cmp", q - 1) + 1, transposed("cmp", q - 1) + 2):
                            relay_quarter(it, q)
                exp(it, E_MOBA, Sm, PAST + 64)
                exp(it, E_WIN, Sw, WIN + 64)

                def gelu(w, ht, r):
                    act.wait_ge(ring_mm, it * N_RING + r + 1 + OPEN)
                    act.activation(hid[:, w, ht, :], ps[4 + r % 2][:, 0:2 * NCMP], ACT.Gelu_apprx_tanh,
                                   bias=t["hbias"][:, 2 * w + ht:2 * w + ht + 1]).then_inc(ring_taken, 1)

                gelu(0, 0, R_HID_K0)
                gelu(0, 1, R_HID_K1)
                gelu(1, 0, R_HID_V0)
                act.wait_ge(ring_mm, it * N_RING + R_KEYS + 1 + OPEN)
                act.activation(ckT[:, 0:NCMP], ps[4 + R_KEYS % 2][:, 0:NCMP], ACT.Identity,
                               bias=t["vecT"][:, V_B2:V_B2 + 1]).then_inc(ring_taken, 1)
                exp(it, E_CMP, Sc, NCMP)
                gelu(1, 1, R_HID_V1)
                act.wait_ge(ring_mm, it * N_RING + R_VALUES + 1 + OPEN)
                copy(cv[0:NCMP, :], ps[4 + R_VALUES % 2][0:NCMP, 0:P]).then_inc(ring_taken, 1)
                prob_copies(it, PTm, R_PTM)
                exp(it, E_SEL, Ss, PAST + 64)
                act.wait_ge(inv_ready, it + 1)
                act.wait_ge(out_mm, it * N_OUT + 1 + OPEN)
                act.activation(t["Om"][:, :], ps[6][0:64, :], ACT.Copy, scale=t["inv"][:, E_MOBA:E_MOBA + 1])\
                   .then_inc(om_taken, 1)
                act.wait_ge(ring_mm, it * N_RING + R_PTW + 1 + OPEN)
                copy(PTw[0:NCMP, 0, :], ps[5][0:NCMP, 0:64])
                copy(PTw[:, 1:5, :].rearrange("p c r -> p (c r)"), ps[5][:, 64:320])
                copy(PTw[0:64, 5, :], ps[5][0:64, 320:384]).then_inc(ring_taken, 1)
                prob_copies(it, PTs, R_PTS)
                act.wait_ge(small_mm, it * N_SMALL + 2)
                stage_queries(it + 1)

        @block.vector
        def _(dve):
            def ranks(steps, value, n, above, equal, tie, rank):
                one = value.unsqueeze(1).to_broadcast([64, n, n])
                other = value.unsqueeze(2).to_broadcast([64, n, n])
                steps.do(dve.tensor_tensor(above, one, other, ALU.is_gt))
                steps.do(dve.tensor_tensor(equal, one, other, ALU.is_equal))
                steps.do(dve.tensor_tensor(equal, equal, tie.rearrange("p (j i) -> p j i", i=n), ALU.mult))
                steps.do(dve.tensor_tensor(above, above, equal, ALU.add))
                steps.do(dve.tensor_reduce(rank, above, AX.X, ALU.add))

            def take_scores(it, s):
                bank = ps[2 + s % 2][0:64, :]
                dve.wait_ge(scored, it * NM + SCORED.index(last_group(s)) + 1 + OPEN)
                q = s // 2
                c0 = 512 * q
                if s == 8:
                    dst, bias = Sw[:, 0:WIN], c64[:, C_BWIN:C_BWIN + WIN]
                elif s % 2:
                    dve.tensor_reduce(t["gates4"][:, :, q], bank.rearrange("p (l n s) -> p n l s", l=4, n=NMB),
                                      AX.XY, ALU.add)
                    dst, bias = Sm[:, c0:c0 + 512], c64[:, C_BDEC + c0:C_BDEC + c0 + 512]
                else:
                    dst, bias = Ss[:, c0:c0 + 512], c64[:, C_BDEC + c0:C_BDEC + c0 + 512]
                dve.scalar_tensor_tensor(dst, bank, SCALE, bias, ALU.mult, ALU.add).then_inc(scores_taken, 1)

            def row_max(which, S, n):
                dve.tensor_reduce(t["nmax"][:, which:which + 1], S[:, 0:n], AX.X, ALU.max, negate=True)\
                   .then_inc(max_done, 1)

            def inverse(it, steps, which):
                dve.wait_ge(exp_done, it * 4 + which + 1)
                steps.do(dve.reciprocal(t["inv"][:, which:which + 1], t["sums"][:, which:which + 1]))

            for nothing_yet in (copied_dve, scores_taken, small_taken, out_taken):
                dve.sem_inc(nothing_yet, OPEN)
            dve.memset(qa[:, :], 0.0).then_inc(q_zeroed, 1)
            dve.memset(qb[:, :], 0.0).then_inc(q_zeroed, 1)
            dve.memset(t["sel_mask"][:, :], 0.0).then_inc(mask_zeroed, 1)
            dve.wait_ge(mask_zeroed, 1)
            with dve.Fori(0, NB) as it:
                steps = Steps(dve, dve_step, it * DVE_STEPS)
                after = {min((last_group(s) + LAG) // 2 * 2, NG - 1): s for s in range(8)}
                for g in range(0, NG, 2):
                    group_copy(dve, dve.tensor_copy, it, g, copied_dve)
                    if g == 0:
                        dve.wait_ge(small_mm, it * N_SMALL + 1)
                        own = c64[:, C_BOWN:C_BOWN + 512].rearrange("p (b u) -> p b u", u=64)[:, bass.ds(it, 1), :]\
                            .rearrange("p b u -> p (b u)")
                        for n, dst in enumerate([Sm[:, OWN:OWN + 64], Ss[:, OWN:OWN + 64], Sw[:, WIN:WIN + 64]]):
                            last = dve.scalar_tensor_tensor(dst, ps[7][0:64, 64 * n:64 * n + 64], SCALE, own, ALU.mult, ALU.add)
                        last.then_inc(small_taken, 1)
                    if g in after:
                        take_scores(it, after[g])
                take_scores(it, 8)
                dve.wait_ge(scores_taken, it * N_SCORE + 9 + OPEN)
                steps.do(dve.tensor_reduce(t["gate"][:, :], t["gates4"][:, :, :], AX.X, ALU.add))
                ranks(steps, t["gate"][:, :], NMB, t["above8"][:, :, :], t["equal8"][:, :, :],
                      c64[:, C_TIE8:C64W], t["rank"][:, 0:NMB])
                steps.do(dve.tensor_scalar(t["mb_mask"][:, :], t["rank"][:, 0:NMB], float(MTOP), NEG, ALU.is_ge, ALU.mult))
                s4 = Sm[:, 0:PAST].rearrange("p (l n s) -> p l n s", l=SEG, n=NMB)
                steps.do(dve.tensor_tensor(s4, s4, t["mb_mask"][:, :].unsqueeze(1).unsqueeze(3)
                                           .to_broadcast([64, SEG, NMB, SEG]), ALU.add))
                row_max(E_MOBA, Sm, PAST + 64)
                row_max(E_WIN, Sw, WIN + 64)
                dve.wait_ge(small_mm, it * N_SMALL + 2)
                dve.tensor_scalar(Sc[:, 0:NCMP], ps[7][0:64, 0:NCMP], SCALE, None, ALU.mult).then_inc(small_taken, 1)
                dve.wait_ge(small_taken, it * N_SMALL + 2 + OPEN)
                row_max(E_CMP, Sc, NCMP)
                inverse(it, steps, E_CMP)
                dve.tensor_scalar(Sc[:, 0:NCMP], Sc[:, 0:NCMP], t["inv"][:, E_CMP:E_CMP + 1], None, ALU.mult)\
                   .then_inc(pc_ready, 1)
                inverse(it, steps, E_MOBA)
                dve.reciprocal(t["inv"][:, E_WIN:E_WIN + 1], t["sums"][:, E_WIN:E_WIN + 1]).then_inc(inv_ready, 1)
                dve.wait_ge(small_mm, it * N_SMALL + 3)
                steps.do(dve.tensor_reduce(t["imp"][:, :], ps[7][0:64, 4:4 + 4 * CAND].rearrange("p (j n) -> p j n", n=4),
                                           AX.X, ALU.add))
                dve.tensor_tensor(t["imp"][:, :], t["imp"][:, :], ps[7][0:64, 3:3 + 4 * CAND:4], ALU.add)\
                   .then_inc(small_taken, 1)
                dve.wait_ge(small_taken, it * N_SMALL + 3 + OPEN)
                above, equal = [KTr[0:64, c:c + 2, :].rearrange("p a b -> p (a b)")[:, 0:CAND * CAND]
                                .rearrange("p (j i) -> p j i", i=CAND) for c in (0, 2)]
                ranks(steps, t["imp"][:, :], CAND, above, equal,
                      c64[:, C_TIE:C_TIE8], t["rank"][:, :])
                steps.do(dve.tensor_scalar(t["sel_mask"][:, 1:1 + CAND], t["rank"][:, :], float(STOP), NEG,
                                           ALU.is_ge, ALU.mult))
                s4 = Ss[:, 0:PAST].rearrange("p (l j s) -> p l j s", l=SEG, j=NSB)
                steps.do(dve.tensor_tensor(s4, s4, t["sel_mask"][:, :].unsqueeze(1).unsqueeze(3)
                                           .to_broadcast([64, SEG, NSB, 4]), ALU.add))
                row_max(E_SEL, Ss, PAST + 64)
                dve.wait_ge(inv_ready, it + 1)
                dve.wait_ge(out_mm, it * N_OUT + 2 + OPEN)
                dve.tensor_copy(t["On"][:, 0, :], ps[6][0:64, 0:P])
                dve.tensor_scalar(t["On"][:, 2, :], ps[6][0:64, P:2 * P], t["inv"][:, E_WIN:E_WIN + 1], None, ALU.mult)\
                   .then_inc(out_taken, 1)
                inverse(it, steps, E_SEL)
                dve.wait_ge(out_mm, it * N_OUT + 3 + OPEN)
                dve.tensor_scalar(t["On"][:, 1, :], ps[6][0:64, 0:P], t["inv"][:, E_SEL:E_SEL + 1], None, ALU.mult)\
                   .then_inc(out_taken, 1)
                dve.wait_ge(small_mm, it * N_SMALL + 4)
                for half in range(2):
                    rows64 = slice(DH * half, DH * half + DH)
                    dve.tensor_copy(oT[rows64, BR_MOBA, :, bass.ds(it * T, T)],
                                    ps[7][rows64, 8 * half:8 * half + 320].rearrange("p (g c) -> p g c", c=80)[:, :, 0:T])
                    last = dve.tensor_copy(oT[rows64, BR_CMP:, :, bass.ds(it * T, T)],
                                           ps[7][rows64, 256:448].rearrange("p (c v g t) -> p c v g t", c=3, v=KV, g=G)
                                           [:, :, half, :, :])
                last.then_inc(small_taken, 1)
                assert steps.n == DVE_STEPS, steps.n
            dve.wait_ge(small_taken, NB * N_SMALL + OPEN)


def square_norm(pe, ones, sq, bank, sq_done, first, ss_mm, order=range(KT)):
    for i, k in enumerate(order):
        pe.wait_ge(sq_done, first + i + 1)
        last = pe.matmul(bank[:, 0:TOK], ones[:, :], sq[:, k, :], start=i == 0, stop=i == KT - 1)
    last.then_inc(ss_mm, 1)


def back_block(nc, sem, t, d, ps):
    slab_landed = t["slab_landed"]
    w_high, w_split, sp_turns = sem("b_w_high"), sem("b_w_split"), sem("b_sp_turns")
    u_back, x_back, o_back, exp_landed, o_whole = ([sem(f"b_u_back{n}") for n in range(2)], sem("b_x_back"), sem("b_o_back"), sem("b_expand"),
                                                   sem("b_o_whole"))
    u_high, u_split, o_split, ge_mm, ge_taken, ob_done = (sem("b_u_high"), sem("b_u_split"), sem("b_o_split"),
                                                          sem("b_ge_mm"), sem("b_ge"), sem("b_ob"))
    gate_mm, gate_done, y_mm, z_part, z_step, z_done = (sem("b_gate_mm"), sem("b_gate"), sem("b_y_mm"),
                                                        sem("b_z_part"), sem("b_z_step"), sem("b_z"))
    mix_mm, x_done = sem("b_mix_mm"), sem("b_x")
    sq_done, ss_mm, root_done = sem("b_sq"), sem("b_ss_mm"), sem("b_root")
    h_pre, h_mid, h_done, h_high, h_split = (sem("b_h_pre"), sem("b_h_mid"), sem("b_h"), sem("b_h_high"),
                                             sem("b_h_split"))
    a_mm, b_mm, silu_done, f_step, f_done = sem("b_a_mm"), sem("b_b_mm"), sem("b_silu"), sem("b_f_step"), sem("b_f")
    last_mm = sem("b_last_mm")
    down_mm, y_done, y_tr, y_act, y_dve, dve_step, stored = (sem("b_down_mm"), sem("b_y"), sem("b_y_tr"), sem("b_y_act"),
                                                             sem("b_y_dve"), sem("b_dve_step"), sem("b_stored"))
    slab, slabH, slabL, xT, uT, uH = t["slab"], t["slabH"], t["slabL"], t["xT"], t["uT"], t["uH"]
    ex = xT[0:24, :, :].rearrange("p k n -> p (k n)")[:, 0:12 * P]
    uL, sq, gn, gates, prod = t["uL"], t["sq"], t["gn"], t["gates"], t["prod"]
    oT, oH, oL, bH, bL, zH, zL, GH, GL, yn = (t["oT"], t["oH"], t["oL"], t["bH"], t["bL"], t["zH"], t["zL"],
                                              t["GH"], t["GL"], t["yn"])
    mod, ident = t["mod"], t["ident"]
    N_OUT, N_GU, N_DOWN, N_END = 16, 20, 42, 53
    HALF = 1024
    GE_BANKS = (2, 3, 6, 7)

    with nc.Block() as block:

        @block.sync
        def _(sp):
            def load(n, it, dst, src):
                sp.wait_ge(w_split, it * 4 + n - 3 + OPEN)
                apart(sp, sp_turns)
                sp.dma_start(dst, src).then_inc(slab_landed[n % SLOTS], 16)

            def in_tiles(n, k, values=SLABW):
                return slab[:, n % SLOTS, 0:values].rearrange("p (k n) -> p k n", k=k)

            for n in range(2):
                sp.dma_start(uT[:, 4 * n:4 * n + 4, :].rearrange("p k n -> p (k n)"),
                             d["spill_u"][:, 4 * n * TOK:(4 * n + 4) * TOK]).then_inc(u_back[n], 16)
            sp.dma_start(ex, d["c_expand"]).then_inc(exp_landed, 16)
            for br in range(4):
                sp.dma_start(oT[:, br, :, 0:SEQ],
                             d["spill_o"][:, br * 4 * SEQ:(br + 1) * 4 * SEQ].rearrange("p (g t) -> p g t", g=4))\
                    .then_inc(o_back, 16)
            with sp.Fori(1, 4) as it:
                for i in range(4):
                    sp.wait_ge(w_split, it * 4 + i - 3 + OPEN)
                    apart(sp, sp_turns)
                    mix_slab(sp, d, slab, i, it, slab_landed)
            sp.wait_ge(ge_mm, 12)
            sp.dma_start(xT[:, :, :].rearrange("p k n -> p (k n)"), d["spill_x"]).then_inc(x_back, 16)
            w_out = d["w_out"].rearrange("(k p) n -> p k n", p=P)
            for i in range(4):
                load(N_OUT + i, 0, in_tiles(i, KT), w_out[:, :, 256 * i:256 * i + 256])
            w_gu = d["w_gu"].rearrange("(k p) n -> p k n", p=P)
            with sp.Fori(0, 5) as it:
                for i in range(4):
                    load(N_GU + i, it, in_tiles(i, KT),
                         w_gu[:, :, bass.ds(it * 512 + 256 * (i // 2) + FF * (i % 2), 256)])
            for i in range(2):
                load(N_GU + 20 + i, 0, in_tiles(i, KT), w_gu[:, :, 2560 + FF * i:2816 + FF * i])
            w_down = d["w_down"].rearrange("(f p) n -> p f n", p=P)
            with sp.Fori(0, 2) as it:
                for i in range(4):
                    load(N_DOWN + i, it, in_tiles(N_DOWN + i, 2), w_down[:, bass.ds(it * 8 + 2 * i, 2), :])
            for i in range(8, 11):
                load(N_DOWN + i, 0, in_tiles(N_DOWN + i, 2), w_down[:, 2 * i:2 * i + 2, :])
            for i, (t0, n) in enumerate(T_TILES):
                sp.wait_ge(y_act, i + 1)
                sp.wait_ge(y_dve, i + 1)
                dst = d["y_sample"] if i == 2 else d["y_prompt"][t0:t0 + n, :]
                sp.dma_start(dst, yn[0:n, i, :]).then_inc(stored, 16)
            sp.wait_ge(stored, 48)

        @block.gpsimd
        def _(pool):
            def low_part(n, it, values=SLABW):
                s = n % SLOTS
                pool.wait_ge(w_high, it * 4 + n + 1)
                pool.tensor_tensor(slabL[:, s, 0:values], slab[:, s, 0:values], slabH[:, s, 0:values].bitcast(F32),
                                   ALU.subtract).then_inc(w_split, 1)

            pool.sem_inc(w_split, OPEN)
            for br in range(4):
                pool.tensor_copy(oT[:, br, :, SEQ:TOK], t["oT_s"][:, br, :, :]).then_inc(o_whole, 1)
            with pool.Fori(0, 4) as it:
                for i in range(4):
                    low_part(i, it, SLABW if i < 2 else HALF)
            with pool.Fori(4, N_END // 4) as it:
                for i in range(4):
                    low_part(i, it)
            for n in range(N_END // 4 * 4, N_END):
                low_part(n, 0)

        @block.tensor
        def _(pe):
            def split(n, it=0):
                pe.wait_ge(w_split, it * 4 + n + 1 + OPEN)

            def weights(n, c0):
                return slabH[:, n % SLOTS, c0:c0 + P], slabL[:, n % SLOTS, c0:c0 + P]

            for nothing_yet in (gate_mm, y_mm, a_mm, b_mm):
                pe.sem_inc(nothing_yet, OPEN)

            def mix(i, it):
                split(i, it)
                for m in range(2):
                    bank = ps[4 * m + i]
                    if i < 2:
                        pe.wait_ge(gate_done, it * 4 + 2 * i + m - 3 + OPEN)
                    else:
                        pe.wait_ge(z_part, it * 4 + 2 * m + (i - 2) - 3 + OPEN)
                    if i == 2:
                        pe.wait_ge(o_split, 1)
                    if i == 3:
                        pe.wait_ge(ob_done, 1)
                    for k in range(KT if i < 2 else 4):
                        if i == m == 0 and k % 4 == 0:
                            pe.wait_ge(u_split, k // 4 + 1)
                        high, low = {0: (uH, uL), 1: (uH, uL), 2: (oH, oL), 3: (bH, bL)}[i]
                        last = split_matmul(pe, bank[:, 0:TOK], *weights(i, 256 * k + P * m), high[:, k, :],
                                            low[:, k, :], k == 0, k == (KT if i < 2 else 4) - 1)
                    last.then_inc(gate_mm if i < 2 else y_mm, 1)

            mix(0, 0)
            mix(1, 0)
            pe.wait_ge(exp_landed, 16)
            for n in range(12):
                c, g = n // 4, n % 4
                if n >= 4:
                    pe.wait_ge(ge_taken, n - 3)
                pe.matmul(ps[GE_BANKS[n % 4]][:, 0:TOK], ex[:, (c * 4 + g) * P:(c * 4 + g) * P + P], gn[:, :],
                          start=True, stop=True).then_inc(ge_mm, 1)
            mix(2, 0)
            mix(3, 0)
            with pe.Fori(1, 4) as it:
                for i in range(4):
                    mix(i, it)
            pe.wait_ge(gate_done, 16 + OPEN)
            for m in range(KT):
                n = N_OUT + m // 2
                if m % 2 == 0:
                    split(n)
                if m >= 2:
                    pe.wait_ge(x_done, m - 1)
                for k in range(KT):
                    if m == 0:
                        pe.wait_ge(z_done, k + 1 + OPEN)
                    last = split_matmul(pe, ps[m % 2][:, 0:TOK], *weights(n, 256 * k + P * (m % 2)), zH[:, k, :],
                                        zL[:, k, :], k == 0, k == KT - 1)
                last.then_inc(mix_mm, 1)
            square_norm(pe, t["ones"], sq, ps[7], sq_done, 0, ss_mm)

            def up(it, group):
                for f in range(2):
                    pe.wait_ge(f_done, it * 4 + 2 * group + f - 3 + OPEN)
                    for half in range(2):
                        n = N_GU + 2 * group + half
                        if f == 0:
                            split(n, it)
                        bank = ps[4 * group + 2 * f + half]
                        for k in range(KT):
                            if group == f == half == 0:
                                pe.wait_ge(h_split, k + 1)
                            last = split_matmul(pe, bank[:, 0:TOK], *weights(n, 256 * k + P * f), uH[:, k, :],
                                                uL[:, k, :], k == 0, k == KT - 1)
                        last.then_inc(b_mm if half else a_mm, 1)

            with pe.Fori(0, 5) as it:
                for group in range(2):
                    up(it, group)
            up(5, 0)

            def down(n, it, tile, first=False, final=False):
                split(n, it)
                for f in range(2):
                    for m in (4, 5, 6, 7, 0, 1, 2, 3):
                        if first and f == 0 and m % 4 == 0:
                            pe.wait_ge(f_done, (FT - 2 if m else FT) + OPEN)
                        high, low = [g[:, tile + f, :] if isinstance(tile, int) else
                                     g[:, bass.ds(tile + f, 1), :].rearrange("p a b -> p (a b)") for g in (GH, GL)]
                        last = split_matmul(pe, ps[m][:, 0:TOK], *weights(n, D * f + P * m), high, low,
                                            first and f == 0, final and f == 1, skip_group_check=True)
                        if final and f == 1:
                            last.then_inc(last_mm, 1)
                if not final:
                    last.then_inc(down_mm, 1)

            down(N_DOWN, 0, 0, first=True)
            with pe.Fori(0, 2) as it:
                for i in range(4):
                    down(N_DOWN + 1 + i, it, it * 8 + 2 + 2 * i)
            down(N_DOWN + 9, 0, 18)
            down(N_DOWN + 10, 0, 20, final=True)
            pe.wait_ge(x_done, KT + 4)
            square_norm(pe, t["ones"], sq, ps[7], sq_done, KT, ss_mm, (4, 5, 6, 7, 0, 1, 2, 3))
            for j in range(6):
                i, half = j // 2, j % 2
                pe.wait_ge(y_done, 4 * half + 4)
                t0, n = T_TILES[i]
                if j >= 2:
                    pe.wait_ge(y_dve if half else y_act, i)
                for k in range(4):
                    last = pe.transpose(ps[half][0:n, P * k:P * k + P], uT[:, 4 * half + k, t0:t0 + n], ident[:, :])
                last.then_inc(y_tr, 1)

        @block.scalar
        def _(act):
            def high_part(n, it, used, count, values=SLABW):
                s = n % SLOTS
                act.wait_ge(used, count)
                per = 32 if values == HALF and s == 3 else 16
                before = 16 * 4 if values == SLABW and s == 3 else 0
                act.wait_ge(slab_landed[s], it * per + per * (n // SLOTS + 1) + before)
                act.activation(slabH[:, s, 0:values], slab[:, s, 0:values], ACT.Copy).then_inc(w_high, 1)

            def high_mix(i, it):
                high_part(i, it, gate_mm if i < 2 else y_mm, it * 4 + 2 * (i % 2) - 2 + OPEN, SLABW if i < 2 else HALF)

            def high_out(i):
                high_part(N_OUT + i, 0, gate_mm if i < 2 else y_mm, 14 + 2 * (i % 2) + OPEN)

            def high_gu(i, it):
                act.wait_ge(mix_mm, 2 * i + 2)
                high_part(N_GU + i, it, b_mm if i % 2 else a_mm, it * 4 + 2 * (i // 2) - 2 + OPEN)

            def square(n, k, i):
                act.wait_ge(x_done, (n - 1) * KT + i + 1)
                act.activation(sq[:, k, :], xT[:, k, :], ACT.Square).then_inc(sq_done, 1)

            def root(n):
                act.wait_ge(ss_mm, n)
                act.activation(t["root"][:, :], ps[7][:, 0:TOK], ACT.Sqrt, bias=t["eps"][:, 0:1], scale=1.0 / D)\
                   .then_inc(root_done, 1)

            def sigmoids(i, it):
                for m in range(2):
                    act.wait_ge(z_done, it * 2 + m - 1 + OPEN)
                    act.wait_ge(gate_mm, it * 4 + 2 * i + m + 1 + OPEN)
                    act.activation(gates[:, m, i, :], ps[4 * m + i][:, 0:TOK], ACT.Sigmoid).then_inc(gate_done, 1)

            act.sem_inc(gate_done, OPEN)
            high_mix(0, 0)
            for n in range(2):
                act.wait_ge(u_back[n], 16)
                act.activation(uH[:, 4 * n:4 * n + 4, :], uT[:, 4 * n:4 * n + 4, :], ACT.Copy).then_inc(u_high, 1)
            for i in range(1, 4):
                high_mix(i, 0)
            act.wait_ge(o_whole, 4)
            with act.Fori(0, 3) as it:
                for i in range(4):
                    high_mix(i, it + 1)
                    if i < 2:
                        sigmoids(i, it)
            for i in range(4):
                high_out(i)
                if i < 2:
                    sigmoids(i, 3)
            for i in range(2):
                high_gu(i, 0)
            act.activation(t["warm"][:, :], t["eps"][:, 0:1], ACT.Sqrt)
            for k in range(KT):
                square(1, k, k)
            root(1)
            for k in range(KT):
                act.wait_ge(h_done, k + 1)
                act.activation(uH[:, k, :], uT[:, k, :], ACT.Copy).then_inc(h_high, 1)

            def silu(f, it):
                act.wait_ge(f_done, it * 4 + f - 3 + OPEN)
                act.wait_ge(a_mm, it * 4 + f + 1 + OPEN)
                act.activation(gates[:, f % 4 // 2, f % 2, :], ps[2 * (f % 4)][:, 0:TOK], ACT.Silu).then_inc(silu_done, 1)

            with act.Fori(0, 5) as it:
                high_gu(2, it)
                high_gu(3, it)
                silu(0, it)
                silu(1, it)
                high_gu(0, it + 1)
                high_gu(1, it + 1)
                silu(2, it)
                silu(3, it)
            high_part(N_DOWN, 0, a_mm, 20 + OPEN)
            high_part(N_DOWN + 1, 0, b_mm, 20 + OPEN)
            silu(20, 0)
            silu(21, 0)
            high_part(N_DOWN + 2, 0, a_mm, 22 + OPEN)
            high_part(N_DOWN + 3, 0, b_mm, 22 + OPEN)
            for i in range(4, 11):
                high_part(N_DOWN + i, 0, down_mm, i - 3)
            act.activation(t["warm"][:, :], t["eps"][:, 0:1], ACT.Sqrt)
            for i, k in enumerate((4, 5, 6, 7, 0, 1, 2, 3)):
                square(2, k, i)
            root(2)
            for i, (t0, n) in enumerate(T_TILES):
                act.wait_ge(y_tr, 2 * i + 1)
                act.activation(yn[0:n, i, 0:512], ps[0][0:n, :], ACT.Copy).then_inc(y_act, 1)

        @block.vector
        def _(dve):
            steps = Steps(dve, dve_step)
            for nothing_yet in (z_part, z_done, f_done):
                dve.sem_inc(nothing_yet, OPEN)
            for n in range(2):
                dve.wait_ge(u_high, n + 1)
                half = slice(4 * n, 4 * n + 4)
                dve.tensor_tensor(uL[:, half, :], uT[:, half, :], uH[:, half, :], ALU.subtract).then_inc(u_split, 1)
            dve.wait_ge(o_back, 64)
            dve.wait_ge(o_whole, 4)
            for n in range(12):
                c, g = n // 4, n % 4
                dve.wait_ge(ge_mm, n + 1)
                dve.tensor_tensor(oT[:, 1 + c, g, :], oT[:, 1 + c, g, :], ps[GE_BANKS[n % 4]][:, 0:TOK],
                                  ALU.mult)\
                   .then_inc(ge_taken, 1)
            dve.wait_ge(ge_taken, 12)
            steps.do(dve.tensor_copy(oH[:, :, :], oT[:, 0, :, :]))
            dve.tensor_tensor(oL[:, :, :], oT[:, 0, :, :], oH[:, :, :], ALU.subtract).then_inc(o_split, 1)
            steps.do(dve.tensor_tensor(oT[:, 1, :, :], oT[:, 1, :, :], oT[:, 2, :, :], ALU.add))
            steps.do(dve.tensor_tensor(oT[:, 1, :, :], oT[:, 1, :, :], oT[:, 3, :, :], ALU.add))
            steps.do(dve.tensor_copy(bH[:, :, :], oT[:, 1, :, :]))
            dve.tensor_tensor(bL[:, :, :], oT[:, 1, :, :], bH[:, :, :], ALU.subtract).then_inc(ob_done, 1)

            def tile(x, n):
                return x[:, n, :] if isinstance(n, int) else x[:, bass.ds(n, 1), :].rearrange("p a b -> p (a b)")

            with dve.Fori(0, 4) as it:
                for m in range(2):
                    dve.wait_ge(z_done, it * 2 + m + OPEN)
                    for i in range(2):
                        dve.wait_ge(gate_done, it * 4 + 2 * i + m + 1 + OPEN)
                        dve.wait_ge(y_mm, it * 4 + 2 * i + m + 1 + OPEN)
                        dve.tensor_tensor(prod[:, i, :], gates[:, m, i, :], ps[4 * m + 2 + i][:, 0:TOK], ALU.mult)\
                           .then_inc(z_part, 1)
                    dve.wait_ge(z_part, it * 4 + 2 * m + 2 + OPEN)
                    dve.tensor_tensor(prod[:, 0, :], prod[:, 0, :], prod[:, 1, :], ALU.add).then_inc(z_step, 1)
                    dve.wait_ge(z_step, it * 4 + 2 * m + 1)
                    dve.tensor_copy(tile(zH, it * 2 + m), prod[:, 0, :]).then_inc(z_step, 1)
                    dve.wait_ge(z_step, it * 4 + 2 * m + 2)
                    dve.tensor_tensor(tile(zL, it * 2 + m), prod[:, 0, :], tile(zH, it * 2 + m), ALU.subtract)\
                       .then_inc(z_done, 1)

            def residual(m, bank, gate, before, i):
                dve.wait_ge(x_done, i + before)
                dve.scalar_tensor_tensor(xT[:, m, 0:SEQ], bank[:, 0:SEQ], mod[:, gate + m, 0:1], xT[:, m, 0:SEQ],
                                         ALU.mult, ALU.add)
                y = bank[:, SEQ:TOK].rearrange("p (b t) -> p b t", t=T)
                steps.do(dve.tensor_tensor(prod[:, 0, 0:NS].rearrange("p (b t) -> p b t", t=T), y,
                                           mod[:, gate + m, 1:9].unsqueeze(2).to_broadcast([P, NB, T]), ALU.mult))
                dve.tensor_tensor(xT[:, m, SEQ:TOK], xT[:, m, SEQ:TOK], prod[:, 0, 0:NS], ALU.add).then_inc(x_done, 1)

            dve.wait_ge(x_back, 16)
            for m in range(KT):
                dve.wait_ge(mix_mm, m + 1)
                residual(m, ps[m % 2], 16, 0, m)
            dve.wait_ge(root_done, 1)
            steps.do(dve.reciprocal(t["root"][:, :], t["root"][:, :]))
            modulate(dve, t, 1, 24, h_pre, h_mid, h_done, h_high, h_split)

            def product(f, it, col):
                buf = prod[:, f % 2, :]
                dve.wait_ge(f_done, it * 4 + f - 1 + OPEN)
                dve.wait_ge(silu_done, it * 4 + f + 1)
                dve.wait_ge(b_mm, it * 4 + f + 1 + OPEN)
                dve.tensor_tensor(buf, gates[:, f % 4 // 2, f % 2, :], ps[2 * (f % 4) + 1][:, 0:TOK], ALU.mult)\
                   .then_inc(f_step, 1)
                dve.wait_ge(f_step, it * 8 + 2 * f + 1)
                dve.tensor_copy(tile(GH, col), buf).then_inc(f_step, 1)
                dve.wait_ge(f_step, it * 8 + 2 * f + 2)
                dve.tensor_tensor(tile(GL, col), buf, tile(GH, col), ALU.subtract).then_inc(f_done, 1)

            with dve.Fori(0, 5) as it:
                for f in range(4):
                    product(f, it, it * 4 + f)
            for f in range(20, 22):
                product(f, 0, f)
            for i, m in enumerate((4, 5, 6, 7, 0, 1, 2, 3)):
                dve.wait_ge(last_mm, i + 1)
                residual(m, ps[m], 40, KT, i)
            dve.wait_ge(root_done, 2)
            steps.do(dve.reciprocal(t["root"][:, :], t["root"][:, :]))
            for k in range(KT):
                dve.scalar_tensor_tensor(uT[:, k, :], xT[:, k, :], t["vecT"][:, V_GZ + k:V_GZ + k + 1], t["root"][:, :],
                                         ALU.mult, ALU.mult).then_inc(y_done, 1)
            for i, (t0, n) in enumerate(T_TILES):
                dve.wait_ge(y_tr, 2 * i + 2)
                dve.tensor_copy(yn[0:n, i, 512:1024], ps[1][0:n, :]).then_inc(y_dve, 1)


def build(nc, d):
    with ExitStack() as persist:
        def sb(stack, name, shape, dt=F32):
            return stack.enter_context(nc.sbuf_tensor("t_" + name, shape, dt))

        def sem(name):
            return persist.enter_context(nc.semaphore(name))

        t = {}
        for name, shape in [("slab", [P, SLOTS, SLABW]), ("ident", [P, P]), ("ones", [P, P]),
                            ("vecT", [P, NVEC]), ("mod", [P, 48, 9]), ("amp", [P, 2, KT, 9]), ("eps", [P, 1]),
                            ("gn", [24, TOK])]:
            t[name] = sb(persist, name, shape)
        t["rows_stored"] = sem("rows_stored")
        t["slab_landed"] = [sem(f"b_slab_landed{s}") for s in range(SLOTS)]
        to_back, to_decode = ExitStack(), ExitStack()
        t["oT_s"] = sb(to_back, "oT_s", [P, 4, 4, NS])
        t["table"], t["index"] = sb(to_decode, "table", [P, NB], I32), sb(to_decode, "index", [P, NB], U32)
        ps = [persist.enter_context(nc.psum_tensor(f"ps{i}", [P, 512], F32)) for i in range(8)]
        for name, shape in [("hbias", [P, 4]), ("w2", [P, 2, 2, DH]), ("b2v", [1, DH]), ("seg_col", [P, 1]),
                            ("c64", [64, C64W]), ("qaT_s", [P, 4, NS + T]), ("qbT_s", [P, 4, NS + T]),
                            ("kaT_s", [P, 4, NS]), ("ksT_s", [P, NS]), ("kwT_s", [P, NS]), ("rows_s", [NS, ROWW])]:
            t[name] = sb(to_decode, name, shape)
        with ExitStack() as early:
            for name, shape in [("rows_p", [P, 2, ROWW]), ("qaT_p", [P, 4, SEQ]), ("qbT_p", [P, 4, SEQ]),
                                ("kaT_p", [P, 4, SEQ]), ("ksT_p", [P, SEQ]), ("kwT_p", [P, SEQ]),
                                ("cp", [P, CPW])]:
                t[name] = sb(early, name, shape)
            with ExitStack() as temps:
                for name, shape, dt in [("root", [P, TOK], F32), ("wgn", [P, KT * 24], F32),
                                        ("vecn", [P, P], F32), ("cT", [P, 72], F32), ("xT", [P, KT, TOK], F32),
                                        ("uT", [P, KT, TOK], F32), ("uH", [P, KT, TOK], F32R),
                                        ("uL", [P, KT, TOK], F32R), ("sq", [P, KT, TOK], F32)]:
                    t[name] = sb(temps, name, shape, dt)
                for stood, parts in [([("xn", [P, 3, D]), ("cn", [9, D])], ("f_H0", "f_L0")),
                                     ([("modn", [9, NADA * D])], ("f_H1", "f_L1"))]:
                    with ExitStack() as here:
                        for name in parts:
                            t[name] = sb(here, name, [P, SLABW], F32R)
                    for name, shape in stood:
                        t[name] = sb(temps, name, shape)
                front_block(nc, sem, t, d, ps)
            with ExitStack() as temps:
                for name, shape in [("segs", [PSEG, 8, 4, 2, DH]), ("XTp", [P, 2, 2, 8, PC1]),
                                    ("hidn", [PC1, 512]), ("hid_p", [P, 2, 2, 2 * PCMP]), ("ckT_p", [P, PSEG]), ("cv_p", [PSEG, P]),
                                    ("S_p", [P, 3, 2048]), ("PT_p", [P, 2, 2, H, P]),
                                    ("Sc_p", [P, 256]), ("PTc_p", [PSEG, 2 * H, P]), ("oT_p", [P, 4, 4, SEQ]),
                                    ("nmax_p", [P, 3, H]), ("sum_p", [P, 3, H]), ("rsum_p", [P, H]),
                                    ("cstat_p", [P, 2 * H])]:
                    t[name] = sb(temps, name, shape)
                prompt_block(nc, sem, t, d, ps)
        with ExitStack() as mid:
            for name, shape, dt in [("Kr", [P, 8, 512], F32), ("Vr", [P, V_SLOTS, 512], F32), ("nsa", [P, 2, 2048], F32),
                                    ("relay", [P, 2, 512], F32), ("vsel", [P, SEG, P], F32),
                                    ("XT", [P, 2, KV, 8, NSEG], F32), ("KTr", [P, 4, 512], F32),
                                    ("Sm", [64, PAST + 64], F32), ("Ss", [64, PAST + 64], F32), ("Sw", [64, WIN + 64], F32),
                                    ("Sc", [64, P], F32), ("PTm", [P, SEG + 1, 64], F32), ("PTs", [P, SEG + 1, 64], F32),
                                    ("PTw", [P, 6, 64], F32), ("hid", [P, 2, 2, 2 * NCMP], F32), ("ckT", [P, P], F32),
                                    ("cv", [P, P], F32), ("wkv", [P, 4, 256], F32), ("qa_cur", [P, 328], F32),
                                    ("qb_cur", [P, 64], F32), ("above8", [64, NMB, NMB], F32),
                                    ("equal8", [64, NMB, NMB], F32), ("gates4", [64, NMB, 4], F32), ("gate", [64, NMB], F32),
                                    ("rank", [64, CAND], F32), ("mb_mask", [64, NMB], F32), ("sel_mask", [64, NSB], F32),
                                    ("imp", [64, CAND], F32), ("nmax", [64, 4], F32), ("sums", [64, 4], F32),
                                    ("inv", [64, 4], F32), ("Om", [64, 512], F32), ("On", [64, 3, P], F32),
                                    ("index_now", [P, 2], U32)]:
                t[name] = sb(mid, name, shape, dt)
            decode_block(nc, sem, t, d, ps)
        to_decode.close()
        to_back.close()
        with ExitStack() as late:
            def place(stack, tensors):
                for name, shape, dt in tensors:
                    t[name] = stack.enter_context(nc.sbuf_tensor("b_" + name, shape, dt))

            def overlaid(*sets):
                for tensors in sets[:-1]:
                    with ExitStack() as here:
                        place(here, tensors)
                place(late, sets[-1])

            place(late, [("gates", [P, 2, 2, TOK], F32), ("root", [P, TOK], F32), ("xT", [P, KT, TOK], F32),
                         ("uT", [P, KT, TOK], F32), ("uL", [P, KT, TOK], F32R), ("slabH", [P, SLOTS, SLABW], F32R),
                         ("slabL", [P, SLOTS, SLABW], F32R), ("prod", [P, 2, TOK], F32), ("warm", [P, 1], F32)])
            overlaid([("sq", [P, KT, TOK], F32)], [("uH", [P, KT, TOK], F32R)])
            overlaid([("oT", [P, 4, 4, TOK], F32), ("oH", [P, 4, TOK], F32R), ("oL", [P, 4, TOK], F32R),
                      ("zH", [P, KT, TOK], F32R), ("zL", [P, KT, TOK], F32R)],
                     [("below", [P, 2, 4, TOK], F32), ("bH", [P, 4, TOK], F32R), ("bL", [P, 4, TOK], F32R)],
                     [("yn", [P, 3, D], F32)],
                     [("GH", [P, FT, TOK], F32R), ("GL", [P, FT, TOK], F32R)])
            back_block(nc, sem, t, d, ps)


_OUTS = [("y_prompt", (1, 256, 1024)), ("y_sample", (8, 8, 1024)), ("moba_kv_prompt", (1, 256, 2, 8, 64)),
         ("nsa_kv_prompt", (1, 256, 4, 2, 64)), ("nsa_win_prompt", (1, 256, 2, 2, 64)),
         ("moba_kv_sample", (8, 8, 2, 8, 64)), ("nsa_kv_sample", (8, 8, 4, 2, 64)),
         ("nsa_win_sample", (8, 512, 2, 2, 64))]


def constants():
    import numpy as np
    slope = 2.0 ** -(np.arange(H) + 1.0)
    ident = np.eye(P)
    ones = np.ones((P, P))
    row_h, row_t = np.repeat(np.arange(H), T), np.tile(np.arange(T), H)
    row_kv = row_h // G
    c64 = np.zeros((64, C64W))
    c64[:, C_GSUM:C_BDEC] = (row_kv[:, None] == row_kv) & (row_t[:, None] == row_t)
    kpos = SEG * np.arange(NSEG)[None, :] + np.arange(SEG)[:, None]
    c64[:, C_BDEC:C_BOWN] = -slope[row_h][:, None] * (PAST + row_t[:, None] - kpos.reshape(1, -1))
    own = np.full((64, NB, NB, T), NEG)
    for r in range(64):
        for b in range(NB):
            for u in range(row_t[r] + 1):
                own[r, b, b, u] = -slope[row_h[r]] * (row_t[r] - u)
    c64[:, C_BOWN:C_BWIN] = own.reshape(64, -1)
    wpos = PAST - WIN + (4 * np.arange(128)[None, :] + np.arange(4)[:, None]).reshape(1, -1)
    qpos = PAST + row_t[:, None]
    c64[:, C_BWIN:C_TIE] = np.where(wpos > qpos - WIN, -slope[row_h][:, None] * (qpos - wpos), NEG)
    c64[:, C_TIE:C_TIE8] = (np.arange(CAND)[None, :] < np.arange(CAND)[:, None]).reshape(1, -1)
    c64[:, C_TIE8:C64W] = (np.arange(NMB)[None, :] < np.arange(NMB)[:, None]).reshape(1, -1)
    cp = np.zeros((P, CPW))
    q, k = np.arange(P)[:, None, None], np.arange(256)[None, None, :]
    for qt, c0, nk in [(0, C_BP0, 128), (1, C_BP1, 256)]:
        dist = q + P * qt - k[:, :, :nk]
        cp[:, c0:c0 + 8 * nk] = np.where(dist >= 0, -slope[None, :, None] * dist, NEG).reshape(P, -1)
    n = np.arange(PSEG)[None, None, :]
    seen = (SEG * n + 2 * SEG - 1 <= np.arange(P)[:, None, None] + P * np.arange(2)[None, :, None]) & (n < PCMP)
    cp[:, C_MADD:C_MMUL] = np.where(seen, 0.0, NEG).reshape(P, -1)
    cp[:, C_MMUL:CPW] = seen.reshape(P, -1)
    expand = np.zeros((24, 3, 4, P))
    for kv in range(KV):
        for g in range(G):
            for c in range(3):
                expand[(kv * G + g) * 3 + c, c, g, DH * kv:DH * kv + DH] = 1.0
    return {"c_ident": ident, "c_ones": ones, "c_64": c64, "c_p": cp, "c_expand": expand.reshape(24, -1),
            "c_seg": np.arange(P)[:, None] % (PAGE // SEG)}


def kernel(**inputs):
    import numpy as np
    import concourse.bacc as bacc
    from concourse.bass_utils import run_bass_kernel_spmd

    nc = bacc.Bacc("TRN2", target_bir_lowering=False, num_devices=1)
    arrays, d = {}, {}
    shapes = {
        "x_prompt": (256, 1024), "x_sample": (64, 1024), "cache_moba_kv": (160 * 8, 16 * 1024),
        "cache_nsa_kv": (160 * 8, 16 * 512), "cache_nsa_win": (8, 512, 256)}
    for name, a in inputs.items():
        arrays[name] = np.ascontiguousarray(a)
    for name, a in constants().items():
        arrays[name] = np.ascontiguousarray(a.astype(np.float32))
    for name, a in arrays.items():
        if name in shapes:
            arrays[name] = a = a.reshape(shapes[name])
        d[name] = nc.dram_tensor(name, a.shape, mybir.dt.from_np(a.dtype), kind="ExternalInput").ap()
    flat = {"y_prompt": (256, 1024), "y_sample": (64, 1024), "moba_kv_prompt": (256, 1024), "nsa_kv_prompt": (256, 512),
            "nsa_win_prompt": (256, 256), "moba_kv_sample": (64, 1024), "nsa_kv_sample": (64, 512),
            "nsa_win_sample": (8, 512, 256)}
    for name, _ in _OUTS:
        d[name] = nc.dram_tensor(name, flat[name], F32, kind="ExternalOutput").ap()
    for name, shape in [("spill_x", (P, KT * TOK)), ("spill_u", (P, KT * TOK)), ("spill_o", (P, 16 * SEQ))]:
        d[name] = nc.dram_tensor(name, shape, F32, kind="Internal").ap()
    build(nc, d)
    r = run_bass_kernel_spmd(nc, [arrays], core_ids=[0]).results[0]
    return tuple(np.asarray(r[name]).reshape(shape) for name, shape in _OUTS)
```
